# Optimizing a Trainium2 kernel written in Bass

```python
import math
import jax, jax.numpy as jnp
from jax import lax
import numpy as np

D_MODEL = 1024
BATCH = 1
SEQ = 256
DEPTH = 1

HG_HEADS = 4
HG_HEAD_K = 128
HG_HEAD_V = 128
HG_KEY = HG_HEADS * HG_HEAD_K
HG_VAL = HG_HEADS * HG_HEAD_V
GLA_HEADS = 4
GLA_HEAD_K = 64
GLA_HEAD_V = 128
GLA_KEY = GLA_HEADS * GLA_HEAD_K
GLA_VAL = GLA_HEADS * GLA_HEAD_V
GLA_GATE_RANK = 16
GLA_GATE_NORMALIZER = 16.0
MIX_WIDTH = HG_VAL + GLA_VAL
IN_SPLITS = (HG_KEY, HG_KEY, HG_VAL, HG_VAL, GLA_KEY, GLA_KEY, GLA_VAL, GLA_GATE_RANK, GLA_VAL)
IN_WIDTH = sum(IN_SPLITS)
CHUNK = 64
PEER_HEADS = 8
PEER_N_KEYS = 128
PEER_N_EXPERTS = PEER_N_KEYS * PEER_N_KEYS
PEER_QUERY_DIM = 256
PEER_HALF = PEER_QUERY_DIM // 2
PEER_TOPK = 16
PEER_BLOCK = 128
EPS = 1e-6


def rms_norm(x, g):
    xf = x.astype(jnp.float32)
    y = xf * lax.rsqrt(jnp.mean(xf * xf, axis=-1, keepdims=True) + EPS)
    return (y * g.astype(jnp.float32)).astype(x.dtype)

def split_heads(a, n_heads):
    b, t, w = a.shape
    return a.reshape(b, t, n_heads, w // n_heads).transpose(0, 2, 1, 3)

def merge_heads(a):
    b, n, t, d = a.shape
    return a.transpose(0, 2, 1, 3).reshape(b, t, n * d)

def chunk_gated_linear_attention(q, k, v, log_g):
    b, h, t, dk = q.shape
    dv = v.shape[-1]
    n_chunks = t // CHUNK

    def to_chunks(a):
        return a.astype(jnp.float32).reshape(b, h, n_chunks, CHUNK, a.shape[-1]).transpose(2, 0, 1, 3, 4)

    qc, kc, vc, gc = to_chunks(q), to_chunks(k), to_chunks(v), to_chunks(log_g)
    causal = jnp.tril(jnp.ones((CHUNK, CHUNK), dtype=bool))[:, :, None]

    def step(state, inp):
        qb, kb, vb, gb = inp
        cum = jnp.cumsum(gb, axis=2)
        rel = cum[:, :, :, None, :] - cum[:, :, None, :, :]
        decay = jnp.exp(jnp.where(causal, rel, -jnp.inf))
        scores = jnp.einsum('bhid,bhjd,bhijd->bhij', qb, kb, decay)
        out = (jnp.einsum('bhij,bhjv->bhiv', scores, vb)
               + jnp.einsum('bhid,bhdv->bhiv', qb * jnp.exp(cum), state))
        last = cum[:, :, -1:, :]
        state = (jnp.exp(last[:, :, 0, :])[..., None] * state
                 + jnp.einsum('bhjd,bhjv->bhdv', kb * jnp.exp(last - cum), vb))
        return state, out

    s0 = jnp.zeros((b, h, dk, dv), jnp.float32)
    _, o = lax.scan(step, s0, (qc, kc, vc, gc))
    return o.transpose(1, 2, 0, 3, 4).reshape(b, h, t, dv)

def hgrn2_mixer(q, f, i, gate, lower_bound, norm_g):
    q = jax.nn.silu(q)
    forget = lower_bound + (1.0 - lower_bound) * jax.nn.sigmoid(f.astype(jnp.float32))
    key = 1.0 - forget
    log_f = jnp.log(forget)
    o = chunk_gated_linear_attention(split_heads(q, HG_HEADS), split_heads(key, HG_HEADS),
                                     split_heads(i, HG_HEADS), split_heads(log_f, HG_HEADS))
    o = merge_heads(rms_norm(o, norm_g))
    return (o * jax.nn.silu(gate.astype(jnp.float32))).astype(gate.dtype)

def gla_mixer(q, k, v, gate_low, gate, w_gate_up, b_gate, norm_g):
    log_g = jax.nn.log_sigmoid((gate_low @ w_gate_up + b_gate).astype(jnp.float32)) / GLA_GATE_NORMALIZER
    q = q * (GLA_HEAD_K ** -0.5)
    o = chunk_gated_linear_attention(split_heads(q, GLA_HEADS), split_heads(k, GLA_HEADS),
                                     split_heads(v, GLA_HEADS), split_heads(log_g, GLA_HEADS))
    o = merge_heads(rms_norm(o, norm_g))
    return (o * jax.nn.silu(gate.astype(jnp.float32))).astype(gate.dtype)

def peer_ffn(xn, w_q, sub_keys, u, v):
    b, t, d = xn.shape
    blocks = xn.reshape(-1, PEER_BLOCK, d)

    def block(xb):
        q = (xb @ w_q).reshape(PEER_BLOCK, PEER_HEADS, 2, PEER_HALF)
        s = jnp.einsum('thpd,hpnd->thpn', q, sub_keys).astype(jnp.float32)
        s_top, i_top = lax.top_k(s, PEER_TOPK)
        cand = s_top[:, :, 0, :, None] + s_top[:, :, 1, None, :]
        cand_idx = i_top[:, :, 0, :, None] * PEER_N_KEYS + i_top[:, :, 1, None, :]
        cand = cand.reshape(PEER_BLOCK, PEER_HEADS, PEER_TOPK * PEER_TOPK)
        cand_idx = cand_idx.reshape(PEER_BLOCK, PEER_HEADS, PEER_TOPK * PEER_TOPK)
        best, pos = lax.top_k(cand, PEER_TOPK)
        expert = jnp.take_along_axis(cand_idx, pos, axis=-1)
        g = jax.nn.softmax(best, axis=-1)
        act = jax.nn.gelu(jnp.einsum('td,thkd->thk', xb, u[expert]), approximate=False)
        return jnp.einsum('thk,thkd->td', (g * act).astype(xb.dtype), v[expert])

    return lax.map(block, blocks).reshape(b, t, d)

def first_inputs(seed: int = 0) -> dict:
    key = jax.random.key(seed)
    ks = jax.random.split(key, 16)
    nrm = jax.random.normal
    L = DEPTH
    return {
        "x": nrm(ks[0], (BATCH, SEQ, D_MODEL), jnp.float32),
        "norm1_g": 1.0 + 0.02 * nrm(ks[1], (L, D_MODEL), jnp.float32),
        "w_in": nrm(ks[2], (L, D_MODEL, IN_WIDTH), jnp.float32) * D_MODEL ** -0.5,
        "hg_lower_logits": 0.1 * nrm(ks[3], (L + 1, HG_KEY), jnp.float32),
        "hg_norm_g": 1.0 + 0.02 * nrm(ks[4], (L, HG_HEAD_V), jnp.float32),
        "gla_w_gate_up": nrm(ks[5], (L, GLA_GATE_RANK, GLA_KEY), jnp.float32) * GLA_GATE_RANK ** -0.5,
        "gla_b_gate": 0.1 * nrm(ks[6], (L, GLA_KEY), jnp.float32),
        "gla_norm_g": 1.0 + 0.02 * nrm(ks[7], (L, GLA_HEAD_V), jnp.float32),
        "w_out": nrm(ks[8], (L, MIX_WIDTH, D_MODEL), jnp.float32) * MIX_WIDTH ** -0.5,
        "norm2_g": 1.0 + 0.02 * nrm(ks[9], (L, D_MODEL), jnp.float32),
        "peer_w_q": nrm(ks[10], (L, D_MODEL, PEER_HEADS * PEER_QUERY_DIM), jnp.float32) * D_MODEL ** -0.5,
        "peer_sub_keys": nrm(ks[11], (L, PEER_HEADS, 2, PEER_N_KEYS, PEER_HALF), jnp.float32) * PEER_HALF ** -0.5,
        "peer_u": nrm(ks[12], (L, PEER_N_EXPERTS, D_MODEL), jnp.float32) * D_MODEL ** -0.5,
        "peer_v": nrm(ks[13], (L, PEER_N_EXPERTS, D_MODEL), jnp.float32) * 0.3,
        "norm_f_g": 1.0 + 0.02 * nrm(ks[14], (D_MODEL,), jnp.float32),
    }

def first_block(x, norm1_g, w_in, hg_lower_logits, hg_norm_g, gla_w_gate_up, gla_b_gate, gla_norm_g,
              w_out, norm2_g, peer_w_q, peer_sub_keys, peer_u, peer_v, norm_f_g):
    lower_bounds = jnp.cumsum(jax.nn.softmax(hg_lower_logits.astype(jnp.float32), axis=0), axis=0)
    offsets = [int(o) for o in np.cumsum(IN_SPLITS)[:-1]]
    h = x
    for layer in range(DEPTH):
        xn = rms_norm(h, norm1_g[layer])
        proj = xn @ w_in[layer]
        hq, hf, hi, hgate, gq, gk, gv, glow, ggate = jnp.split(proj, offsets, axis=-1)
        o_hgrn = hgrn2_mixer(hq, hf, hi, hgate, lower_bounds[layer], hg_norm_g[layer])
        o_gla = gla_mixer(gq, gk, gv, glow, ggate, gla_w_gate_up[layer], gla_b_gate[layer], gla_norm_g[layer])
        mixed = jnp.concatenate([o_hgrn, o_gla], axis=-1)
        h = h + (mixed @ w_out[layer]).astype(h.dtype)
        hn = rms_norm(h, norm2_g[layer])
        h = h + peer_ffn(hn, peer_w_q[layer], peer_sub_keys[layer], peer_u[layer], peer_v[layer]).astype(h.dtype)
    return rms_norm(h, norm_f_g)


N_BRANCH = 4
BRANCH_W = D_MODEL // 2
DN_HEADS = 4
DN_DK = BRANCH_W // DN_HEADS
DN_DV = BRANCH_W // DN_HEADS
DN_CHUNK = 64
CONV_W = 4
GM_GROUPS = 4
GM_CH = BRANCH_W // GM_GROUPS
GM_CHUNK = 128
SW_HEADS = 8
SW_KV_HEADS = 2
SW_HD = BRANCH_W // SW_HEADS
SW_WINDOW = 128
SW_BLOCK = 128
MEM_LEN = 256
XM_HEADS = 4
XM_HD = BRANCH_W // XM_HEADS

NEG_INF = -1e30

IN_SPLITS_2 = [
    3 * BRANCH_W,
    BRANCH_W,
    DN_HEADS,
    DN_HEADS,
    2 * BRANCH_W,
    BRANCH_W,
    SW_HEADS * SW_HD,
    SW_KV_HEADS * SW_HD,
    SW_KV_HEADS * SW_HD,
    BRANCH_W,
    XM_HEADS * XM_HD,
    BRANCH_W,
    N_BRANCH * D_MODEL,
]
D_IN = sum(IN_SPLITS_2)


def _rmsnorm(x, g):
    xf = x.astype(jnp.float32)
    y = xf * lax.rsqrt(jnp.mean(xf * xf, axis=-1, keepdims=True) + EPS)
    return (y * g.astype(jnp.float32)).astype(x.dtype)

def _l2norm(x):
    return x * lax.rsqrt(jnp.sum(x * x, axis=-1, keepdims=True) + EPS)

def _split_cols(cols):
    idx, acc = [], 0
    for s in IN_SPLITS_2[:-1]:
        acc += s
        idx.append(acc)
    return jnp.split(cols, idx, axis=-1)

def _causal_dwconv(x, w):
    c = x.shape[-1]
    return lax.conv_general_dilated(
        x, w[:, None, :].astype(x.dtype), window_strides=(1,),
        padding=[(CONV_W - 1, 0)], dimension_numbers=("NWC", "WIO", "NWC"),
        feature_group_count=c)

def _gated_delta_chunked(q, k, v, g, beta):
    B, T, H, dk = q.shape
    dv = v.shape[-1]
    C = DN_CHUNK
    n = T // C

    def blk(a):
        return jnp.moveaxis(a.reshape((B, n, C, H) + a.shape[3:]), 3, 1)

    q, k, v, g, beta = blk(q), blk(k), blk(v), blk(g), blk(beta)
    gc = jnp.cumsum(g, axis=-1)
    diff = gc[..., :, None] - gc[..., None, :]
    ii = jnp.arange(C)
    strict = ii[:, None] > ii[None, :]
    incl = ii[:, None] >= ii[None, :]
    kb = k * beta[..., None]
    L = jnp.where(strict, jnp.einsum("bhncd,bhnsd->bhncs", kb, k)
                  * jnp.exp(jnp.where(strict, diff, 0.0)), 0.0)
    eye = jnp.eye(C, dtype=q.dtype)
    rhs = jnp.concatenate([v * beta[..., None], kb * jnp.exp(gc)[..., None]], axis=-1)
    sol = lax.linalg.triangular_solve(eye + L, rhs, left_side=True, lower=True,
                                      unit_diagonal=True)
    u, w = sol[..., :dv], sol[..., dv:]
    a_qk = jnp.where(incl, jnp.einsum("bhncd,bhnsd->bhncs", q, k)
                     * jnp.exp(jnp.where(incl, diff, 0.0)), 0.0)
    g_last = gc[..., -1]
    qg = q * jnp.exp(gc)[..., None]
    kd = k * jnp.exp(g_last[..., None] - gc)[..., None]
    d_last = jnp.exp(g_last)
    xs = tuple(jnp.moveaxis(a, 2, 0) for a in (qg, kd, u, w, a_qk, d_last))

    def step(S, inp):
        qg_c, kd_c, u_c, w_c, a_c, d_c = inp
        v_new = u_c - jnp.einsum("bhck,bhkv->bhcv", w_c, S)
        o = (jnp.einsum("bhck,bhkv->bhcv", qg_c, S)
             + jnp.einsum("bhcs,bhsv->bhcv", a_c, v_new))
        S = S * d_c[..., None, None] + jnp.einsum("bhck,bhcv->bhkv", kd_c, v_new)
        return S, o

    S0 = jnp.zeros((B, H, dk, dv), jnp.float32)
    _, o = lax.scan(step, S0, xs)
    o = jnp.moveaxis(o, 0, 2)
    return jnp.moveaxis(o, 1, 3).reshape(B, T, H, dv)

def _deltanet_branch(qkv, z, b_logit, a_logit, conv_w, a_log, dt_bias, o_norm):
    B, T, _ = qkv.shape
    qkv = jax.nn.silu(_causal_dwconv(qkv, conv_w)).astype(jnp.float32)
    q, k, v = jnp.split(qkv, 3, axis=-1)
    q = _l2norm(q.reshape(B, T, DN_HEADS, DN_DK)) * (DN_DK ** -0.5)
    k = _l2norm(k.reshape(B, T, DN_HEADS, DN_DK))
    v = v.reshape(B, T, DN_HEADS, DN_DV)
    beta = jax.nn.sigmoid(b_logit.astype(jnp.float32))
    g = -jnp.exp(a_log.astype(jnp.float32)) * jax.nn.softplus(
        a_logit.astype(jnp.float32) + dt_bias.astype(jnp.float32))
    o = _gated_delta_chunked(q, k, v, g, beta)
    o = _rmsnorm(o, o_norm) * jax.nn.silu(z.astype(jnp.float32).reshape(B, T, DN_HEADS, DN_DV))
    return o.reshape(B, T, BRANCH_W).astype(z.dtype)

def _spatial_gating_branch(uv, z, v_gain, w_s, b_s):
    B, T, _ = uv.shape
    u, v = jnp.split(jax.nn.gelu(uv), 2, axis=-1)
    v = _rmsnorm(v, v_gain)
    n = T // GM_CHUNK
    vb = v.reshape(B, n, GM_CHUNK, GM_GROUPS, GM_CH)
    causal = jnp.tril(jnp.ones((GM_CHUNK, GM_CHUNK), dtype=bool))
    ws = jnp.where(causal, w_s, 0.0).astype(v.dtype)
    s = jnp.einsum("gpq,bnqgc->bnpgc", ws, vb) + b_s.T.astype(v.dtype)[None, None, :, :, None]
    return u * s.reshape(B, T, BRANCH_W) * jax.nn.silu(z)

def _sliding_window_branch(q, k, v, z, sinks):
    B, T, _ = q.shape
    P = SW_BLOCK
    n = T // P
    G = SW_HEADS // SW_KV_HEADS
    q = q.reshape(B, n, P, SW_KV_HEADS, G, SW_HD)
    k = k.reshape(B, n, P, SW_KV_HEADS, SW_HD)
    v = v.reshape(B, n, P, SW_KV_HEADS, SW_HD)
    pad = jnp.zeros_like(k[:, :1])
    kb = jnp.concatenate([jnp.concatenate([pad, k[:, :-1]], axis=1), k], axis=2)
    vb = jnp.concatenate([jnp.concatenate([pad, v[:, :-1]], axis=1), v], axis=2)
    s = jnp.einsum("bnqkgd,bnskd->bnkgqs", q, kb).astype(jnp.float32) * (SW_HD ** -0.5)
    qi = jnp.arange(P)[:, None]
    kj = jnp.arange(2 * P)[None, :]
    dist = qi + P - kj
    blk = jnp.arange(n)[:, None, None]
    valid = (dist >= 0) & (dist < SW_WINDOW) & (blk * P - P + kj >= 0)
    s = jnp.where(valid[None, :, None, None], s, NEG_INF)
    sink = jnp.broadcast_to(
        sinks.astype(jnp.float32).reshape(SW_KV_HEADS, G)[None, None, :, :, None, None],
        s.shape[:-1] + (1,))
    p = jax.nn.softmax(jnp.concatenate([s, sink], axis=-1), axis=-1)[..., :-1]
    o = jnp.einsum("bnkgqs,bnskd->bnqkgd", p.astype(vb.dtype), vb).reshape(B, T, BRANCH_W)
    return o * jax.nn.silu(z)

def _memory_branch(q, z, mem_kv):
    B, T, _ = q.shape
    q = q.reshape(B, T, XM_HEADS, XM_HD)
    mk, mv = jnp.split(mem_kv, 2, axis=-1)
    mk = mk.reshape(B, -1, XM_HEADS, XM_HD)
    mv = mv.reshape(B, -1, XM_HEADS, XM_HD)
    s = jnp.einsum("bthd,bmhd->bhtm", q, mk).astype(jnp.float32) * (XM_HD ** -0.5)
    p = jax.nn.softmax(s, axis=-1)
    o = jnp.einsum("bhtm,bmhd->bthd", p.astype(mv.dtype), mv).reshape(B, T, BRANCH_W)
    return o * jax.nn.silu(z)

def _layer(x, mem, norm_pre, norm_post, norm_mem, w_in, conv_w, a_log, dt_bias, dn_norm,
           gm_norm, spatial_w, spatial_b, sinks, w_mem_kv, w_up, w_out):
    B, T, D = x.shape
    h = _rmsnorm(x, norm_pre)
    cols = h @ w_in
    (dn_qkv, dn_z, dn_b, dn_a, gm_uv, gm_z, sw_q, sw_k, sw_v, sw_z,
     xm_q, xm_z, gate_logits) = _split_cols(cols)
    mem_kv = _rmsnorm(mem, norm_mem) @ w_mem_kv
    y_a = _deltanet_branch(dn_qkv, dn_z, dn_b, dn_a, conv_w, a_log, dt_bias, dn_norm)
    y_b = _spatial_gating_branch(gm_uv, gm_z, gm_norm, spatial_w, spatial_b)
    y_c = _sliding_window_branch(sw_q, sw_k, sw_v, sw_z, sinks)
    y_m = _memory_branch(xm_q, xm_z, mem_kv)
    ys = jnp.stack([y_a, y_b, y_c, y_m], axis=2)
    proj = jnp.einsum("btnc,ncd->btnd", ys, w_up)
    gates = jax.nn.sigmoid(gate_logits.reshape(B, T, N_BRANCH, D))
    merged = jnp.sum(gates * proj, axis=2)
    out = merged @ w_out
    return x + _rmsnorm(out, norm_post)

def second_inputs(seed: int = 0) -> dict:
    key = jax.random.key(seed)
    ks = jax.random.split(key, 20)
    f32 = jnp.float32
    nrm = lambda k, shape, scale: jax.random.normal(k, shape, f32) * scale
    dt = jnp.exp(jax.random.uniform(ks[8], (DEPTH, DN_HEADS), f32,
                                    math.log(1e-3), math.log(1e-1)))
    return {
        "x": nrm(ks[0], (BATCH, SEQ, D_MODEL), 1.0),
        "mem": nrm(ks[1], (BATCH, MEM_LEN, D_MODEL), 1.0),
        "norm_pre": 1.0 + nrm(ks[2], (DEPTH, D_MODEL), 0.1),
        "norm_post": 1.0 + nrm(ks[3], (DEPTH, D_MODEL), 0.1),
        "norm_mem": 1.0 + nrm(ks[4], (DEPTH, D_MODEL), 0.1),
        "w_in": nrm(ks[5], (DEPTH, D_MODEL, D_IN), D_MODEL ** -0.5),
        "conv_w": nrm(ks[6], (DEPTH, CONV_W, 3 * BRANCH_W), CONV_W ** -0.5),
        "a_log": jnp.log(jax.random.uniform(ks[7], (DEPTH, DN_HEADS), f32, 1.0, 16.0)),
        "dt_bias": dt + jnp.log(-jnp.expm1(-dt)),
        "dn_norm": 1.0 + nrm(ks[9], (DEPTH, DN_DV), 0.1),
        "gm_norm": 1.0 + nrm(ks[10], (DEPTH, BRANCH_W), 0.1),
        "spatial_w": nrm(ks[11], (DEPTH, GM_GROUPS, GM_CHUNK, GM_CHUNK), GM_CHUNK ** -0.5),
        "spatial_b": 1.0 + nrm(ks[12], (DEPTH, GM_GROUPS, GM_CHUNK), 0.1),
        "sinks": nrm(ks[13], (DEPTH, SW_HEADS), 1.0),
        "w_mem_kv": nrm(ks[14], (DEPTH, D_MODEL, 2 * BRANCH_W), D_MODEL ** -0.5),
        "w_up": nrm(ks[15], (DEPTH, N_BRANCH, BRANCH_W, D_MODEL), BRANCH_W ** -0.5),
        "w_out": nrm(ks[16], (DEPTH, D_MODEL, D_MODEL), D_MODEL ** -0.5),
    }

def second_block(x, mem, norm_pre, norm_post, norm_mem, w_in, conv_w, a_log, dt_bias, dn_norm,
              gm_norm, spatial_w, spatial_b, sinks, w_mem_kv, w_up, w_out):
    for l in range(DEPTH):
        x = _layer(x, mem, norm_pre[l], norm_post[l], norm_mem[l], w_in[l], conv_w[l],
                   a_log[l], dt_bias[l], dn_norm[l], gm_norm[l], spatial_w[l], spatial_b[l],
                   sinks[l], w_mem_kv[l], w_up[l], w_out[l])
    return x


def setup_inputs(seed=0):
    out = dict(first_inputs(seed))
    for name, value in second_inputs(seed + 1).items():
        if name != "x":
            out[name + "_2"] = value
    return out


def reference(
    x, norm1_g, w_in, hg_lower_logits, hg_norm_g, gla_w_gate_up, gla_b_gate, gla_norm_g, w_out,
    norm2_g, peer_w_q, peer_sub_keys, peer_u, peer_v, norm_f_g, mem_2, norm_pre_2, norm_post_2,
    norm_mem_2, w_in_2, conv_w_2, a_log_2, dt_bias_2, dn_norm_2, gm_norm_2, spatial_w_2,
    spatial_b_2, sinks_2, w_mem_kv_2, w_up_2, w_out_2,
):
    x = first_block(
        x, norm1_g, w_in, hg_lower_logits, hg_norm_g, gla_w_gate_up, gla_b_gate, gla_norm_g,
        w_out, norm2_g, peer_w_q, peer_sub_keys, peer_u, peer_v, norm_f_g,
    )
    return second_block(
        x, mem_2, norm_pre_2, norm_post_2, norm_mem_2, w_in_2, conv_w_2, a_log_2, dt_bias_2,
        dn_norm_2, gm_norm_2, spatial_w_2, spatial_b_2, sinks_2, w_mem_kv_2, w_up_2, w_out_2,
    )


_drawn_inputs = setup_inputs


def setup_inputs(seed=0):
    import zlib

    import numpy as np

    out = dict(_drawn_inputs(seed))
    spreads = {}
    factors = {'hg_lower_logits': 4.292,
     'hg_norm_g': 3.03,
     'gla_norm_g': 2.877,
     'norm_mem_2': 6.334,
     'sinks_2': 120.897,
     'dn_norm_2': 4.532,
     'gm_norm_2': 8.0,
     'spatial_b_2': 5.462,
     'norm2_g': 2.878}
    for name, (base, spread) in spreads.items():
        noise = np.random.default_rng([zlib.crc32(name.encode()), seed]).standard_normal(out[name].shape)
        drawn = base * np.exp(spread * noise) if base else spread * noise
        out[name] = __import__('jax').numpy.asarray(drawn.astype(out[name].dtype))
    for name, factor in factors.items():
        out[name] = (out[name] * factor).astype(out[name].dtype)
    return out
```

```python
import concourse.bass as bass
from concourse import mybir
from contextlib import ExitStack

F32 = mybir.dt.float32
F32R = mybir.dt.float32r
U32 = mybir.dt.uint32
I32 = mybir.dt.int32
U8 = mybir.dt.uint8
ALU = mybir.AluOpType
ACT = mybir.ActivationFunctionType
AX = mybir.AxisListType

P = 128
D = 1024
T = 256
NT = T // P
KC = D // P
EPS = 1e-6
TILE = 512
RING = 3

HQ, HF, HI, HGATE, GQ, GV, GLOW, GGATE = 0, 512, 1024, 1536, 2048, 2560, 3072, 3088
RANK = 16
HEADS1 = 8
NF = 6
LEVELS = 7
GLA_SCALE = 64.0 ** -0.5
GATE_NORM = 16.0

PH = 8
HP = 2 * PH
NKEY = 128
TOP = 16
SLOTS = PH * TOP
NEG = -3.0e38
GT = 4
NGRP = T // GT

DNQ, DNK, DNV, DNZ, DNBA, GMU, GMV, GMZ, SWQ, SWKV, SWZ, XMQ, XMZ, GATES = (
    0, 512, 1024, 1536, 2048, 2056, 2568, 3080, 3592, 4104, 4360, 4872, 5384, 5896)
DH = 4
TH = NT * DH
CONV = 4
SH, SHD = 8, 64
XH = 4
HEAD = 128
NBR = 4
MASKED = -1.0e30


def bcast(ap, dim, n):
    a = ap.unsqueeze(dim)
    shape = list(a.shape)
    shape[dim] = n
    return a.broadcast_to(shape)


def head_rows(h):
    if h < 4:
        return h, slice(0, P)
    g = h - 4
    return 4 + g // 2, slice(64 * (g % 2), 64 * (g % 2) + 64)


PLACE = [0, 1, 4, 5, 2, 6, 3, 7]


def build(nc, t, out):
    ctx = ExitStack()
    with ctx:
        def sb(name, shape, dt=F32):
            return ctx.enter_context(nc.sbuf_tensor(name, shape, dt))

        def sem(name):
            return ctx.enter_context(nc.semaphore(name))

        def lease(*tensors):
            with ExitStack() as own:
                return [own.enter_context(nc.sbuf_tensor(name, shape, dt)) for name, shape, dt in tensors]

        big = sb("big", [P, NKEY * T])
        resid = sb("resid", [P, NT, D])
        ident = sb("ident", [P, P])
        oi = sb("oi", [P, 2, P])
        ones, iota = oi[:, 0], oi[:, 1]
        act_j = oi[:].rearrange("p a b -> p (a b)")
        upper = sb("upper", [P, P])
        masks = sb("masks", [P, LEVELS + 1, P], U8)
        cols = sb("cols", [P, 94])
        mhalf = sb("mhalf", [P, 16])
        wh = sb("wh", [P, T], F32R)
        wl = sb("wl", [P, T], F32R)
        small = sb("small", [P, 512])
        ring, actT, mkv = lease(("ring", [P, RING, KC * TILE], F32), ("actT", [P, KC, T], F32), ("mkv", [P, 2, 1024], F32))
        raw, hi, lo, xh, xl = lease(("raw", [P, 2, 2, D], F32), ("hi", [P, 2, 2, D], F32R), ("lo", [P, 2, 2, D], F32R),
                                    ("xh", [P, KC, T], F32R), ("xl", [P, KC, T], F32R))
        mkT = mkv[:, 0].rearrange("p (h m) -> p h m", h=4)
        mv = mkv[:, 1].rearrange("p (n d) -> p n d", n=NT)
        ps = ctx.enter_context(nc.psum_tensor("ps", [P, 8, TILE], F32))

        C_N1, C_N2, C_PRE, C_MEM, C_LOG, C_BG, C_CONV, C_SB = 0, 8, 16, 24, 32, 40, 42, 90

        def arena(base, width):
            at = [0]

            def take(*shape, dt=F32):
                n = 1
                for s in shape:
                    n *= s
                assert at[0] + n <= width, (at[0], n)
                v = base[:, at[0]:at[0] + n]
                at[0] += n
                if dt is not F32:
                    v = v.bitcast(dt)
                if len(shape) == 1:
                    return v
                names = " ".join(f"a{i}" for i in range(len(shape)))
                return v.rearrange(f"p ({names}) -> p {names}", **{f"a{i}": s for i, s in enumerate(shape)})
            return take

        take_small = arena(small[:], 512)
        sumsq = take_small(NT)
        mean = take_small(NT)
        rstd = take_small(NT)
        lbe = take_small(2, 4)
        lbm = take_small(4)
        lbs = take_small(4)
        lbr = take_small(4)
        lb = take_small(4)
        lb1 = take_small(4)
        sumsq_o = take_small(NT, HEADS1)
        mean_o = take_small(NT, HEADS1)
        rstd_o = take_small(NT, HEADS1)
        sumsq_m = take_small(NT)
        mean_m = take_small(NT)
        rstd_m = take_small(NT)
        sumsq_h = take_small(NT)
        mean_h = take_small(NT)
        rstd_h = take_small(NT)
        esum = take_small(NT, PH)
        einv = take_small(NT, PH)

        take1 = arena(big[:], NKEY * T)
        scaled = take1(NT, D)
        qF = take1(NF, T)
        kF = take1(NF, T)
        gF = take1(NF, T)
        cum = take1(NF, T)
        dec = take1(2, NF, T)
        qd = take1(2, NF, T)
        kd = take1(2, NF, T)
        vtok = take1(NT, D)
        gate1 = take1(NT, D)
        glowT = take1(T)
        gate_up = take1(2, P)[0:RANK]
        zg = gate1[:, 0, 0:TILE].rearrange("p (a t) -> p a t", a=2)
        zabs = gate1[:, 0, TILE:D].rearrange("p (a t) -> p a t", a=2)
        own = take1(NT, HEADS1, P)
        cross = take1(HEADS1, P)
        mixed = take1(NT, D)
        mixT = take1(KC, T)
        sqtmp = take1(NT, D)
        xi = take1(P, dt=I32)
        xj = take1(P, dt=I32)
        xx = take1(P, dt=I32)
        xf = take1(P)
        ge = cross
        gnorm = take1(2, P)
        glow_w = take1(KC, RANK)
        memtok = mixed

        x_loaded = sem("x_loaded")
        params_loaded = sem("params_loaded")
        mem_loaded = sem("mem_loaded")
        tile_loaded = [sem(f"tile_loaded{i}") for i in range(RING)]
        consts_made = sem("consts_made")
        pool_step = sem("pool_step")
        dve_step = sem("dve_step")
        act_step = sem("act_step")
        sumsq_done = sem("sumsq_done")
        rstd_done = sem("rstd_done")
        scaled_done = sem("scaled_done")
        transposed = sem("transposed")
        actT_done = [sem("actT_by_act"), sem("actT_by_dve")]
        group_done = sem("group_done")
        group_out = sem("group_out")
        fgate_done = sem("fgate_done")
        logf_done = sem("logf_done")
        gate_mm = sem("gate_mm")
        softplus_done = sem("softplus_done")
        cum_done = sem("cum_done")
        keys_done = sem("keys_done")
        lb_in = sem("lb_in")
        lb_exp = sem("lb_exp")
        own_diag = sem("own_diag")
        gates_done = sem("gates_done")
        lvl_init = sem("lvl_init")
        scores_in = sem("scores_in")
        masks_done = sem("masks_done")
        lvl_exponent = sem("lvl_exponent")
        lvl_decay = sem("lvl_decay")
        lvl_scaled = sem("lvl_scaled")
        lvl_scores = sem("lvl_scores")
        lvl_kept = sem("lvl_kept")
        cross_out = sem("cross_out")
        o_done = sem("o_done")
        osq_done = sem("osq_done")
        osum_done = sem("osum_done")
        orstd_done = sem("orstd_done")
        mixed_done = sem("mixed_done")
        wout_done = sem("wout_done")
        h_done = sem("h_done")
        sub_done = sem("sub_done")
        sub_out = sem("sub_out")
        picks_done = sem("picks_done")
        pick_mm = sem("pick_mm")
        pickT_done = sem("pickT_done")
        soft_in = sem("soft_in")
        soft_exp = sem("soft_exp")
        onehot_ready = sem("onehot_ready")
        g_mm = sem("g_mm")
        g_out = sem("g_out")
        u_loaded = [sem(f"u_loaded{i}") for i in range(2)]
        v_loaded = [sem(f"v_loaded{i}") for i in range(2)]
        u_mm = sem("u_mm")
        gelu_done = sem("gelu_done")
        prod_done = sem("prod_done")
        wh_done = sem("wh_done")
        wl_done = sem("wl_done")
        hi_done = [sem("u_hi_done"), sem("v_hi_done")]
        lo_done = [sem("u_lo_done"), sem("v_lo_done")]
        x_round = sem("x_round")
        x_split = sem("x_split")
        mkv_stored = sem("mkv_stored")
        mkv_loaded = sem("mkv_loaded")
        v_mm = sem("v_mm")
        peer_out = sem("peer_out")

        t["mkv_keep"] = nc.dram_tensor("mkv_keep", (P, 2048), F32, kind="Internal").ap()

        def wtile(name, c0, n=TILE):
            src = t[name][:, c0:c0 + n].rearrange("(c p) n -> p c n", p=P)
            return lambda s: (ring[:, s, 0:KC * n].rearrange("p (c n) -> p c n", c=KC), src)

        tiles1 = [("hq", wtile("w_in", HQ)), ("hf", wtile("w_in", HF)), ("gqk", wtile("w_in", GQ)),
                  ("hi", wtile("w_in", HI)), ("gv", wtile("w_in", GV)),
                  ("hgate", wtile("w_in", HGATE)), ("ggate", wtile("w_in", GGATE)),
                  ("mk", wtile("w_mem_kv_2", 0)), ("mv", wtile("w_mem_kv_2", TILE)),
                  ("wo0", wtile("w_out", 0)), ("wo1", wtile("w_out", TILE)),
                  ("wq0", wtile("peer_w_q", 0)), ("wq1", wtile("peer_w_q", TILE)),
                  ("wq2", wtile("peer_w_q", 2 * TILE)), ("wq3", wtile("peer_w_q", 3 * TILE)),
                  ("subkeys", lambda s: (ring[:, s, 0:HP * NKEY], t["sub_keys_t"]))]
        tile_no = {name: i for i, (name, _) in enumerate(tiles1)}
        N1 = len(tiles1)

        def slot(name):
            return tile_no[name] % RING

        def tile_view(name):
            return ring[:, slot(name), :].rearrange("p (c n) -> p c n", c=KC)

        groups1 = ["hq0", "hq1", "hf0", "hf1", "gqk0", "gqk1", "glow", "hi0", "hi1", "gv0", "gv1",
                   "hgate0", "hgate1", "ggate0", "ggate1", "mk0", "mk1", "mv0", "mv1",
                   "wq00", "wq01", "wq10", "wq11", "wq20", "wq21", "wq30", "wq31"]
        group_no = {g: i for i, g in enumerate(groups1)}

        def gbank(g):
            return group_no[g] % 4

        def tile_used(name):
            if name == "subkeys":
                return sub_done, 8
            if name in ("wo0", "wo1"):
                return wout_done, 2 * int(name[2]) + 2
            return group_done, group_no[name + "1"] + 1

        takeP = arena(big[:], NKEY * T)
        scaled_p = takeP(NT, D)
        qT = takeP(HP, T)
        ssb = takeP(NT, HP, NKEY)
        srest = takeP(HP, NKEY)
        stop_ = takeP(NT, HP, TOP)
        sidx = takeP(NT, HP, TOP, dt=U32)
        sidxf = takeP(NT, HP, TOP)
        cand = takeP(PH, TOP * TOP)
        crest = takeP(PH, TOP * TOP)
        best = takeP(NT, PH, TOP)
        pos = takeP(NT, PH, TOP, dt=U32)
        posi = takeP(2, PH, TOP, dt=U32)
        posf = takeP(2, PH, TOP)
        pick = takeP(PH, TOP, TOP)
        chosen = takeP(NT, 3, SLOTS)
        G = big[:].rearrange("p (t j) -> p t j", j=NKEY)
        takeR = arena(ring[:, 2, :], KC * TILE)
        chosenT = takeR(3, T)
        hotA = takeR(2, GT, NKEY)
        hotB = takeR(2, GT, NKEY)
        xround = takeP(KC, T)
        U, V = 0, 1

        take2 = arena(big[:], NKEY * T)
        u1 = take2(3108)
        u2 = take2(2048)
        u3 = take2(3072)
        u4 = take2(3072)
        u5 = take2(2048)
        u6 = take2(3072 + 512)
        zdn = take2(NT, TILE)
        gu = take2(NT, TILE)
        gv2 = take2(NT, TILE)
        gz = take2(NT, TILE)
        swqT = take2(4, T)
        swkv = take2(TILE)
        swz = take2(NT, TILE)
        prob = take2(3072)
        probT = take2(3072)
        xmqT = take2(4, T)
        xmz = take2(NT, TILE)
        rows = take2(656)
        window = take2(2, P)
        gm_gain, dn_gain = rows[:, 0:TILE], rows[:, TILE:TILE + P]
        a_log, dt_bias, sinks = rows[:, 640:644], rows[:, 644:648], rows[:, 648:656]
        scaled2 = u1[:, 0:2048].rearrange("p (n d) -> p n d", n=NT)
        convin = u1.rearrange("p (f t) -> p f t", f=3 * DH)
        a1 = arena(u1, 3108)
        LT, AQ, BT = a1(TH, P), a1(TH, P), a1(TH, P)
        norm_f = u2[:, 0:D]
        sqk = u2.rearrange("p (f t) -> p f t", f=2 * DH)
        a2 = arena(u2, 2048)
        X, Z = a2(TH, P), a2(TH, P)
        rep = u3.rearrange("p (a h m) -> p a h m", a=3, h=TH)
        a3 = arena(u3, 3072)
        Y, kbg, vb = a3(TH, P), a3(TH, P), a3(TH, P)
        convT = u4.rearrange("p (f t) -> p f t", f=3 * DH)
        a5 = arena(u5, 2048)
        du, wT, S1 = a5(TH, P), a5(DH, P), a5(DH, P)
        a6 = arena(u6, 3584)
        Dm, brow, qrow, qg = a6(TH, P), a6(TH, P), a6(TH, P), a6(DH, P)
        a3b = arena(brow.rearrange("p h c -> p (h c)"), 1024)
        kdl, vnew = a3b(DH, P), a3b(DH, P)
        wsT = probT[:, 0:4 * P].rearrange("p (g q) -> p g q", g=4)
        swkT, swv = swkv[:, 0:T], swkv[:, T:2 * T].rearrange("p (n d) -> p n d", n=NT)
        take3 = arena(big[:, 0:17000], 17000)
        yT = take3(NBR * 4, T)
        gsb = take3(2, 4, TILE)
        merged = take3(NT, D)
        outsb = take3(NT, D)
        norm_post = take3(D)
        sumsq_f, mean_f, rstd_f = (take_small(NT) for _ in range(3))
        sumsq_x, mean_x, rstd_x = (take_small(NT) for _ in range(3))
        sumsq_p, mean_p, rstd_p = (take_small(NT) for _ in range(3))
        ba_w = take_small(KC, 2 * DH)
        ba = take_small(NT, 2 * DH)
        beta = take_small(NT, DH)
        dz = take_small(NT, DH)
        dsp = take_small(NT, DH)
        nega = take_small(DH)
        dg = take_small(NT, DH)
        rin = take_small(NT, 2 * DH)
        rr = take_small(NT, 2 * DH)
        gcs = take_small(2, TH)
        egc = take_small(NT, DH)
        ekd = take_small(DH)
        brk = take_small(NT, DH)
        rqs = take_small(NT, DH)
        kbf = take_small(NT, DH)
        sumsq_a, mean_a, rstd_a = (take_small(NT, DH) for _ in range(3))
        sumsq_v, mean_v, rstd_v = (take_small(NT) for _ in range(3))
        smax, snm, sden, srec, ssk = (take_small(NT, SH) for _ in range(5))
        xmax, xnm, xden, xrec = (take_small(NT, XH) for _ in range(4))

        rows_loaded = sem("rows_loaded")
        post_loaded = sem("post_loaded")
        ws_loaded = sem("ws_loaded")
        x1_done = sem("x1_done")
        g2_done = sem("g2_done")
        g2_out = sem("g2_out")
        conv_done = sem("conv_done")
        conv_zero = sem("conv_zero")
        dnsilu_done = sem("dnsilu_done")
        dnsq_done = sem("dnsq_done")
        ss_mm = sem("ss_mm")
        rin_done = sem("rin_done")
        rr_done = sem("rr_done")
        beta_done = sem("beta_done")
        dz_done = sem("dz_done")
        dln_done = sem("dln_done")
        dg_done = sem("dg_done")
        gc_mm = sem("gc_mm")
        gcs_done = sem("gcs_done")
        egc_done = sem("egc_done")
        rep_done = sem("rep_done")
        row_mm = sem("row_mm")
        dm_in = sem("dm_in")
        dm_done = sem("dm_done")
        brow_done = sem("brow_done")
        qrow_done = sem("qrow_done")
        kk_mm = sem("kk_mm")
        lt_done = sem("lt_done")
        qk_mm = sem("qk_mm")
        aq_done = sem("aq_done")
        kv_tr = sem("kv_tr")
        kv_out = sem("kv_out")
        z0_done = sem("z0_done")
        x0_tr = sem("x0_tr")
        x_done = sem("x_done")
        bt_done = sem("bt_done")
        y_mm = sem("y_mm")
        y_out = sem("y_out")
        px_mm = sem("px_mm")
        pz_mm = sem("pz_mm")
        z_done = sem("z_done")
        u_out_mm = sem("u_out_mm")
        du_done = sem("du_done")
        wt_done = sem("wt_done")
        s1_mm = sem("s1_mm")
        s1_done = sem("s1_done")
        ws_mm = sem("ws_mm")
        vnew_done = sem("vnew_done")
        qg_done = sem("qg_done")
        do_mm = sem("do_mm")
        dosq_done = sem("dosq_done")
        dosum_done = sem("dosum_done")
        dors_done = sem("dors_done")
        y_done = [sem(f"y_done{n}") for n in range(NBR)]
        gmv_sq = sem("gmv_sq")
        gmv_rstd = sem("gmv_rstd")
        gmv_done = sem("gmv_done")
        gm_mm = sem("gm_mm")
        ss_mm2 = sem("sw_scores")
        s_masked = sem("sw_masked")
        s_exp = sem("sw_exp")
        s_tr = sem("sw_transposed")
        s_trout = sem("sw_probT")
        so_mm = sem("sw_out")
        xs_mm = sem("xm_scores")
        xs_max = sem("xm_max")
        xs_exp = sem("xm_exp")
        xs_tr = sem("xm_transposed")
        xs_trout = sem("xm_probT")
        xo_mm = sem("xm_out")
        yT_mm = sem("yT_mm")
        yT_done = sem("yT_done")
        gate_out = sem("gate_out")
        up_mm = sem("up_mm")
        up_out = sem("up_out")
        merged_done = sem("merged_done")
        fin_mm = sem("fin_mm")
        fin_copied = sem("fin_copied")
        out_done = sem("out_done")
        stored = sem("stored")

        def up_tile(n):
            src = t["w_up_2"][n].rearrange("(c p) n -> p c n", p=P)
            return lambda s: (ring[:, s, :].rearrange("p (c n) -> p c n", c=4), src)

        tiles2 = [(name, wtile("w_in_2", c)) for name, c in
                  (("dnq", DNQ), ("dnk", DNK), ("dnv", DNV), ("dnz", DNZ), ("gmu", GMU), ("gmv", GMV),
                   ("gmz", GMZ))]
        tiles2 += [("swq", wtile("w_swq_2", 0)), ("swkv", wtile("w_in_2", SWKV, T)), ("swz", wtile("w_in_2", SWZ)),
                   ("xmq", wtile("w_in_2", XMQ)), ("xmz", wtile("w_in_2", XMZ))]
        for n in range(NBR):
            tiles2 += [(f"gate{n}{h}", wtile("w_in_2", GATES + n * D + h * TILE)) for h in range(2)]
            tiles2 += [(f"up{n}", up_tile(n))]
        tiles2 += [("out0", wtile("w_out_2", 0)), ("out1", wtile("w_out_2", TILE))]
        tile2_no = {name: i for i, (name, _) in enumerate(tiles2)}
        loads1 = [len(range(s, N1, RING)) for s in range(RING)]
        groups2 = ["dnq0", "dnq1", "dnk0", "dnk1", "dnv0", "dnv1", "ba", "dnz0", "dnz1", "gmu0", "gmu1", "gmv0", "gmv1",
                   "gmz0", "gmz1", "swq0", "swq1", "swkv", "swz0", "swz1", "xmq0", "xmq1", "xmz0", "xmz1"]
        for n in range(NBR):
            groups2 += [f"gate{n}{h}{k}" for h in range(2) for k in range(NT)]
        g2_no = {g: i for i, g in enumerate(groups2)}

        def tile2_used(name):
            if name[:2] == "up":
                return up_mm, 4 * int(name[2]) + 4
            if name[:3] == "out":
                return fin_mm, 2 * int(name[3]) + 2
            return g2_done, g2_no["swkv" if name == "swkv" else name + "1"] + 1

        block = ctx.enter_context(nc.Block())

        @block.sync
        def _(sp):
            sp.dma_start(resid[:], t["x"].rearrange("b (n p) d -> p (b n) d", p=P)).then_inc(x_loaded, 16)
            sp.wait_ge(params_loaded, 80)
            for k, (name, make) in enumerate(tiles1):
                if k == RING:
                    sp.dma_start(memtok, t["mem_2"].rearrange("b (n p) d -> p (b n) d", p=P)).then_inc(mem_loaded, 16)
                if k >= RING:
                    sp.wait_ge(*tile_used(tiles1[k - RING][0]))
                dst, src = make(k % RING)
                sp.dma_start(dst, src).then_inc(tile_loaded[k % RING], 16)
            sp.wait_ge(group_out, group_no["mv1"] + 1)
            sp.dma_start(t["mkv_keep"], mkv[:].rearrange("p a n -> p (a n)")).then_inc(mkv_stored, 16)
            sp.wait_ge(*tile_used("wq3"))
            sp.wait_ge(*tile_used("subkeys"))
            loaded = (u_loaded, v_loaded)

            def load_rows(which, j, par, before=None):
                if before is not None:
                    sp.wait_ge(lo_done[which], before)
                sp.dma_start(raw[:, which, par], t[("u_t", "v_t")[which]][bass.ds(j, 1), :, :].rearrange("o p n -> p (o n)")).then_inc(loaded[which][par], 16)

            for j in range(2):
                load_rows(U, j, j)
                load_rows(V, j, j)
            with sp.Fori(1, NKEY // 2) as i:
                for par in range(2):
                    load_rows(U, 2 * i + par, par, 2 * i + (par - 1))
                    load_rows(V, 2 * i + par, par, 2 * i + (par - 1))
            sp.wait_ge(prod_done, NKEY)
            sp.dma_start(norm_f, t["norm_f_g"].partition_broadcast(P)).then_inc(rows_loaded, 16)
            sp.dma_start(rows, t["rows"].partition_broadcast(P)).then_inc(rows_loaded, 16)
            sp.dma_start(ba_w, t["w_in_2"][:, DNBA:DNBA + 2 * DH].rearrange("(c p) n -> p c n", p=P)).then_inc(rows_loaded, 16)
            sp.dma_start(wsT, t["spatial_w_t"].rearrange("p (g q) -> p g q", g=4)).then_inc(ws_loaded, 16)
            sp.wait_ge(u_mm, NKEY)
            sp.wait_ge(mkv_stored, 16)
            sp.dma_start(mkv[:].rearrange("p a n -> p (a n)"), t["mkv_keep"]).then_inc(mkv_loaded, 16)
            sp.wait_ge(v_mm, NKEY)
            for k, (name, make) in enumerate(tiles2):
                if k >= RING:
                    sp.wait_ge(*tile2_used(tiles2[k - RING][0]))
                dst, src = make(k % RING)
                sp.dma_start(dst, src).then_inc(tile_loaded[k % RING], 16)
            sp.dma_start(norm_post, t["norm_post_2"][0].partition_broadcast(P)).then_inc(post_loaded, 16)
            for n in range(NT):
                sp.wait_ge(out_done, n + 1)
                sp.dma_start(out[0, n * P:(n + 1) * P, :], outsb[:, n]).then_inc(stored, 16)
            sp.wait_ge(stored, 16 * NT)

        @block.gpsimd
        def _(pool):
            steps = [0]

            def link(ins):
                steps[0] += 1
                ins.then_inc(pool_step, 1)
                pool.wait_ge(pool_step, steps[0])

            def rsqrt(o, m, s, width, n):
                link(pool.tensor_scalar(m, s, 1.0 / width, EPS, ALU.mult, ALU.add))
                return pool.tensor_tensor(o, m, n, ALU.pow)

            pool.memset(ident[:], 0.0).then_inc(pool_step, 1)
            pool.memset(ones, 1.0).then_inc(pool_step, 1)
            pool.memset(mhalf[:], -0.5).then_inc(pool_step, 1)
            steps[0] = 3
            pool.wait_ge(pool_step, 3)
            pool.affine_select(out=ident[:], in_=ident[:], compare_op=ALU.not_equal, fill=1.0, base=0,
                               pattern=[[-1, P]], channel_multiplier=1)
            pool.affine_select(out=upper[:], in_=ones, compare_op=ALU.is_ge, fill=0.0, base=0,
                               pattern=[[1, P]], channel_multiplier=-1)
            pool.iota(iota, pattern=[[1, P]], base=0, channel_multiplier=0, allow_small_or_imprecise_dtypes=True)
            pool.iota(xi, pattern=[[1, P]], base=0, channel_multiplier=0)
            pool.iota(xj, pattern=[[0, P]], base=0, channel_multiplier=1).then_inc(consts_made, 1)
            pool.wait_ge(sumsq_done, 2)
            rsqrt(rstd, mean, sumsq, D, mhalf[:, 0:NT]).then_inc(rstd_done, 1)
            pool.wait_ge(sumsq_done, 4)
            rsqrt(rstd_m, mean_m, sumsq_m, D, mhalf[:, 0:NT]).then_inc(rstd_done, 1)
            for l in range(LEVELS):
                m = 1 << l
                if l == 0:
                    pool.wait_ge(cum_done, 2 * NF)
                if l >= 2:
                    pool.wait_ge(lvl_scaled, l - 1)
                c = cum.rearrange("p f (b two m) -> p (f b) two m", two=2, m=m)
                d = dec[:, l % 2].rearrange("p f (b two m) -> p (f b) two m", two=2, m=m)
                mid = c[:, :, 0, m - 1:m].broadcast_to([P, NF * T // (2 * m), m])
                pool.tensor_tensor(d[:, :, 1, :], c[:, :, 1, :], mid, ALU.subtract)
                pool.tensor_tensor(d[:, :, 0, :], mid, c[:, :, 0, :], ALU.subtract).then_inc(lvl_exponent, 1)
            pool.wait_ge(lvl_scaled, LEVELS - 1)
            last = cum[:, :, P - 1:P].broadcast_to([P, NF, P])
            pool.tensor_tensor(dec[:, 1, :, 0:P], last, cum[:, :, 0:P], ALU.subtract).then_inc(lvl_exponent, 1)
            for n in range(NT):
                pool.wait_ge(osum_done, n + 1)
                rsqrt(rstd_o[:, n], mean_o[:, n], sumsq_o[:, n], P, mhalf[:, 0:HEADS1]).then_inc(orstd_done, 1)
            pool.wait_ge(sumsq_done, 6)
            rsqrt(rstd_h, mean_h, sumsq_h, D, mhalf[:, 0:NT]).then_inc(rstd_done, 1)
            pool.wait_ge(wl_done, NKEY)
            pool.memset(ones, 1.0).then_inc(consts_made, 1)
            pool.wait_ge(sumsq_done, 8)
            rsqrt(rstd_f, mean_f, sumsq_f, D, mhalf[:, 0:NT]).then_inc(rstd_done, 1)
            pool.wait_ge(sumsq_done, 10)
            rsqrt(rstd_x, mean_x, sumsq_x, D, mhalf[:, 0:NT]).then_inc(rstd_done, 1)
            pool.wait_ge(rin_done, 1)
            pool.tensor_tensor(rr.rearrange("p n f -> p (n f)"), rin.rearrange("p n f -> p (n f)"), mhalf[:], ALU.pow).then_inc(rr_done, 1)
            pool.wait_ge(gmv_sq, 2)
            rsqrt(rstd_v, mean_v, sumsq_v, TILE, mhalf[:, 0:NT]).then_inc(gmv_rstd, 1)
            for n in range(NT):
                pool.wait_ge(dosum_done, n + 1)
                rsqrt(rstd_a[:, n], mean_a[:, n], sumsq_a[:, n], HEAD, mhalf[:, 0:DH]).then_inc(dors_done, 1)
            pool.wait_ge(sumsq_done, 12)
            rsqrt(rstd_p, mean_p, sumsq_p, D, mhalf[:, 0:NT]).then_inc(rstd_done, 1)

        @block.scalar
        def _(act):
            steps = [0]

            def link(ins):
                steps[0] += 1
                ins.then_inc(act_step, 1)
                act.wait_ge(act_step, steps[0])

            act.dma_start(cols[:], t["cols"]).then_inc(params_loaded, 16)
            act.dma_start(glow_w, t["w_in"][:, GLOW:GLOW + RANK].rearrange("(c p) n -> p c n", p=P)).then_inc(params_loaded, 16)
            act.dma_start(gate_up.rearrange("p a n -> p (a n)"), t["gla_w_gate_up"][0]).then_inc(params_loaded, 16)
            act.dma_start(gnorm[:, 0], t["hg_norm_g"][0].partition_broadcast(P)).then_inc(params_loaded, 16)
            act.dma_start(gnorm[:, 1], t["gla_norm_g"][0].partition_broadcast(P)).then_inc(params_loaded, 16)
            act.wait_ge(x_loaded, 16)
            for n in range(NT):
                act.activation(sqtmp[:, n], resid[:, n], ACT.Square, accum_out=sumsq[:, n:n + 1]).then_inc(sumsq_done, 1)
            act.wait_ge(params_loaded, 80)
            act.wait_ge(lb_in, 1)
            act.activation(lbe.rearrange("p a f -> p (a f)"), lbe.rearrange("p a f -> p (a f)"), ACT.Exp).then_inc(lb_exp, 1)

            def copy_out_T(n_before, dst, gcol=None, first=4):
                for c in (2, 3, 6, 7):
                    act.wait_ge(transposed, n_before + c // 2 + 1)
                    src = ps[:, 4 + c // 2, (c % 2) * T:(c % 2 + 1) * T]
                    if gcol is None:
                        ins = act.activation(dst[:, c], src, ACT.Copy)
                    else:
                        ins = act.activation(dst[:, c], src, ACT.Copy, scale=cols[:, gcol + c:gcol + c + 1])
                    ins.then_inc(actT_done[0], 1)

            copy_out_T(0, actT, C_N1)

            def from_group(g):
                act.wait_ge(group_done, group_no[g] + 1)
                return ps[:, gbank(g), :]

            def out_group(g, dst, func, **kw):
                act.activation(dst, from_group(g), func, **kw).then_inc(group_out, 1)

            def feat(ap):
                return ap.rearrange("p f t -> p (f t)")

            for a in range(2):
                out_group(f"hq{a}", feat(qF[:, 2 * a:2 * a + 2]), ACT.Silu)
            for a in range(2):
                out_group(f"hf{a}", feat(gF[:, 2 * a:2 * a + 2]), ACT.Sigmoid)
            out_group("gqk0", feat(qF[:, 4:6]), ACT.Copy, scale=GLA_SCALE)
            out_group("gqk1", feat(kF[:, 4:6]), ACT.Copy)
            act.wait_ge(group_done, group_no["glow"] + 1)
            act.activation(glowT[0:RANK], ps[0:RANK, gbank("glow"), 0:T], ACT.Copy).then_inc(group_out, 1)
            act.wait_ge(mem_loaded, 16)
            act.wait_ge(scaled_done, 2)
            for n in range(NT):
                act.activation(sqtmp[:, n], memtok[:, n], ACT.Square, accum_out=sumsq_m[:, n:n + 1]).then_inc(sumsq_done, 1)
            act.wait_ge(fgate_done, 1)
            act.activation(feat(gF[:, 0:4]), feat(gF[:, 0:4]), ACT.Ln).then_inc(logf_done, 1)
            act.wait_ge(gate_mm, 1)
            for a in range(2):
                act.activation(zg[:, a], ps[:, 7, a * T:(a + 1) * T], ACT.Identity,
                               bias=cols[:, C_BG + a:C_BG + a + 1]).then_inc(act_step, 1)
            steps[0] += 2
            act.wait_ge(act_step, steps[0])
            link(act.activation(feat(zabs), feat(zg), ACT.Abs))
            link(act.activation(feat(zabs), feat(zabs), ACT.Exp, scale=-1.0))
            act.activation(feat(zabs), feat(zabs), ACT.Ln, bias=1.0).then_inc(softplus_done, 1)
            for a in range(NT):
                out_group(f"hi{a}", vtok[:, a, 0:TILE], ACT.Copy)
            for a in range(NT):
                out_group(f"gv{a}", vtok[:, a, TILE:D], ACT.Copy)
            copy_out_T(4, mixT, C_MEM)
            for l in range(LEVELS):
                act.wait_ge(lvl_exponent, l + 1)
                act.activation(feat(dec[:, l % 2]), feat(dec[:, l % 2]), ACT.Exp).then_inc(lvl_decay, 1)
            act.wait_ge(lvl_exponent, LEVELS + 1)
            act.activation(dec[:, 1, :, 0:P], dec[:, 1, :, 0:P], ACT.Exp)
            act.activation(dec[:, 1, :, P:T], cum[:, :, P:T], ACT.Exp).then_inc(lvl_decay, 1)
            for g, dst, f in (("hgate0", gate1[:, 0, 0:TILE], ACT.Silu), ("hgate1", gate1[:, 1, 0:TILE], ACT.Silu),
                              ("ggate0", gate1[:, 0, TILE:D], ACT.Silu), ("ggate1", gate1[:, 1, TILE:D], ACT.Silu),
                              ("mk0", feat(mkT[:, 0:2]), ACT.Copy), ("mk1", feat(mkT[:, 2:4]), ACT.Copy),
                              ("mv0", mv[:, 0], ACT.Copy), ("mv1", mv[:, 1], ACT.Copy)):
                out_group(g, dst, f)
            act.wait_ge(lvl_scores, 2 * (LEVELS + 1) + 1)
            act.activation(cross.rearrange("p h i -> p (h i)"), ps[:, 4:6, :].rearrange("p b n -> p (b n)"), ACT.Copy).then_inc(cross_out, 1)
            for n in range(NT):
                act.wait_ge(o_done, n + 1)
                act.activation(sqtmp[:, n], ps[:, 4 + 2 * n:6 + 2 * n, :].rearrange("p b n -> p (b n)"), ACT.Square).then_inc(osq_done, 1)
            copy_out_T(8, mixT)
            act.wait_ge(h_done, 4)
            for n in range(NT):
                act.activation(sqtmp[:, n], resid[:, n], ACT.Square, accum_out=sumsq_h[:, n:n + 1]).then_inc(sumsq_done, 1)
            copy_out_T(12, actT, C_N2)
            for a in range(4):
                for b in range(2):
                    out_group(f"wq{a}{b}", feat(qT[:, 4 * a + 2 * b:4 * a + 2 * b + 2]), ACT.Copy)
            for k in range(8):
                act.wait_ge(sub_done, k + 1)
                act.activation(ssb[:, k // 4, 4 * (k % 4):4 * (k % 4) + 4].rearrange("p a n -> p (a n)"), ps[:, 4 + k % 4, :], ACT.Copy).then_inc(sub_out, 1)
            act.activation(feat(xround.bitcast(F32R)), feat(actT), ACT.Copy).then_inc(x_round, 1)
            for n in range(NT):
                act.wait_ge(soft_in, n + 1)
                e = best[:, n].rearrange("p h k -> p (h k)")
                act.activation(e, e, ACT.Exp).then_inc(soft_exp, 1)

            def g_evac(n, at, par):
                act.wait_ge(g_mm, n)
                act.activation(G[:, at, :].rearrange("p t j -> p (t j)"), ps[:, par, :], ACT.Copy).then_inc(g_out, 1)

            act.wait_ge(x_split, 2)
            act.wait_ge(pickT_done, 2)
            with act.Fori(0, NGRP // 2) as i:
                for par in range(2):
                    g_evac(2 * i + (par + 1), bass.ds(i * (2 * GT) + par * GT, GT), par)

            loaded = (u_loaded, v_loaded)

            def split_hi(which, loads, par):
                act.wait_ge(loaded[which][par], loads)
                act.activation(hi[:, which, par], raw[:, which, par], ACT.Copy).then_inc(hi_done[which], 1)

            def second_key(n, loads, par, first=False, last=False, wait=True):
                if wait:
                    act.wait_ge(v_mm, n - 2)
                split_hi(V, loads, par)
                act.wait_ge(u_mm, n)
                if not first:
                    act.wait_ge(wl_done, n - 1)
                act.activation(act_j, ps[:, par, 0:T], ACT.Gelu).then_inc(gelu_done, 1)
                if not last:
                    split_hi(U, loads + 16, par)
                act.wait_ge(prod_done, n)
                if not first:
                    act.wait_ge(v_mm, n - 1)
                act.activation(wh[:], act_j, ACT.Copy).then_inc(wh_done, 1)

            act.wait_ge(pickT_done, 2)
            for par in range(2):
                split_hi(U, 16, par)
            second_key(1, 16, 0, first=True, wait=False)
            second_key(2, 16, 1, wait=False)
            with act.Fori(1, NKEY // 2 - 1) as i:
                for par in range(2):
                    second_key(2 * i + (par + 1), 16 * i + 16, par)
            for par in range(2):
                second_key(NKEY - 1 + par, 8 * NKEY, par, last=True)
            def sums_of_squares(src, dst):
                for n in range(NT):
                    act.activation(sq2[:, n], src[:, n], ACT.Square, accum_out=dst[:, n:n + 1]).then_inc(sumsq_done, 1)

            sq2 = probT[:, 512:512 + 2 * D].rearrange("p (n d) -> p n d", n=NT)
            act.wait_ge(peer_out, 4)
            sums_of_squares(resid, sumsq_f)
            act.wait_ge(x1_done, NT)
            act.wait_ge(sumsq_done, 8)
            sums_of_squares(resid, sumsq_x)
            copy_out_T(16, actT, C_PRE)

            def from2(g):
                act.wait_ge(g2_done, g2_no[g] + 1)
                return ps[:, g2_no[g] % 4, :]

            def out2(g, dst, func, **kw):
                act.activation(dst, from2(g), func, **kw).then_inc(g2_out, 1)

            def flat(ap):
                return ap.rearrange("p a b -> p (a b)")

            act.wait_ge(conv_zero, 1)
            for k, name in enumerate(("dnq", "dnk", "dnv")):
                for a in range(2):
                    f = 4 * k + 2 * a
                    act.activation(convin[:, f:f + 2, CONV - 1:], from2(f"{name}{a}").rearrange("p (f t) -> p f t", f=2), ACT.Copy).then_inc(g2_out, 1)
            act.wait_ge(g2_done, g2_no["ba"] + 1)
            act.activation(flat(ba), ps[:, g2_no["ba"] % 4, 0:2 * TH], ACT.Copy).then_inc(g2_out, 1)
            act.wait_ge(g2_out, g2_no["ba"] + 1)
            act.activation(beta, ba[:, :, 0:DH], ACT.Sigmoid).then_inc(beta_done, 1)
            for k in range(3):
                act.wait_ge(conv_done, k + 1)
                act.activation(flat(convT[:, 4 * k:4 * k + 4]), flat(convT[:, 4 * k:4 * k + 4]), ACT.Silu).then_inc(dnsilu_done, 1)
            act.wait_ge(dnsilu_done, 2)
            act.activation(flat(sqk), flat(convT[:, 0:2 * DH]), ACT.Square).then_inc(dnsq_done, 1)
            for a in range(NT):
                out2(f"dnz{a}", zdn[:, a], ACT.Silu)
            act.wait_ge(dz_done, 1)
            link(act.activation(flat(dsp), flat(dz), ACT.Abs))
            link(act.activation(flat(dsp), flat(dsp), ACT.Exp, scale=-1.0))
            act.activation(flat(dsp), flat(dsp), ACT.Ln, bias=1.0)
            act.activation(nega, a_log, ACT.Exp).then_inc(dln_done, 1)
            for a in range(NT):
                out2(f"gmu{a}", gu[:, a], ACT.Gelu_apprx_tanh)
            act.wait_ge(gcs_done, 2)
            act.activation(flat(egc), gcs[:, 0], ACT.Exp)
            act.activation(ekd, ekd, ACT.Exp).then_inc(egc_done, 1)
            for a in range(NT):
                out2(f"gmv{a}", gv2[:, a], ACT.Gelu_apprx_tanh)
            act.wait_ge(g2_out, g2_no["gmv1"] + 1)
            for n in range(NT):
                act.activation(prob[:, n * TILE:(n + 1) * TILE], gv2[:, n], ACT.Square, accum_out=sumsq_v[:, n:n + 1]).then_inc(gmv_sq, 1)
            for a in range(NT):
                out2(f"gmz{a}", gz[:, a], ACT.Silu)
            act.wait_ge(row_mm, 2)
            act.activation(flat(brow), ps[:, 6:8, :].rearrange("p b n -> p (b n)"), ACT.Copy).then_inc(brow_done, 1)
            act.wait_ge(dm_in, 1)
            act.activation(flat(qg), ps[:, 5, :], ACT.Exp)
            act.activation(flat(Dm), flat(Dm), ACT.Exp).then_inc(dm_done, 1)
            for a in range(2):
                out2(f"swq{a}", flat(swqT[:, 2 * a:2 * a + 2]), ACT.Copy)
            act.wait_ge(row_mm, 3)
            act.activation(flat(qrow), ps[:, 4:6, :].rearrange("p b n -> p (b n)"), ACT.Copy).then_inc(qrow_done, 1)
            out2("swkv", swkv, ACT.Copy)
            act.wait_ge(x0_tr, 1)
            act.activation(flat(X), ps[:, 4:6, :].rearrange("p b n -> p (b n)"), ACT.Copy).then_inc(x_done, 1)
            for l in range(1, LEVELS):
                for n in range(NT):
                    act.wait_ge(y_mm, NT * (l - 1) + n + 1)
                    act.activation(flat(Y[:, 4 * n:4 * n + 4]), ps[:, 4 + n, :], ACT.Copy).then_inc(y_out, 1)
                if l == 1:
                    for a in range(NT):
                        out2(f"swz{a}", swz[:, a], ACT.Silu)
                if l == 2:
                    for a in range(2):
                        out2(f"xmq{a}", flat(xmqT[:, 2 * a:2 * a + 2]), ACT.Copy)
                if l == 3:
                    for a in range(NT):
                        out2(f"xmz{a}", xmz[:, a], ACT.Silu)
            act.wait_ge(u_out_mm, 1)
            act.activation(flat(du), ps[:, 4:6, :].rearrange("p b n -> p (b n)"), ACT.Copy).then_inc(du_done, 1)
            act.activation(flat(wT), ps[:, 6, :], ACT.Copy).then_inc(wt_done, 1)
            act.wait_ge(s1_mm, 1)
            act.activation(flat(S1), ps[:, 7, :], ACT.Copy).then_inc(s1_done, 1)
            for n in range(NT):
                act.wait_ge(do_mm, n + 1)
                act.activation(prob[:, n * TILE:(n + 1) * TILE], ps[:, 4 + n, :], ACT.Square).then_inc(dosq_done, 1)
            off = 0
            for n in range(NT):
                width = (n + 1) * P
                pr = prob[:, off:off + SH * width].rearrange("p (h j) -> p h j", h=SH)
                prT = probT[:, off:off + SH * width]
                off += SH * width
                act.wait_ge(s_masked, n + 1)
                for h in range(SH):
                    act.activation(pr[:, h], pr[:, h], ACT.Exp, bias=snm[:, n, h:h + 1], accum_out=sden[:, n, h:h + 1])
                act.activation(ssk[:, n], ssk[:, n], ACT.Exp).then_inc(s_exp, 1)
                act.wait_ge(s_tr, n + 1)
                act.activation(prT, ps[:, (0 if n else 4):(4 if n else 6), :].rearrange("p b n -> p (b n)"), ACT.Copy).then_inc(s_trout, 1)
            for n in range(NT):
                pr = prob[:, n * 1024:(n + 1) * 1024].rearrange("p (h j) -> p h j", h=XH)
                prT = probT[:, n * 1024:(n + 1) * 1024]
                act.wait_ge(xs_max, n + 1)
                for h in range(XH):
                    ins = act.activation(pr[:, h], ps[:, 4 + 2 * n + h // 2, (h % 2) * T:(h % 2 + 1) * T], ACT.Exp, scale=HEAD ** -0.5,
                                         bias=xnm[:, n, h:h + 1], accum_out=xden[:, n, h:h + 1])
                ins.then_inc(xs_exp, 1)
            for n in range(NT):
                prT = probT[:, n * 1024:(n + 1) * 1024]
                act.wait_ge(xs_tr, n + 1)
                act.activation(prT, ps[:, 4 + 2 * n:6 + 2 * n, :].rearrange("p b n -> p (b n)"), ACT.Copy).then_inc(xs_trout, 1)
            for n in range(NBR):
                for k in range(4):
                    if n >= 2:
                        act.wait_ge(up_out, 4 * (n - 2) + k + 1)
                    out2(f"gate{n}{k // 2}{k % 2}", gsb[:, n % 2, k], ACT.Sigmoid)
            copy_out_T(20, actT)
            for n in range(NT):
                for h in range(2):
                    act.wait_ge(fin_mm, 2 * h + n + 1)
                    act.activation(outsb[:, n, h * TILE:(h + 1) * TILE], ps[:, 2 * h + n, :], ACT.Copy).then_inc(fin_copied, 1)
            act.wait_ge(fin_copied, 2 * NT)
            act.wait_ge(merged_done, 4)
            for n in range(NT):
                act.activation(merged[:, n], outsb[:, n], ACT.Square, accum_out=sumsq_p[:, n:n + 1]).then_inc(sumsq_done, 1)

        @block.vector
        def _(dve):
            steps = [0]

            def link(ins):
                steps[0] += 1
                ins.then_inc(dve_step, 1)
                dve.wait_ge(dve_step, steps[0])

            def mark(ins):
                steps[0] += 1
                ins.then_inc(dve_step, 1)

            def wait_marked():
                dve.wait_ge(dve_step, steps[0])

            mark(dve.memset(own, 0.0))
            mark(dve.memset(qd, 0.0))
            mark(dve.memset(kd, 0.0))
            dve.wait_ge(params_loaded, 80)
            logit = cols[:, C_LOG:C_LOG + 8].rearrange("p (a f) -> p a f", a=2)
            link(dve.tensor_tensor(lbm, logit[:, 0], logit[:, 1], ALU.max))
            dve.tensor_tensor(lbe, logit, bcast(lbm, 1, 2), ALU.subtract).then_inc(lb_in, 1)
            dve.wait_ge(rstd_done, 1)
            for n in range(NT):
                dve.tensor_scalar(scaled[:, n], resid[:, n], rstd[:, n:n + 1], None, ALU.mult).then_inc(scaled_done, 1)
            dve.wait_ge(params_loaded, 80)

            def copy_out_T(n_before, dst, gcol=None, first=4):
                for c in (0, 1, 4, 5):
                    dve.wait_ge(transposed, n_before + c // 2 + 1)
                    src = ps[:, 4 + c // 2, (c % 2) * T:(c % 2 + 1) * T]
                    if gcol is None:
                        ins = dve.tensor_copy(dst[:, c], src)
                    else:
                        ins = dve.tensor_scalar(dst[:, c], src, cols[:, gcol + c:gcol + c + 1], None, ALU.mult)
                    ins.then_inc(actT_done[1], 1)

            copy_out_T(0, actT, C_N1)
            dve.wait_ge(consts_made, 1)
            link(dve.tensor_tensor(xx, xi, xj, ALU.bitwise_xor))
            link(dve.tensor_copy(xf, xx))
            link(dve.tensor_tensor(xf, xf, upper[:], ALU.mult))
            for l in range(LEVELS + 1):
                mark(dve.tensor_scalar(ge[:, l], xf, float(1 << l), None, ALU.is_ge))
            wait_marked()
            dve.tensor_tensor(masks[:, 0:LEVELS], ge[:, 0:LEVELS], ge[:, 1:LEVELS + 1], ALU.subtract)
            dve.tensor_copy(masks[:, LEVELS], ident[:]).then_inc(masks_done, 1)
            dve.wait_ge(lb_exp, 1)
            link(dve.tensor_tensor(lbs, lbe[:, 0], lbe[:, 1], ALU.add))
            link(dve.reciprocal(lbr, lbs))
            link(dve.tensor_tensor(lb, lbe[:, 0], lbr, ALU.mult))
            link(dve.tensor_scalar(lb1, lb, -1.0, 1.0, ALU.mult, ALU.add))
            dve.wait_ge(group_out, group_no["hf1"] + 1)
            for f in range(4):
                mark(dve.tensor_scalar(gF[:, f], gF[:, f], lb1[:, f:f + 1], lb[:, f:f + 1], ALU.mult, ALU.add))
            wait_marked()
            dve.tensor_scalar(kF[:, 0:4], gF[:, 0:4], -1.0, 1.0, ALU.mult, ALU.add).then_inc(fgate_done, 1)
            dve.wait_ge(softplus_done, 1)
            link(dve.tensor_scalar(zg, zg, 0.0, 1.0 / GATE_NORM, ALU.min, ALU.mult))
            link(dve.scalar_tensor_tensor(gF[:, 4:6], zabs, -1.0 / GATE_NORM, zg, ALU.mult, ALU.add))
            dve.wait_ge(logf_done, 1)
            for f in range(NF):
                for n in range(NT):
                    tok = slice(n * P, n * P + P)
                    dve.tensor_tensor_scan(cum[:, f, tok], ones, gF[:, f, tok], 0.0, ALU.mult, ALU.add).then_inc(cum_done, 1)
            dve.wait_ge(rstd_done, 2)
            dve.wait_ge(transposed, KC // 2)
            for n in range(NT):
                dve.tensor_scalar(scaled[:, n], memtok[:, n], rstd_m[:, n:n + 1], None, ALU.mult).then_inc(scaled_done, 1)
            copy_out_T(4, mixT, C_MEM)

            def keep(n, mask):
                for k in range(4):
                    tau, half = k // 2, k % 2
                    dve.wait_ge(lvl_scores, 2 * n + tau + 1)
                    if n:
                        dve.wait_ge(lvl_kept, 4 * (n - 1) + k + 1)
                    dve.copy_predicated(own[:, tau, 4 * half:4 * half + 4, :], bcast(mask, 1, 4),
                                        ps[:, 4 + k, :].rearrange("p (h i) -> p h i", h=4)).then_inc(lvl_kept, 1)

            for l in range(LEVELS + 1):
                m = 1 << l
                b = l % 2
                dve.wait_ge(lvl_decay, l + 1)
                if l >= 2:
                    dve.wait_ge(lvl_scores, 2 * l)
                half = lambda a: a.rearrange("p f (b two m) -> p (f b) two m", two=2, m=m)
                dve.tensor_tensor(half(qd[:, b])[:, :, 1, :], half(qF)[:, :, 1, :], half(dec[:, b])[:, :, 1, :], ALU.mult)
                dve.tensor_tensor(half(kd[:, b])[:, :, 0, :], half(kF)[:, :, 0, :], half(dec[:, b])[:, :, 0, :], ALU.mult).then_inc(lvl_scaled, 1)
                if l == 0:
                    dve.wait_ge(masks_done, 1)
                keep(l, masks[:, LEVELS if l == 0 else l - 1])
            dve.wait_ge(group_out, group_no["ggate1"] + 1)
            for n in range(NT):
                for a in range(2):
                    g = gate1[:, n, a * TILE:(a + 1) * TILE].rearrange("p (h v) -> p h v", h=4)
                    mark(dve.tensor_tensor(g, g, bcast(gnorm[:, a], 1, 4), ALU.mult))
            for n in range(NT):
                dve.wait_ge(osq_done, n + 1)
                dve.tensor_reduce(sumsq_o[:, n], sqtmp[:, n].rearrange("p (h v) -> p h v", h=HEADS1), AX.X, ALU.add).then_inc(osum_done, 1)
            wait_marked()
            for n in range(NT):
                dve.wait_ge(orstd_done, n + 1)
                for h in range(HEADS1):
                    dve.scalar_tensor_tensor(mixed[:, n, h * P:(h + 1) * P], ps[:, 4 + 2 * n + h // 4, (h % 4) * P:(h % 4 + 1) * P],
                                             rstd_o[:, n, h:h + 1], gate1[:, n, h * P:(h + 1) * P], ALU.mult, ALU.mult).then_inc(mixed_done, 1)
            copy_out_T(8, mixT)
            for k in range(4):
                half, n = k // 2, k % 2
                dve.wait_ge(wout_done, k + 1)
                part = resid[:, n, half * TILE:(half + 1) * TILE]
                dve.tensor_tensor(part, part, ps[:, k, :], ALU.add).then_inc(h_done, 1)
            dve.wait_ge(rstd_done, 3)
            for n in range(NT):
                dve.tensor_scalar(scaled_p[:, n], resid[:, n], rstd_h[:, n:n + 1], None, ALU.mult).then_inc(scaled_done, 1)
            copy_out_T(12, actT, C_N2)
            iota16 = iota[:, 0:TOP]
            for n in range(NT):
                dve.wait_ge(sub_out, 4 * n + 4)
                for a in range(HP):
                    mark(dve.max(stop_[:, n, a, 0:8], ssb[:, n, a]))
                wait_marked()
                for a in range(HP):
                    mark(dve.max_index(sidx[:, n, a, 0:8], stop_[:, n, a, 0:8], ssb[:, n, a]))
                    mark(dve.match_replace(srest[:, a], stop_[:, n, a, 0:8], ssb[:, n, a], NEG))
                wait_marked()
                for a in range(HP):
                    mark(dve.max(stop_[:, n, a, 8:16], srest[:, a]))
                wait_marked()
                for a in range(HP):
                    mark(dve.max_index(sidx[:, n, a, 8:16], stop_[:, n, a, 8:16], srest[:, a]))
                pair = stop_[:, n].rearrange("p (h a) k -> p h a k", a=2)
                mark(dve.tensor_tensor(cand.rearrange("p h (a b) -> p h a b", a=TOP),
                                       bcast(pair[:, :, 0], 3, TOP), bcast(pair[:, :, 1], 2, TOP), ALU.add))
                wait_marked()
                mark(dve.tensor_copy(sidxf[:, n], sidx[:, n]))
                for h in range(PH):
                    mark(dve.max(best[:, n, h, 0:8], cand[:, h]))
                wait_marked()
                for h in range(PH):
                    mark(dve.max_index(pos[:, n, h, 0:8], best[:, n, h, 0:8], cand[:, h]))
                    mark(dve.match_replace(crest[:, h], best[:, n, h, 0:8], cand[:, h], NEG))
                wait_marked()
                for h in range(PH):
                    mark(dve.max(best[:, n, h, 8:16], crest[:, h]))
                wait_marked()
                for h in range(PH):
                    mark(dve.max_index(pos[:, n, h, 8:16], best[:, n, h, 8:16], crest[:, h]))
                wait_marked()
                mark(dve.tensor_scalar(posi[:, 0], pos[:, n], 4, None, ALU.logical_shift_right))
                mark(dve.tensor_scalar(posi[:, 1], pos[:, n], 15, None, ALU.bitwise_and))
                top1 = einv[:, n]
                mark(dve.tensor_copy(top1, best[:, n, :, 0]))
                wait_marked()
                mark(dve.tensor_copy(posf, posi))
                dve.tensor_tensor(best[:, n], best[:, n], bcast(top1, 2, TOP), ALU.subtract).then_inc(soft_in, 1)
                wait_marked()
                keys = sidxf[:, n].rearrange("p (h a) k -> p h a k", a=2)
                for a in range(2):
                    link(dve.tensor_tensor(pick, bcast(posf[:, a], 3, TOP), bcast(bcast(iota16, 1, TOP), 1, PH), ALU.is_equal))
                    link(dve.tensor_tensor(pick, pick, bcast(keys[:, :, a], 2, TOP), ALU.mult))
                    link(dve.tensor_reduce(chosen[:, n, a].rearrange("p (h k) -> p h k", h=PH), pick, AX.X, ALU.add))
                dve.wait_ge(soft_exp, n + 1)
                link(dve.tensor_reduce(esum[:, n], best[:, n], AX.X, ALU.add))
                link(dve.reciprocal(einv[:, n], esum[:, n]))
                dve.tensor_tensor(chosen[:, n, 2].rearrange("p (h k) -> p h k", h=PH), best[:, n], bcast(einv[:, n], 2, TOP), ALU.mult).then_inc(picks_done, 1)
            for n in range(NT):
                dve.wait_ge(pick_mm, n + 1)
                dve.tensor_copy(chosenT[:, :, n * P:(n + 1) * P], ps[:, n, 0:3 * P].rearrange("p (a t) -> p a t", a=3)).then_inc(pickT_done, 1)
            dve.wait_ge(x_round, 1)
            dve.wait_ge(mkv_stored, 16)
            dve.tensor_tensor(xl[:], actT[:], xround, ALU.subtract).then_inc(x_split, 1)
            dve.wait_ge(x_split, 1)
            dve.tensor_copy(xh[:], xround).then_inc(x_split, 1)
            dve.wait_ge(pickT_done, 2)

            def onehots(at, par):
                for k in range(GT):
                    first, second, weight = (chosenT[:, a, at(k)] for a in range(3))
                    dve.tensor_scalar(hotA[:, par, k], iota, first, None, ALU.is_equal)
                    ins = dve.tensor_scalar(hotB[:, par, k], iota, second, weight, ALU.is_equal, ALU.mult)
                ins.then_inc(onehot_ready, 1)

            for par in range(2):
                onehots(lambda k: slice(par * GT + k, par * GT + k + 1), par)
            with dve.Fori(1, NGRP // 2) as i:
                for par in range(2):
                    dve.wait_ge(g_mm, 2 * i + (par - 1))
                    onehots(lambda k: bass.ds(i * (2 * GT) + (par * GT + k), 1), par)
            dve.wait_ge(g_out, NGRP)

            def split_lo(which, n, par):
                dve.wait_ge(hi_done[which], n)
                dve.tensor_tensor(lo[:, which, par], raw[:, which, par], hi[:, which, par].bitcast(F32), ALU.subtract).then_inc(lo_done[which], 1)

            def second_key(n, at, par, last=False):
                split_lo(V, n, par)
                dve.wait_ge(gelu_done, n)
                dve.tensor_tensor(act_j, act_j, G[:, :, at].rearrange("p t j -> p (t j)"), ALU.mult).then_inc(prod_done, 1)
                if not last:
                    split_lo(U, n + 2, par)
                dve.wait_ge(wh_done, n)
                dve.tensor_tensor(wl[:], act_j, wh[:].bitcast(F32), ALU.subtract).then_inc(wl_done, 1)

            for par in range(2):
                split_lo(U, par + 1, par)
            for n in range(2):
                second_key(n + 1, slice(n, n + 1), n)
            with dve.Fori(1, NKEY // 2 - 1) as i:
                for par in range(2):
                    second_key(2 * i + (par + 1), bass.ds(2 * i + par, 1), par)
            for n in range(NKEY - 2, NKEY):
                second_key(n + 1, slice(n, n + 1), n % 2, last=True)
            for k in range(4):
                dve.wait_ge(v_mm, NKEY)
                part = resid[:, k // 2, (k % 2) * TILE:(k % 2 + 1) * TILE]
                dve.tensor_tensor(part, part, ps[:, 4 + k, :], ALU.add).then_inc(peer_out, 1)
            dve.wait_ge(rows_loaded, 48)
            dve.wait_ge(rstd_done, 4)
            for n in range(NT):
                dve.scalar_tensor_tensor(resid[:, n], resid[:, n], rstd_f[:, n:n + 1], norm_f, ALU.mult, ALU.mult).then_inc(x1_done, 1)
            dve.wait_ge(rstd_done, 5)
            for n in range(NT):
                dve.tensor_scalar(scaled2[:, n], resid[:, n], rstd_x[:, n:n + 1], None, ALU.mult).then_inc(scaled_done, 1)
            link(dve.tensor_tensor(window[:, 0], ident[:], upper[:], ALU.subtract))
            link(dve.tensor_scalar(window[:, 0], window[:, 0], 1.0, None, ALU.add))
            mark(dve.tensor_scalar(window[:, 1], window[:, 0], -MASKED, MASKED, ALU.mult, ALU.add))
            wait_marked()
            mark(dve.tensor_scalar(window[:, 0], window[:, 0], MASKED, None, ALU.mult))
            dve.wait_ge(ws_loaded, 16)
            mark(dve.tensor_tensor(wsT, wsT, bcast(upper[:], 1, 4), ALU.mult))
            copy_out_T(16, actT, C_PRE)
            dve.wait_ge(transposed, 20)
            dve.memset(convin[:, :, 0:CONV - 1], 0.0).then_inc(conv_zero, 1)
            for k, name in enumerate(("dnq", "dnk", "dnv")):
                dve.wait_ge(g2_out, g2_no[name + "1"] + 1)
                for tap in reversed(range(CONV)):
                    for f in range(4 * k, 4 * k + 4):
                        w = cols[:, C_CONV + tap * 12 + f:C_CONV + tap * 12 + f + 1]
                        src = convin[:, f, tap:tap + T]
                        if tap == CONV - 1:
                            mark(dve.tensor_scalar(convT[:, f], src, w, None, ALU.mult))
                        elif tap:
                            mark(dve.scalar_tensor_tensor(convT[:, f], src, w, convT[:, f], ALU.mult, ALU.add))
                        else:
                            ins = dve.scalar_tensor_tensor(convT[:, f], src, w, convT[:, f], ALU.mult, ALU.add)
                    wait_marked()
                ins.then_inc(conv_done, 1)
            dve.wait_ge(g2_out, g2_no["ba"] + 1)
            dve.tensor_tensor(dz, ba[:, :, DH:2 * DH], bcast(dt_bias, 1, NT), ALU.add).then_inc(dz_done, 1)
            dve.wait_ge(ss_mm, 1)
            dve.tensor_scalar(rin.rearrange("p n f -> p (n f)"), ps[:, 4, 0:2 * TH], EPS, None, ALU.add).then_inc(rin_done, 1)
            dve.wait_ge(dln_done, 1)
            link(dve.scalar_tensor_tensor(dsp, dz, 0.0, dsp, ALU.max, ALU.add))
            dve.scalar_tensor_tensor(dg, dsp, -1.0, bcast(nega, 1, NT), ALU.mult, ALU.mult).then_inc(dg_done, 1)
            dve.wait_ge(rr_done, 1)
            dve.wait_ge(beta_done, 1)
            mark(dve.tensor_tensor(brk, beta, rr[:, :, DH:2 * DH], ALU.mult))
            mark(dve.tensor_scalar(rqs, rr[:, :, 0:DH], HEAD ** -0.5, None, ALU.mult))
            dve.wait_ge(dg_done, 1)
            wait_marked()
            for a, v in enumerate((dg, brk, rqs)):
                ins = dve.tensor_copy(rep[:, a], bcast(v.rearrange("p n h -> p (n h)"), 2, P))
            ins.then_inc(rep_done, 1)
            dve.wait_ge(gc_mm, 1)
            dve.tensor_copy(gcs, ps[:, 5, 0:2 * TH].rearrange("p (a h) -> p a h", a=2)).then_inc(gcs_done, 1)
            dve.wait_ge(gcs_done, 1)
            dve.tensor_tensor(ekd, gcs[:, 1, 0:DH], gcs[:, 0, 0:DH], ALU.subtract).then_inc(gcs_done, 1)
            dve.wait_ge(row_mm, 1)
            for th in range(TH):
                ins = dve.tensor_scalar(Dm[:, th], ps[:, 4 + th // DH, (th % DH) * P:(th % DH + 1) * P], gcs[:, 0, th:th + 1], 0.0, ALU.subtract, ALU.min)
            ins.then_inc(dm_in, 1)
            dve.wait_ge(egc_done, 1)
            mark(dve.tensor_tensor(kbf, brk, egc, ALU.mult))
            mark(dve.tensor_tensor(ekd, ekd, rr[:, 0, DH:2 * DH], ALU.mult))
            wait_marked()
            dve.wait_ge(gmv_rstd, 1)
            for n in range(NT):
                dve.scalar_tensor_tensor(gv2[:, n], gv2[:, n], rstd_v[:, n:n + 1], gm_gain, ALU.mult, ALU.mult).then_inc(gmv_done, 1)

            def head_cols(k):
                return slice((k % DH) * P, (k % DH + 1) * P)

            dve.wait_ge(dm_done, 1)
            dve.wait_ge(kk_mm, 1)
            for th in range(TH):
                mark(dve.scalar_tensor_tensor(LT[:, th], ps[:, 6 + th // DH, head_cols(th)], rr[:, th // DH, DH + th % DH:DH + th % DH + 1], Dm[:, th], ALU.mult, ALU.mult))
            dve.wait_ge(brow_done, 1)
            wait_marked()
            dve.tensor_tensor(LT, LT, brow, ALU.mult).then_inc(lt_done, 1)
            dve.wait_ge(lt_done, 1)
            link(dve.tensor_tensor(BT, LT, bcast(masks[:, 0], 1, TH), ALU.mult))
            dve.tensor_tensor(Z, bcast(ident[:], 1, TH), BT, ALU.subtract).then_inc(z0_done, 1)
            dve.wait_ge(kv_tr, 1)
            for h in range(DH):
                dve.tensor_scalar(kdl[:, h], ps[:, 6, head_cols(h)], ekd[:, h:h + 1], None, ALU.mult)
            for th in range(TH):
                n, h = th // DH, th % DH
                ins = dve.tensor_scalar(kbg[:, th], ps[:, 6 + n, head_cols(th)], kbf[:, n, h:h + 1], None, ALU.mult)
            ins.then_inc(kv_out, 1)
            dve.wait_ge(kv_tr, 2)
            for th in range(TH):
                n, h = th // DH, th % DH
                ins = dve.tensor_scalar(vb[:, th], ps[:, 6 + n, head_cols(th)], beta[:, n, h:h + 1], None, ALU.mult)
            ins.then_inc(kv_out, 1)
            dve.wait_ge(qk_mm, 1)
            for th in range(TH):
                mark(dve.scalar_tensor_tensor(AQ[:, th], ps[:, 6 + th // DH, head_cols(th)], rr[:, th // DH, DH + th % DH:DH + th % DH + 1], Dm[:, th], ALU.mult, ALU.mult))
            dve.wait_ge(qrow_done, 1)
            wait_marked()
            link(dve.tensor_tensor(AQ, AQ, qrow, ALU.mult))
            dve.tensor_tensor(AQ, AQ, bcast(upper[:], 1, TH), ALU.mult).then_inc(aq_done, 1)
            link(dve.tensor_tensor(qg, qg, qrow[:, DH:TH], ALU.mult))
            dve.tensor_tensor(qg, qg, convT[:, 0:DH, P:T], ALU.mult).then_inc(qg_done, 1)
            for l in range(1, LEVELS):
                if l >= 2:
                    dve.wait_ge(y_mm, NT * (l - 1))
                else:
                    dve.wait_ge(z0_done, 1)
                dve.tensor_tensor(BT, LT, bcast(masks[:, l], 1, TH), ALU.mult).then_inc(bt_done, 1)
                for n in range(NT):
                    part = slice(DH * n, DH * n + DH)
                    dve.wait_ge(pz_mm, NT * (l - 1) + n + 1)
                    if l < LEVELS - 1:
                        dve.tensor_tensor(X[:, part], X[:, part], ps[:, 6 + n, :].rearrange("p (h c) -> p h c", h=DH), ALU.subtract).then_inc(x_done, 1)
                    dve.tensor_tensor(Z[:, part], Z[:, part], ps[:, 4 + n, :].rearrange("p (h c) -> p h c", h=DH), ALU.subtract).then_inc(z_done, 1)
            dve.wait_ge(ws_mm, 1)
            dve.wait_ge(du_done, 1)
            dve.tensor_tensor(vnew, du[:, DH:TH], ps[:, 6, :].rearrange("p (h c) -> p h c", h=DH), ALU.subtract).then_inc(vnew_done, 1)
            for n in range(NT):
                dve.wait_ge(gm_mm, n + 1)
                for g in range(4):
                    part = gu[:, n, g * P:(g + 1) * P]
                    mark(dve.scalar_tensor_tensor(part, ps[:, 2 + n, g * P:(g + 1) * P], cols[:, C_SB + g:C_SB + g + 1], part, ALU.add, ALU.mult))
                wait_marked()
                dve.tensor_tensor(gu[:, n], gu[:, n], gz[:, n], ALU.mult).then_inc(y_done[1], 1)
            for n in range(NT):
                zz = zdn[:, n].rearrange("p (h v) -> p h v", h=DH)
                mark(dve.tensor_tensor(zz, zz, bcast(dn_gain, 1, DH), ALU.mult))
            for n in range(NT):
                dve.wait_ge(dosq_done, n + 1)
                dve.tensor_reduce(sumsq_a[:, n], prob[:, n * TILE:(n + 1) * TILE].rearrange("p (h v) -> p h v", h=DH), AX.X, ALU.add).then_inc(dosum_done, 1)
            wait_marked()
            for n in range(NT):
                dve.wait_ge(dors_done, n + 1)
                for h in range(DH):
                    part = zdn[:, n, h * P:(h + 1) * P]
                    ins = dve.scalar_tensor_tensor(part, ps[:, 4 + n, h * P:(h + 1) * P], rstd_a[:, n, h:h + 1], part, ALU.mult, ALU.mult)
                ins.then_inc(y_done[0], 1)
            off = 0
            for n in range(NT):
                width = (n + 1) * P
                pr = prob[:, off:off + SH * width].rearrange("p (h j) -> p h j", h=SH)
                off += SH * width
                banks, per = ((4, 4), (0, 2))[n]
                add = window[:, 1] if n == 0 else window.rearrange("p a j -> p (a j)")
                dve.wait_ge(ss_mm2, n + 1)
                for b in range(SH // per):
                    mark(dve.scalar_tensor_tensor(pr[:, per * b:per * b + per], ps[:, banks + b, :].rearrange("p (h j) -> p h j", h=per), SHD ** -0.5,
                                                  bcast(add, 1, per), ALU.mult, ALU.add))
                wait_marked()
                link(dve.tensor_reduce(smax[:, n], pr, AX.X, ALU.max))
                link(dve.tensor_tensor(smax[:, n], smax[:, n], sinks, ALU.max))
                mark(dve.tensor_tensor(ssk[:, n], sinks, smax[:, n], ALU.subtract))
                dve.tensor_scalar(snm[:, n], smax[:, n], -1.0, None, ALU.mult).then_inc(s_masked, 1)
            for n in range(NT):
                dve.wait_ge(s_exp, n + 1)
                link(dve.tensor_tensor(sden[:, n], sden[:, n], ssk[:, n], ALU.add))
                link(dve.reciprocal(srec[:, n], sden[:, n]))
                dve.wait_ge(so_mm, n + 1)
                for h in range(SH):
                    part = swz[:, n, h * SHD:(h + 1) * SHD]
                    ins = dve.scalar_tensor_tensor(part, ps[:, 6 + n, h * SHD:(h + 1) * SHD], srec[:, n, h:h + 1], part, ALU.mult, ALU.mult)
                ins.then_inc(y_done[2], 1)
            for n in range(NT):
                dve.wait_ge(xs_mm, n + 1)
                link(dve.tensor_reduce(xmax[:, n], ps[:, 4 + 2 * n:6 + 2 * n, :].rearrange("p b (h j) -> p (b h) j", h=2), AX.X, ALU.max))
                dve.tensor_scalar(xnm[:, n], xmax[:, n], -(HEAD ** -0.5), None, ALU.mult).then_inc(xs_max, 1)
            for n in range(NT):
                dve.wait_ge(xs_exp, n + 1)
                link(dve.reciprocal(xrec[:, n], xden[:, n]))
                dve.wait_ge(xo_mm, n + 1)
                for h in range(XH):
                    part = xmz[:, n, h * HEAD:(h + 1) * HEAD]
                    ins = dve.scalar_tensor_tensor(part, ps[:, n, h * HEAD:(h + 1) * HEAD], xrec[:, n, h:h + 1], part, ALU.mult, ALU.mult)
                ins.then_inc(y_done[3], 1)
            for n in range(NBR):
                dve.wait_ge(yT_mm, n + 1)
                b = 4 + 2 * (n % 2)
                dve.tensor_copy(yT[:, 4 * n:4 * n + 4].rearrange("p c t -> p (c t)"), ps[:, b:b + 2, :].rearrange("p b n -> p (b n)")).then_inc(yT_done, 1)
            for n in range(NBR):
                for k in range(4):
                    dve.wait_ge(up_mm, 4 * n + k + 1)
                    dve.wait_ge(g2_out, g2_no[f"gate{n}{k // 2}{k % 2}"] + 1)
                    part = merged[:, k % 2, (k // 2) * TILE:(k // 2 + 1) * TILE]
                    g = gsb[:, n % 2, k]
                    if n == 0:
                        dve.tensor_tensor(part, g, ps[:, 4 + k, :], ALU.mult).then_inc(up_out, 1)
                    else:
                        link(dve.tensor_tensor(g, g, ps[:, 4 + k, :], ALU.mult))
                        dve.wait_ge(up_out, 4 * (n - 1) + k + 1)
                        dve.tensor_tensor(part, part, g, ALU.add).then_inc(merged_done if n == NBR - 1 else up_out, 1)
            copy_out_T(20, actT)
            dve.wait_ge(rstd_done, 6)
            dve.wait_ge(post_loaded, 16)
            for n in range(NT):
                mark(dve.scalar_tensor_tensor(outsb[:, n], outsb[:, n], rstd_p[:, n:n + 1], norm_post, ALU.mult, ALU.mult))
                wait_marked()
                dve.tensor_tensor(outsb[:, n], outsb[:, n], resid[:, n], ALU.add).then_inc(out_done, 1)

        @block.tensor
        def _(pe):
            def transpose_all(src, waits, dst_free):
                waits()
                dst_free()
                for c in range(KC):
                    for n in range(NT):
                        ins = pe.transpose(ps[:, 4 + c // 2, (c % 2) * T + n * P:(c % 2) * T + (n + 1) * P],
                                           src[:, n, c * P:(c + 1) * P], ident[:])
                    if c % 2:
                        ins.then_inc(transposed, 1)

            def actT_ready(n):
                pe.wait_ge(actT_done[0], 4 * n)
                pe.wait_ge(actT_done[1], 4 * n)

            def need(name):
                pe.wait_ge(tile_loaded[slot(name)], 16 * (tile_no[name] // RING + 1))

            def bank_free(g):
                k = group_no[g]
                if k >= 4:
                    pe.wait_ge(group_out, k - 3)

            def features(name, xT, subs):
                need(name)
                w = tile_view(name)
                for s in subs:
                    g = f"{name}{s}"
                    bank_free(g)
                    for a in range(2):
                        f0 = (2 * s + a) * P
                        for c in range(KC):
                            ins = pe.matmul(ps[:, gbank(g), a * T:(a + 1) * T], w[:, c, f0:f0 + P], xT[:, c, :], start=(c == 0), stop=(c == KC - 1))
                    ins.then_inc(group_done, 1)

            def tokens(name, xT):
                need(name)
                w = tile_view(name)
                for n in range(NT):
                    g = f"{name}{n}"
                    bank_free(g)
                    for c in range(KC):
                        ins = pe.matmul(ps[:, gbank(g), :], xT[:, c, n * P:(n + 1) * P], w[:, c, :], start=(c == 0), stop=(c == KC - 1))
                    ins.then_inc(group_done, 1)

            pe.wait_ge(consts_made, 1)
            transpose_all(scaled, lambda: pe.wait_ge(scaled_done, 2), lambda: None)
            actT_ready(1)
            features("hq", actT, (0, 1))
            features("hf", actT, (0, 1))
            features("gqk", actT, (0, 1))
            bank_free("glow")
            for c in range(KC):
                ins = pe.matmul(ps[0:RANK, gbank("glow"), 0:T], glow_w[:, c], actT[:, c], start=(c == 0), stop=(c == KC - 1))
            ins.then_inc(group_done, 1)
            pe.wait_ge(group_out, group_no["glow"] + 1)
            for a in range(2):
                ins = pe.matmul(ps[:, 7, a * T:(a + 1) * T], gate_up[:, a], glowT[0:RANK], start=True, stop=True)
            ins.then_inc(gate_mm, 1)
            for name in ("hi", "gv"):
                tokens(name, actT)
            transpose_all(scaled, lambda: pe.wait_ge(scaled_done, 4), lambda: pe.wait_ge(softplus_done, 1))

            def scores(n, q, k):
                for tau in range(NT):
                    if n:
                        pe.wait_ge(lvl_kept, 4 * (n - 1) + 2 * tau + 2)
                    tok = slice(tau * P, tau * P + P)
                    for h in range(HEADS1):
                        f, rows = head_rows(h)
                        ins = pe.matmul(ps[:, 4 + 2 * tau + PLACE[h] // 4, (PLACE[h] % 4) * P:(PLACE[h] % 4 + 1) * P], k[rows, f, tok], q[rows, f, tok], start=True, stop=True)
                    ins.then_inc(lvl_scores, 1)

            actT_ready(2)
            pe.wait_ge(fgate_done, 1)
            scores(0, qF, kF)
            for l in range(LEVELS):
                if l in (1, 3):
                    tokens("hgate" if l == 1 else "ggate", actT)
                pe.wait_ge(lvl_scaled, l + 1)
                scores(l + 1, qd[:, l % 2], kd[:, l % 2])
            pe.wait_ge(lvl_scaled, LEVELS + 1)
            pe.wait_ge(lvl_kept, 4 * LEVELS + 2)
            for h in range(HEADS1):
                f, rows = head_rows(h)
                ins = pe.matmul(ps[:, 4 + PLACE[h] // 4, (PLACE[h] % 4) * P:(PLACE[h] % 4 + 1) * P], kd[rows, 1, f, 0:P], qd[rows, 1, f, P:T], start=True, stop=True)
            ins.then_inc(lvl_scores, 1)
            features("mk", mixT, (0, 1))
            tokens("mv", mixT)
            pe.wait_ge(cross_out, 1)
            pe.wait_ge(lvl_kept, 4 * (LEVELS + 1))
            for n in range(NT):
                for h in range(HEADS1):
                    o = ps[:, 4 + 2 * n + h // 4, (h % 4) * P:(h % 4 + 1) * P]
                    ins = pe.matmul(o, own[:, n, PLACE[h]], vtok[:, n, h * P:(h + 1) * P], start=True, stop=(n == 0))
                    if n:
                        ins = pe.matmul(o, cross[:, PLACE[h]], vtok[:, 0, h * P:(h + 1) * P], start=False, stop=True)
                ins.then_inc(o_done, 1)
            transpose_all(mixed, lambda: pe.wait_ge(mixed_done, 2 * HEADS1), lambda: pe.wait_ge(group_out, group_no["mv1"] + 1))
            actT_ready(3)
            for k in range(4):
                half, n = k // 2, k % 2
                name = f"wo{half}"
                need(name)
                for c in range(KC):
                    ins = pe.matmul(ps[:, k, :], mixT[:, c, n * P:(n + 1) * P], tile_view(name)[:, c, :], start=(c == 0), stop=(c == KC - 1))
                ins.then_inc(wout_done, 1)
            transpose_all(scaled_p, lambda: pe.wait_ge(scaled_done, 6), lambda: None)
            actT_ready(4)
            pe.wait_ge(h_done, 4)
            for a in range(4):
                features(f"wq{a}", actT, (0, 1))
            need("subkeys")
            keysT = ring[:, slot("subkeys"), 0:HP * NKEY].rearrange("p (a n) -> p a n", a=HP)
            for k in range(8):
                n = k // 4
                if k >= 4:
                    pe.wait_ge(sub_out, k - 3)
                for a in range(4):
                    hp = 4 * (k % 4) + a
                    if n == 0 and a % 2 == 0:
                        pe.wait_ge(group_out, group_no["wq00"] + hp // 2 + 1)
                    ins = pe.matmul(ps[:, 4 + k % 4, a * P:(a + 1) * P], qT[:, hp, n * P:(n + 1) * P], keysT[:, hp], start=True, stop=True)
                ins.then_inc(sub_done, 1)
            for n in range(NT):
                pe.wait_ge(picks_done, n + 1)
                for a in range(3):
                    ins = pe.transpose(ps[:, n, a * P:(a + 1) * P], chosen[:, n, a], ident[:])
                ins.then_inc(pick_mm, 1)
            pe.wait_ge(pickT_done, 2)

            def weights_of(n, par):
                pe.wait_ge(onehot_ready, n)
                for k in range(GT):
                    ins = pe.matmul(ps[:, par, k * P:(k + 1) * P], hotA[:, par, k], hotB[:, par, k], start=True, stop=True)
                ins.then_inc(g_mm, 1)

            for par in range(2):
                weights_of(par + 1, par)
            with pe.Fori(1, NGRP // 2) as i:
                for par in range(2):
                    pe.wait_ge(g_out, 2 * i + (par - 1))
                    weights_of(2 * i + (par + 1), par)

            u_hi, u_lo = (v[:, U].rearrange("p s (c i) -> p s c i", c=KC) for v in (hi, lo))

            def u_pass(n, par):
                pe.wait_ge(lo_done[U], n)
                o = ps[:, par, 0:T]
                for c in range(KC):
                    pe.matmul(o, u_hi[:, par, c], xh[:, c], start=(c == 0), stop=False)
                    pe.matmul(o, u_hi[:, par, c], xl[:, c], start=False, stop=False)
                    ins = pe.matmul(o, u_lo[:, par, c], xh[:, c], start=False, stop=(c == KC - 1))
                ins.then_inc(u_mm, 1)

            def v_pass(n, par, first=False, last=False):
                pe.wait_ge(lo_done[V], n)
                pe.wait_ge(wl_done, n)
                for tau in range(NT):
                    tok = slice(tau * P, (tau + 1) * P)
                    for k, (w, v) in enumerate(((wh, hi), (wh, lo), (wl, hi))):
                        for half in range(2):
                            ins = pe.matmul(ps[:, 4 + 2 * tau + half, :], w[:, tok], v[:, V, par, half * TILE:(half + 1) * TILE],
                                            start=(first and k == 0), stop=(last and k == 2))
                ins.then_inc(v_mm, 1)

            pe.wait_ge(g_out, NGRP)
            pe.wait_ge(x_split, 2)
            u_pass(1, 0)
            u_pass(2, 1)
            v_pass(1, 0, first=True)
            with pe.Fori(1, NKEY // 2) as i:
                pe.wait_ge(gelu_done, 2 * i - 1)
                u_pass(2 * i + 1, 0)
                v_pass(2 * i, 1)
                pe.wait_ge(gelu_done, 2 * i)
                u_pass(2 * i + 2, 1)
                v_pass(2 * i + 1, 0)
            v_pass(NKEY, 1, last=True)
            transpose_all(scaled2, lambda: pe.wait_ge(scaled_done, 8), lambda: pe.wait_ge(peer_out, 4))
            actT_ready(5)

            def need2(name):
                k = tile2_no[name]
                pe.wait_ge(tile_loaded[k % RING], 16 * (loads1[k % RING] + k // RING + 1))
                return ring[:, k % RING, :]

            def free2(g):
                k = g2_no[g]
                if k >= 4:
                    pe.wait_ge(g2_out, k - 3)
                return ps[:, k % 4, :]

            def features2(name):
                w = need2(name).rearrange("p (c n) -> p c n", c=KC)
                for s in range(2):
                    o = free2(f"{name}{s}")
                    for a in range(2):
                        for c in range(KC):
                            ins = pe.matmul(o[:, a * T:(a + 1) * T], w[:, c, (2 * s + a) * P:(2 * s + a + 1) * P], actT[:, c], start=(c == 0), stop=(c == KC - 1))
                    ins.then_inc(g2_done, 1)

            def tokens2(name, suffix=""):
                w = need2(name).rearrange("p (c n) -> p c n", c=KC)
                for n in range(NT):
                    o = free2(f"{name}{n}")
                    for c in range(KC):
                        ins = pe.matmul(o, actT[:, c, n * P:(n + 1) * P], w[:, c], start=(c == 0), stop=(c == KC - 1))
                    ins.then_inc(g2_done, 1)

            for name in ("dnq", "dnk", "dnv"):
                features2(name)
            pe.wait_ge(rows_loaded, 48)
            o = free2("ba")
            for n in range(NT):
                for c in range(KC):
                    ins = pe.matmul(o[:, n * 2 * DH:(n + 1) * 2 * DH], actT[:, c, n * P:(n + 1) * P], ba_w[:, c], start=(c == 0), stop=(c == KC - 1))
            ins.then_inc(g2_done, 1)
            tokens2("dnz")
            tokens2("gmu")
            pe.wait_ge(consts_made, 2)
            pe.wait_ge(dnsq_done, 1)
            for n in range(NT):
                for f in range(2 * DH):
                    ins = pe.matmul(ps[:, 4, n * 2 * DH + f:n * 2 * DH + f + 1], sqk[:, f, n * P:(n + 1) * P], ones[:, 0:1], start=True, stop=True)
            ins.then_inc(ss_mm, 1)
            pe.wait_ge(dg_done, 1)
            pe.matmul(ps[:, 5, 0:TH], upper[:], dg.rearrange("p n h -> p (n h)"), start=True, stop=True)
            pe.matmul(ps[:, 5, TH:2 * TH], ones, dg.rearrange("p n h -> p (n h)"), start=True, stop=True).then_inc(gc_mm, 1)
            tokens2("gmv")

            def th_out(b, th):
                return ps[:, b + th // DH, (th % DH) * P:(th % DH + 1) * P]

            def repeat_row(b, a, m):
                for th in range(TH):
                    ins = pe.matmul(th_out(b, th), rep[:, a, th], m, start=True, stop=True)
                ins.then_inc(row_mm, 1)

            pe.wait_ge(rep_done, 1)
            pe.wait_ge(rin_done, 1)
            pe.wait_ge(gcs_done, 1)
            repeat_row(4, 0, upper[:])
            repeat_row(6, 1, ident[:])
            tokens2("gmz")
            pe.wait_ge(brow_done, 1)
            pe.wait_ge(dnsilu_done, 3)
            for th in range(TH):
                n, h = th // DH, th % DH
                k = convT[:, DH + h, n * P:(n + 1) * P]
                ins = pe.matmul(th_out(6, th), k, k, start=True, stop=True)
            ins.then_inc(kk_mm, 1)
            pe.wait_ge(dm_done, 1)
            repeat_row(4, 2, ident[:])
            features2("swq")
            pe.wait_ge(lt_done, 1)
            for a in range(2):
                if a:
                    pe.wait_ge(kv_out, 1)
                for th in range(TH):
                    n, h = th // DH, th % DH
                    ins = pe.transpose(th_out(6, th), convT[:, (1 + a) * DH + h, n * P:(n + 1) * P], ident[:])
                ins.then_inc(kv_tr, 1)
            w = need2("swkv")[:, 0:KC * T].rearrange("p (c n) -> p c n", c=KC)
            o = free2("swkv")
            for c in range(KC):
                pe.matmul(o[:, 0:T], w[:, c, 0:P], actT[:, c], start=(c == 0), stop=(c == KC - 1))
            for n in range(NT):
                for c in range(KC):
                    ins = pe.matmul(o[:, T + n * P:T + (n + 1) * P], actT[:, c, n * P:(n + 1) * P], w[:, c, P:2 * P], start=(c == 0), stop=(c == KC - 1))
            ins.then_inc(g2_done, 1)
            pe.wait_ge(kv_out, 2)
            for th in range(TH):
                n, h = th // DH, th % DH
                ins = pe.matmul(th_out(6, th), convT[:, DH + h, n * P:(n + 1) * P], convT[:, h, n * P:(n + 1) * P], start=True, stop=True)
            ins.then_inc(qk_mm, 1)
            pe.wait_ge(z0_done, 1)
            pe.wait_ge(qrow_done, 1)
            for th in range(TH):
                ins = pe.transpose(th_out(4, th), Z[:, th], ident[:])
            ins.then_inc(x0_tr, 1)
            for l in range(1, LEVELS):
                pe.wait_ge(bt_done, l)
                for n in range(NT):
                    pe.wait_ge(x_done, NT * (l - 1) + n if l > 1 else 1)
                    if l > 1:
                        pe.wait_ge(x_done, 1 + NT * (l - 2) + n + 1)
                        pe.wait_ge(z_done, NT * (l - 2) + n + 1)
                    for th in range(DH * n, DH * n + DH):
                        ins = pe.matmul(th_out(4, th), BT[:, th], X[:, th], start=True, stop=True)
                    ins.then_inc(y_mm, 1)
                if l == 1:
                    pe.wait_ge(aq_done, 1)
                for n in range(NT):
                    pe.wait_ge(y_out, NT * (l - 1) + n + 1)
                    if l < LEVELS - 1:
                        for th in range(DH * n, DH * n + DH):
                            ins = pe.matmul(th_out(6, th), Z[:, th], Y[:, th], start=True, stop=True)
                    for th in range(DH * n, DH * n + DH):
                        ins = pe.matmul(th_out(4, th), Y[:, th], Z[:, th], start=True, stop=True)
                    ins.then_inc(pz_mm, 1)
                if l == 1:
                    tokens2("swz")
                if l == 2:
                    features2("xmq")
                if l == 3:
                    tokens2("xmz")
            pe.wait_ge(z_done, NT * (LEVELS - 1))
            pe.wait_ge(kv_out, 2)
            for th in range(TH):
                pe.matmul(th_out(4, th), Z[:, th], vb[:, th], start=True, stop=True)
            for h in range(DH):
                ins = pe.matmul(ps[:, 6, h * P:(h + 1) * P], kbg[:, DH + h], Z[:, DH + h], start=True, stop=True)
            ins.then_inc(u_out_mm, 1)
            pe.wait_ge(du_done, 1)
            for h in range(DH):
                ins = pe.matmul(ps[:, 7, h * P:(h + 1) * P], kdl[:, h], du[:, h], start=True, stop=True)
            ins.then_inc(s1_mm, 1)
            pe.wait_ge(s1_done, 1)
            pe.wait_ge(wt_done, 1)
            for h in range(DH):
                ins = pe.matmul(ps[:, 6, h * P:(h + 1) * P], wT[:, h], S1[:, h], start=True, stop=True)
            ins.then_inc(ws_mm, 1)
            pe.wait_ge(gmv_done, NT)
            pe.wait_ge(g2_out, g2_no["xmz1"] + 1)
            for n in range(NT):
                for g in range(4):
                    ins = pe.matmul(ps[:, 2 + n, g * P:(g + 1) * P], wsT[:, g], gv2[:, n, g * P:(g + 1) * P], start=True, stop=True)
                ins.then_inc(gm_mm, 1)
            pe.wait_ge(aq_done, 1)
            for h in range(DH):
                ins = pe.matmul(th_out(4, h), AQ[:, h], du[:, h], start=True, stop=True)
            ins.then_inc(do_mm, 1)
            pe.wait_ge(qg_done, 1)
            pe.wait_ge(vnew_done, 1)
            for h in range(DH):
                pe.matmul(th_out(4, DH + h), qg[:, h], S1[:, h], start=True, stop=False)
                ins = pe.matmul(th_out(4, DH + h), AQ[:, DH + h], vnew[:, h], start=False, stop=True)
            ins.then_inc(do_mm, 1)
            pe.wait_ge(y_done[0], NT)
            pe.wait_ge(y_done[1], NT)
            for n in range(NT):
                banks, per = ((4, 4), (0, 2))[n]
                width = (n + 1) * P
                for h in range(SH):
                    half = slice(SHD * (h // 4), SHD * (h // 4) + SHD)
                    ins = pe.matmul(ps[:, banks + h // per, (h % per) * width:(h % per + 1) * width], swqT[half, h % 4, n * P:(n + 1) * P], swkT[half, 0:width],
                                    start=True, stop=True)
                ins.then_inc(ss_mm2, 1)
            off = 0
            for n in range(NT):
                width = (n + 1) * P
                pr = prob[:, off:off + SH * width].rearrange("p (h j) -> p h j", h=SH)
                off += SH * width
                pe.wait_ge(s_exp, n + 1)
                if n:
                    pe.wait_ge(s_masked, 2)
                for h in range(SH):
                    for b in range(n + 1):
                        at = (h * (n + 1) + b) * P
                        ins = pe.transpose(ps[:, (0 if n else 4) + at // TILE, at % TILE:at % TILE + P], pr[:, h, b * P:(b + 1) * P], ident[:])
                ins.then_inc(s_tr, 1)
            off = 0
            for n in range(NT):
                width = (n + 1) * P
                prT = probT[:, off:off + SH * width].rearrange("p (h b i) -> p h b i", h=SH, b=n + 1)
                off += SH * width
                pe.wait_ge(s_trout, n + 1)
                for h in range(SH):
                    for b in range(n + 1):
                        ins = pe.matmul(ps[:, 6 + n, h * SHD:(h + 1) * SHD], prT[:, h, b], swv[:, b, SHD * (h // 4):SHD * (h // 4) + SHD], start=(b == 0), stop=(b == n))
                ins.then_inc(so_mm, 1)
            pe.wait_ge(mkv_loaded, 16)
            for n in range(NT):
                if n:
                    pe.wait_ge(y_done[2], NT)
                for h in range(XH):
                    ins = pe.matmul(ps[:, 4 + 2 * n + h // 2, (h % 2) * T:(h % 2 + 1) * T], xmqT[:, h, n * P:(n + 1) * P], mkT[:, h], start=True, stop=True)
                ins.then_inc(xs_mm, 1)
            for n in range(NT):
                pr = prob[:, n * 1024:(n + 1) * 1024].rearrange("p (h j) -> p h j", h=XH)
                pe.wait_ge(xs_exp, n + 1)
                for h in range(XH):
                    for b in range(2):
                        at = (2 * h + b) * P
                        ins = pe.transpose(ps[:, 4 + 2 * n + at // TILE, at % TILE:at % TILE + P], pr[:, h, b * P:(b + 1) * P], ident[:])
                ins.then_inc(xs_tr, 1)
            for n in range(NT):
                prT = probT[:, n * 1024:(n + 1) * 1024].rearrange("p (h b i) -> p h b i", h=XH, b=2)
                pe.wait_ge(xs_trout, n + 1)
                for h in range(XH):
                    for b in range(2):
                        ins = pe.matmul(ps[:, n, h * HEAD:(h + 1) * HEAD], prT[:, h, b], mv[:, b, h * HEAD:(h + 1) * HEAD], start=(b == 0), stop=(b == 1))
                ins.then_inc(xo_mm, 1)
            for n, y in enumerate((zdn, gu, swz, xmz)):
                pe.wait_ge(y_done[n], NT)
                if n >= 2:
                    pe.wait_ge(yT_done, n - 1)
                b = 4 + 2 * (n % 2)
                for c in range(4):
                    for k in range(NT):
                        at = c * T + k * P
                        ins = pe.transpose(ps[:, b + at // TILE, at % TILE:at % TILE + P], y[:, k, c * P:(c + 1) * P], ident[:])
                ins.then_inc(yT_mm, 1)
            for n in range(NBR):
                for h in range(2):
                    name = f"gate{n}{h}"
                    tokens2(name)
                w = need2(f"up{n}").rearrange("p (c n) -> p c n", c=4)
                pe.wait_ge(yT_done, NBR)
                for k in range(4):
                    half, tau = k // 2, k % 2
                    if n:
                        pe.wait_ge(up_out, 4 * (n - 1) + k + 1)
                    for c in range(4):
                        ins = pe.matmul(ps[:, 4 + k, :], yT[:, 4 * n + c, tau * P:(tau + 1) * P], w[:, c, half * TILE:(half + 1) * TILE], start=(c == 0), stop=(c == 3))
                    ins.then_inc(up_mm, 1)
            transpose_all(merged, lambda: pe.wait_ge(merged_done, 4), lambda: None)
            actT_ready(6)
            pe.wait_ge(g2_out, len(groups2))
            for k in range(4):
                half, n = k // 2, k % 2
                w = need2(f"out{half}").rearrange("p (c n) -> p c n", c=KC)
                for c in range(KC):
                    ins = pe.matmul(ps[:, k, :], actT[:, c, n * P:(n + 1) * P], w[:, c], start=(c == 0), stop=(c == KC - 1))
                ins.then_inc(fin_mm, 1)


def layout(inputs):
    import numpy as np
    a = {k: np.asarray(v) for k, v in inputs.items()}

    def col(v):
        return v.reshape(-1, P).T

    r = {}
    for n in ("x", "mem_2", "gla_w_gate_up", "hg_norm_g", "gla_norm_g"):
        r[n] = a[n]
    for n in ("w_in", "w_out", "peer_w_q", "w_in_2", "w_mem_kv_2", "w_out_2"):
        r[n] = a[n][0]
    r["w_up_2"] = a["w_up_2"][0]
    r["cols"] = np.concatenate([col(a["norm1_g"]), col(a["norm2_g"]), col(a["norm_pre_2"]), col(a["norm_mem_2"]),
                                col(a["hg_lower_logits"]), col(a["gla_b_gate"]),
                                col(a["conv_w_2"]), col(a["spatial_b_2"])], axis=1)
    r["w_swq_2"] = a["w_in_2"][0][:, SWQ:SWQ + TILE].reshape(D, 2, 4, SHD).transpose(0, 2, 1, 3).reshape(D, TILE)
    r["norm_f_g"] = a["norm_f_g"]
    r["norm_post_2"] = a["norm_post_2"]
    r["rows"] = np.concatenate([a["gm_norm_2"][0], a["dn_norm_2"][0], a["a_log_2"][0], a["dt_bias_2"][0], a["sinks_2"][0]])
    r["spatial_w_t"] = a["spatial_w_2"][0].transpose(2, 0, 1).reshape(P, 4 * P)
    r["sub_keys_t"] = a["peer_sub_keys"][0].reshape(HP, NKEY, P).transpose(2, 0, 1).reshape(P, HP * NKEY)
    r["u_t"] = a["peer_u"][0].reshape(NKEY, NKEY, KC, P).transpose(1, 3, 2, 0).reshape(NKEY, P, D)
    r["v_t"] = a["peer_v"][0].reshape(NKEY, NKEY, D).transpose(1, 0, 2)
    return r


def kernel(**inputs):
    import concourse.bacc as bacc
    from concourse import mybir as mb
    from concourse.bass_utils import run_bass_kernel_spmd

    nc = bacc.Bacc("TRN2", target_bir_lowering=False, num_devices=1)
    arrays, t = {}, {}
    import numpy as np
    for name, a in layout(inputs).items():
        a = np.ascontiguousarray(a)
        arrays[f"in_{name}"] = a
        t[name] = nc.dram_tensor(f"in_{name}", a.shape, mb.dt.from_np(a.dtype), kind="ExternalInput").ap()
    out = nc.dram_tensor("out_0", (1, T, D), F32, kind="ExternalOutput").ap()
    build(nc, t, out)
    r = run_bass_kernel_spmd(nc, [arrays], core_ids=[0])
    return r.results[0]["out_0"]
```

```python
import concourse.bass as bass
from concourse import mybir
from contextlib import ExitStack

F32 = mybir.dt.float32
F32R = mybir.dt.float32r
U32 = mybir.dt.uint32
I32 = mybir.dt.int32
U8 = mybir.dt.uint8
ALU = mybir.AluOpType
ACT = mybir.ActivationFunctionType
AX = mybir.AxisListType

P = 128
D = 1024
T = 256
NT = T // P
KC = D // P
EPS = 1e-6
TILE = 512
RING = 3

HQ, HF, HI, HGATE, GQ, GV, GLOW, GGATE = 0, 512, 1024, 1536, 2048, 2560, 3072, 3088
RANK = 16
HEADS1 = 8
NF = 6
LEVELS = 7
GLA_SCALE = 64.0 ** -0.5
GATE_NORM = 16.0

PH = 8
HP = 2 * PH
NKEY = 128
TOP = 16
SLOTS = PH * TOP
NEG = -3.0e38
GT = 4
GBUF = 4
ROUNDS = 4
FULL = 4
CAND = FULL * TOP + (TOP - FULL) * 4
NGRP = T // GT

DNQ, DNK, DNV, DNZ, DNBA, GMU, GMV, GMZ, SWQ, SWKV, SWZ, XMQ, XMZ, GATES = (
    0, 512, 1024, 1536, 2048, 2056, 2568, 3080, 3592, 4104, 4360, 4872, 5384, 5896)
DH = 4
TH = NT * DH
CONV = 4
SH, SHD = 8, 64
XH = 4
HEAD = 128
NBR = 4
MASKED = -1.0e30


def bcast(ap, dim, n):
    a = ap.unsqueeze(dim)
    shape = list(a.shape)
    shape[dim] = n
    return a.broadcast_to(shape)


def head_rows(h):
    if h < 4:
        return h, slice(0, P)
    g = h - 4
    return 4 + g // 2, slice(64 * (g % 2), 64 * (g % 2) + 64)


PLACE = [0, 1, 4, 5, 2, 6, 3, 7]


def build(nc, t, out):
    ctx = ExitStack()
    with ctx:
        def sb(name, shape, dt=F32):
            return ctx.enter_context(nc.sbuf_tensor(name, shape, dt))

        def sem(name):
            return ctx.enter_context(nc.semaphore(name))

        def lease(*tensors):
            with ExitStack() as own:
                return [own.enter_context(nc.sbuf_tensor(name, shape, dt)) for name, shape, dt in tensors]

        big = sb("big", [P, NKEY * T])
        resid = sb("resid", [P, NT, D])
        ident = sb("ident", [P, P])
        oi = sb("oi", [P, 2, P])
        ones, iota = oi[:, 0], oi[:, 1]
        act_j = oi[:].rearrange("p a b -> p (a b)")
        upper = sb("upper", [P, P])
        masks = sb("masks", [P, LEVELS + 1, P], U8)
        cols = sb("cols", [P, 94])
        mhalf = sb("mhalf", [P, 16])
        wh = sb("wh", [P, T], F32R)
        wl = sb("wl", [P, T], F32R)
        small = sb("small", [P, 512])
        ring, actT, mkv = lease(("ring", [P, RING, KC * TILE], F32), ("actT", [P, KC, T], F32), ("mkv", [P, 2, 1024], F32))
        raw, hi, lo, xh, xl = lease(("raw", [P, 2, 2, D], F32), ("hi", [P, 2, 2, D], F32R), ("lo", [P, 2, 2, D], F32R),
                                    ("xh", [P, KC, T], F32R), ("xl", [P, KC, T], F32R))
        mkT = mkv[:, 0].rearrange("p (h m) -> p h m", h=4)
        mv = mkv[:, 1].rearrange("p (n d) -> p n d", n=NT)
        ps = ctx.enter_context(nc.psum_tensor("ps", [P, 8, TILE], F32))

        C_N1, C_N2, C_PRE, C_MEM, C_LOG, C_BG, C_CONV, C_SB = 0, 8, 16, 24, 32, 40, 42, 90

        def arena(base, width):
            at = [0]

            def take(*shape, dt=F32):
                n = 1
                for s in shape:
                    n *= s
                assert at[0] + n <= width, (at[0], n)
                v = base[:, at[0]:at[0] + n]
                at[0] += n
                if dt is not F32:
                    v = v.bitcast(dt)
                if len(shape) == 1:
                    return v
                names = " ".join(f"a{i}" for i in range(len(shape)))
                return v.rearrange(f"p ({names}) -> p {names}", **{f"a{i}": s for i, s in enumerate(shape)})
            return take

        take_small = arena(small[:], 512)
        sumsq = take_small(NT)
        mean = take_small(NT)
        rstd = take_small(NT)
        lbe = take_small(2, 4)
        lbm = take_small(4)
        lbs = take_small(4)
        lbr = take_small(4)
        lb = take_small(4)
        lb1 = take_small(4)
        sumsq_o = take_small(NT, HEADS1)
        mean_o = take_small(NT, HEADS1)
        rstd_o = take_small(NT, HEADS1)
        sumsq_m = take_small(NT)
        mean_m = take_small(NT)
        rstd_m = take_small(NT)
        sumsq_h = take_small(NT)
        mean_h = take_small(NT)
        rstd_h = take_small(NT)
        esum = take_small(NT, PH)
        einv = take_small(NT, PH)

        take1 = arena(big[:], NKEY * T)
        scaled = take1(NT, D)
        qF = take1(NF, T)
        kF = take1(NF, T)
        gF = take1(NF, T)
        cum = take1(NF, T)
        dec = take1(2, NF, T)
        qd = take1(2, NF, T)
        kd = take1(2, NF, T)
        vtok = take1(NT, D)
        gate1 = take1(NT, D)
        glowT = take1(T)
        gate_up = take1(2, P)[0:RANK]
        zg = gate1[:, 0, 0:TILE].rearrange("p (a t) -> p a t", a=2)
        zabs = gate1[:, 0, TILE:D].rearrange("p (a t) -> p a t", a=2)
        own = take1(NT, HEADS1, P)
        cross = take1(HEADS1, P)
        mixed = take1(NT, D)
        mixT = take1(KC, T)
        sqtmp = take1(NT, D)
        xi = take1(P, dt=I32)
        xj = take1(P, dt=I32)
        xx = take1(P, dt=I32)
        xf = take1(P)
        ge = cross
        gnorm = take1(2, P)
        glow_w = take1(KC, RANK)
        memtok = own.rearrange("p n h i -> p n (h i)")
        memT = mixT
        mkv_new = sqtmp

        x_loaded = sem("x_loaded")
        keys_loaded = sem("keys_loaded")
        params_loaded = sem("params_loaded")
        mem_loaded = sem("mem_loaded")
        mem_scaled = sem("mem_scaled")
        mem_T = sem("mem_T")
        memT_done = sem("memT_done")
        tile_loaded = [sem(f"tile_loaded{i}") for i in range(RING)]
        consts_made = sem("consts_made")
        pool_step = sem("pool_step")
        dve_step = sem("dve_step")
        act_step = sem("act_step")
        sumsq_done = sem("sumsq_done")
        rstd_done = sem("rstd_done")
        scaled_done = sem("scaled_done")
        transposed = sem("transposed")
        actT_done = [sem("actT_by_act"), sem("actT_by_dve")]
        group_done = sem("group_done")
        group_out = sem("group_out")
        fgate_done = sem("fgate_done")
        logf_done = sem("logf_done")
        gate_mm = sem("gate_mm")
        softplus_done = sem("softplus_done")
        cum_done = sem("cum_done")
        lb_in = sem("lb_in")
        lb_exp = sem("lb_exp")
        masks_done = sem("masks_done")
        lvl_exponent = sem("lvl_exponent")
        lvl_decay = sem("lvl_decay")
        lvl_scaled = sem("lvl_scaled")
        lvl_scores = sem("lvl_scores")
        lvl_kept = sem("lvl_kept")
        cross_out = sem("cross_out")
        o_done = sem("o_done")
        osq_done = sem("osq_done")
        osum_done = sem("osum_done")
        orstd_done = sem("orstd_done")
        mixed_done = sem("mixed_done")
        wout_done = sem("wout_done")
        h_done = sem("h_done")
        sub_done = sem("sub_done")
        sub_out = sem("sub_out")
        matched = sem("matched")
        pick_kept = sem("pick_kept")
        picks_done = sem("picks_done")
        pick_mm = sem("pick_mm")
        pickT_done = sem("pickT_done")
        soft_in = sem("soft_in")
        soft_exp = sem("soft_exp")
        onehot_ready = sem("onehot_ready")
        onehot_weighted = sem("onehot_weighted")
        onehot_by_act = sem("onehot_by_act")
        dist_done = sem("dist_done")
        g_mm = sem("g_mm")
        g_out = sem("g_out")
        u_loaded = [sem(f"u_loaded{i}") for i in range(2)]
        v_loaded = [sem(f"v_loaded{i}") for i in range(2)]
        u_mm = sem("u_mm")
        gelu_done = sem("gelu_done")
        prod_done = sem("prod_done")
        wh_done = sem("wh_done")
        wl_done = sem("wl_done")
        hi_done = [sem("u_hi_done"), sem("v_hi_done")]
        lo_done = [sem("u_lo_done"), sem("v_lo_done")]
        x_split = sem("x_split")
        mkv_stored = sem("mkv_stored")
        mkv_loaded = sem("mkv_loaded")
        v_mm = sem("v_mm")
        peer_out = sem("peer_out")

        t["mkv_keep"] = nc.dram_tensor("mkv_keep", (P, 2048), F32, kind="Internal").ap()

        def wtile(name, c0, n=TILE):
            src = t[name][:, c0:c0 + n].rearrange("(c p) n -> p c n", p=P)
            return lambda s: (ring[:, s, 0:KC * n].rearrange("p (c n) -> p c n", c=KC), src)

        tiles1 = [("hq", wtile("w_in", HQ)), ("hf", wtile("w_in", HF)), ("gqk", wtile("w_in", GQ)),
                  ("hi", wtile("w_in", HI)), ("gv", wtile("w_in", GV)),
                  ("hgate", wtile("w_in", HGATE)), ("ggate", wtile("w_in", GGATE)),
                  ("wo0", wtile("w_out", 0)), ("wo1", wtile("w_out", TILE)),
                  ("wq0", wtile("peer_w_q", 0)), ("wq1", wtile("peer_w_q", TILE)),
                  ("wq2", wtile("peer_w_q", 2 * TILE)), ("wq3", wtile("peer_w_q", 3 * TILE)),
                  ("mk", wtile("w_mem_kv_2", 0)), ("mv", wtile("w_mem_kv_2", TILE))]
        tile_no = {name: i for i, (name, _) in enumerate(tiles1)}
        N1 = len(tiles1)

        def slot(name):
            return tile_no[name] % RING

        def tile_view(name):
            return ring[:, slot(name), :].rearrange("p (c n) -> p c n", c=KC)

        groups1 = ["hq0", "hq1", "hf0", "hf1", "gqk0", "gqk1", "glow", "hi0", "hi1", "gv0", "gv1",
                   "hgate0", "hgate1", "ggate0", "ggate1",
                   "wq00", "wq01", "wq10", "wq11", "wq20", "wq21", "wq30", "wq31", "mk0", "mk1", "mv0", "mv1"]
        group_no = {g: i for i, g in enumerate(groups1)}

        def gbank(g):
            return group_no[g] % 4

        def tile_used(name):
            if name in ("wo0", "wo1"):
                return wout_done, 2 * int(name[2]) + 2
            return group_done, group_no[name + "1"] + 1

        takeP = arena(big[:], NKEY * T)
        scaled_p = takeP(NT, D)
        qT = takeP(HP, T)
        ssb = takeP(NT, HP, NKEY)
        srest = takeP(NT, 4, NKEY)
        stop_ = takeP(ROUNDS, 2, NT * 2, TOP)
        sidx = takeP(ROUNDS, 2, NT * 2, TOP, dt=U32)
        sidxf = takeP(ROUNDS, 2, NT * 2, TOP)
        cand = takeP(NT * 2, CAND)
        crest = takeP(NT * 2, CAND)
        best = takeP(NT, PH, TOP)
        pos = takeP(NT, PH, TOP, dt=U32)
        posi = takeP(3, NT, 2 * TOP, dt=U32)
        posf = takeP(3, NT, 2 * TOP)
        place = takeP(2, NT * 2, TOP)
        pick = takeP(2, 2, NT * 2, TOP, TOP)
        chosen = takeP(NT, 3, SLOTS)
        G = big[:].rearrange("p (t j) -> p t j", j=NKEY)
        takeR = arena(ring[:, 1:3, :].rearrange("p s n -> p (s n)"), 2 * KC * TILE)
        chosenT = takeR(3, T)
        hotA = takeR(GBUF, GT, NKEY)
        matchB = takeR(GBUF, GT, NKEY)
        hotB = takeR(GBUF, GT, NKEY)
        dist = takeR(GBUF, NKEY)
        minus_w = takeR(T)
        xround = takeP(KC, T)

        def round_keys(r, a):
            return bcast(sidxf[:, r, a], 2, TOP)

        keysT = mixed.rearrange("p n (a m) -> p (n a) m", m=NKEY)
        U, V = 0, 1

        take2 = arena(big[:], NKEY * T)
        u1 = take2(3108)
        u2 = take2(2048)
        u3 = take2(3072)
        u4 = take2(3072)
        u5 = take2(2048)
        u6 = take2(3072 + 512)
        zdn = take2(NT, TILE)
        gu = take2(NT, TILE)
        gv2 = take2(NT, TILE)
        gz = take2(NT, TILE)
        swqT = take2(4, T)
        swkv = take2(TILE)
        swz = take2(NT, TILE)
        prob = take2(3072)
        probT = take2(3072)
        xmqT = take2(4, T)
        xmz = take2(NT, TILE)
        rows = take2(656)
        window = take2(2, P)
        gm_gain, dn_gain = rows[:, 0:TILE], rows[:, TILE:TILE + P]
        a_log, dt_bias, sinks = rows[:, 640:644], rows[:, 644:648], rows[:, 648:656]
        scaled2 = u1[:, 0:2048].rearrange("p (n d) -> p n d", n=NT)
        convin = u1.rearrange("p (f t) -> p f t", f=3 * DH)
        a1 = arena(u1, 3108)
        LT, AQ, BT = a1(TH, P), a1(TH, P), a1(TH, P)
        norm_f = u2[:, 0:D]
        sqk = u2.rearrange("p (f t) -> p f t", f=2 * DH)
        a2 = arena(u2, 2048)
        X, Z = a2(TH, P), a2(TH, P)
        rep = u3.rearrange("p (a h m) -> p a h m", a=3, h=TH)
        a3 = arena(u3, 3072)
        Y, kbg, vb = a3(TH, P), a3(TH, P), a3(TH, P)
        convT = u4.rearrange("p (f t) -> p f t", f=3 * DH)
        a5 = arena(u5, 2048)
        du, wT, S1 = a5(TH, P), a5(DH, P), a5(DH, P)
        a6 = arena(u6, 3584)
        Dm, brow, qrow, qg = a6(TH, P), a6(TH, P), a6(TH, P), a6(DH, P)
        a3b = arena(brow.rearrange("p h c -> p (h c)"), 1024)
        kdl, vnew = a3b(DH, P), a3b(DH, P)
        wsT = probT[:, 0:4 * P].rearrange("p (g q) -> p g q", g=4)
        swkT, swv = swkv[:, 0:T], swkv[:, T:2 * T].rearrange("p (n d) -> p n d", n=NT)
        take3 = arena(big[:, 0:17000], 17000)
        yT = take3(NBR * 4, T)
        gsb = take3(2, 4, TILE)
        merged = take3(NT, D)
        outsb = take3(NT, D)
        norm_post = take3(D)
        sumsq_f, mean_f, rstd_f = (take_small(NT) for _ in range(3))
        sumsq_x, mean_x, rstd_x = (take_small(NT) for _ in range(3))
        sumsq_p, mean_p, rstd_p = (take_small(NT) for _ in range(3))
        ba_w = take_small(KC, 2 * DH)
        ba = take_small(NT, 2 * DH)
        beta = take_small(NT, DH)
        dz = take_small(NT, DH)
        dsp = take_small(NT, DH)
        nega = take_small(DH)
        dg = take_small(NT, DH)
        rin = take_small(NT, 2 * DH)
        rr = take_small(NT, 2 * DH)
        gcs = take_small(2, TH)
        egc = take_small(NT, DH)
        ekd = take_small(DH)
        brk = take_small(NT, DH)
        rqs = take_small(NT, DH)
        kbf = take_small(NT, DH)
        sumsq_a, mean_a, rstd_a = (take_small(NT, DH) for _ in range(3))
        sumsq_v, mean_v, rstd_v = (take_small(NT) for _ in range(3))
        smax, snm, sden, srec, ssk = (take_small(NT, SH) for _ in range(5))
        xmax, xnm, xden, xrec = (take_small(NT, XH) for _ in range(4))

        rows_loaded = sem("rows_loaded")
        x1_done = sem("x1_done")
        g2_done = sem("g2_done")
        g2_out = sem("g2_out")
        conv_done = sem("conv_done")
        conv_zero = sem("conv_zero")
        dnsilu_done = sem("dnsilu_done")
        dnsq_done = sem("dnsq_done")
        ss_mm = sem("ss_mm")
        rin_done = sem("rin_done")
        rr_done = sem("rr_done")
        beta_done = sem("beta_done")
        dz_done = sem("dz_done")
        dln_done = sem("dln_done")
        dg_done = sem("dg_done")
        gc_mm = sem("gc_mm")
        gcs_done = sem("gcs_done")
        egc_done = sem("egc_done")
        rep_done = sem("rep_done")
        row_mm = sem("row_mm")
        dm_in = sem("dm_in")
        dm_done = sem("dm_done")
        brow_done = sem("brow_done")
        qrow_done = sem("qrow_done")
        kk_mm = sem("kk_mm")
        lt_done = sem("lt_done")
        qk_mm = sem("qk_mm")
        aq_done = sem("aq_done")
        kv_tr = sem("kv_tr")
        kv_out = sem("kv_out")
        z0_done = sem("z0_done")
        x0_tr = sem("x0_tr")
        x_done = sem("x_done")
        bt_done = sem("bt_done")
        y_mm = sem("y_mm")
        y_out = sem("y_out")
        pz_mm = sem("pz_mm")
        z_done = sem("z_done")
        u_out_mm = sem("u_out_mm")
        du_done = sem("du_done")
        wt_done = sem("wt_done")
        s1_mm = sem("s1_mm")
        s1_done = sem("s1_done")
        ws_mm = sem("ws_mm")
        vnew_done = sem("vnew_done")
        qg_done = sem("qg_done")
        do_mm = sem("do_mm")
        dosq_done = sem("dosq_done")
        dosum_done = sem("dosum_done")
        dors_done = sem("dors_done")
        y_done = [sem(f"y_done{n}") for n in range(NBR)]
        gmv_sq = sem("gmv_sq")
        gmv_rstd = sem("gmv_rstd")
        gmv_done = sem("gmv_done")
        gm_mm = sem("gm_mm")
        ss_mm2 = sem("sw_scores")
        s_masked = sem("sw_masked")
        s_exp = sem("sw_exp")
        s_tr = sem("sw_transposed")
        s_trout = sem("sw_probT")
        so_mm = sem("sw_out")
        xs_mm = sem("xm_scores")
        xs_max = sem("xm_max")
        xs_exp = sem("xm_exp")
        xs_tr = sem("xm_transposed")
        xs_trout = sem("xm_probT")
        xo_mm = sem("xm_out")
        yT_mm = sem("yT_mm")
        yT_done = sem("yT_done")
        up_mm = sem("up_mm")
        up_out = sem("up_out")
        merged_done = sem("merged_done")
        fin_mm = sem("fin_mm")
        fin_copied = sem("fin_copied")
        out_done = sem("out_done")
        stored = sem("stored")

        def up_tile(n):
            src = t["w_up_2"][n].rearrange("(c p) n -> p c n", p=P)
            return lambda s: (ring[:, s, :].rearrange("p (c n) -> p c n", c=4), src)

        tiles2 = [(name, wtile("w_in_2", c)) for name, c in
                  (("dnq", DNQ), ("dnk", DNK), ("dnv", DNV), ("dnz", DNZ), ("gmu", GMU), ("gmv", GMV),
                   ("gmz", GMZ))]
        tiles2 += [("swq", wtile("w_swq_2", 0)), ("swkv", wtile("w_in_2", SWKV, T)), ("swz", wtile("w_in_2", SWZ)),
                   ("xmq", wtile("w_in_2", XMQ)), ("xmz", wtile("w_in_2", XMZ))]
        for n in range(NBR):
            tiles2 += [(f"gate{n}{h}", wtile("w_in_2", GATES + n * D + h * TILE)) for h in range(2)]
            tiles2 += [(f"up{n}", up_tile(n))]
        tiles2 += [("out0", wtile("w_out_2", 0)), ("out1", wtile("w_out_2", TILE))]
        tile2_no = {name: i for i, (name, _) in enumerate(tiles2)}
        loads1 = [len(range(s, N1, RING)) for s in range(RING)]
        groups2 = ["dnq0", "dnq1", "dnk0", "dnk1", "dnv0", "dnv1", "ba", "dnz0", "dnz1", "gmu0", "gmu1", "gmv0", "gmv1",
                   "gmz0", "gmz1", "swq0", "swq1", "swkv", "swz0", "swz1", "xmq0", "xmq1", "xmz0", "xmz1"]
        for n in range(NBR):
            groups2 += [f"gate{n}{h}{k}" for h in range(2) for k in range(NT)]
        g2_no = {g: i for i, g in enumerate(groups2)}

        def tile2_used(name):
            if name[:2] == "up":
                return up_mm, 4 * int(name[2]) + 4
            if name[:3] == "out":
                return fin_mm, 2 * int(name[3]) + 2
            return g2_done, g2_no["swkv" if name == "swkv" else name + "1"] + 1

        block = ctx.enter_context(nc.Block())

        @block.sync
        def _(sp):
            sp.dma_start(resid[:], t["x"].rearrange("b (n p) d -> p (b n) d", p=P)).then_inc(x_loaded, 16)
            sp.wait_ge(params_loaded, 80)
            for k, (name, make) in enumerate(tiles1):
                if k >= RING:
                    sp.wait_ge(*tile_used(tiles1[k - RING][0]))
                dst, src = make(k % RING)
                sp.dma_start(dst, src).then_inc(tile_loaded[k % RING], 16)
                if name == "wo1":
                    sp.wait_ge(o_done, NT)
                    sp.dma_start(memtok, t["mem_2"].rearrange("b (n p) d -> p (b n) d", p=P)).then_inc(mem_loaded, 16)
                if name == "wq0":
                    sp.wait_ge(transposed, 8)
                    sp.dma_start(keysT.rearrange("p a n -> p (a n)"), t["sub_keys_t"]).then_inc(keys_loaded, 16)
            sp.wait_ge(*tile_used("wq3"))
            loaded = (u_loaded, v_loaded)

            def load_rows(which, j, par, before=None):
                if before is not None:
                    sp.wait_ge(lo_done[which], before)
                sp.dma_start(raw[:, which, par], t[("u_t", "v_t")[which]][bass.ds(j, 1), :, :].rearrange("o p n -> p (o n)")).then_inc(loaded[which][par], 16)

            for j in range(2):
                load_rows(U, j, j)
                load_rows(V, j, j)
            sp.wait_ge(group_out, group_no["mv1"] + 1)
            sp.dma_start(t["mkv_keep"], mkv_new.rearrange("p a n -> p (a n)")).then_inc(mkv_stored, 16)
            with sp.Fori(1, NKEY // 2) as i:
                for par in range(2):
                    load_rows(U, 2 * i + par, par, 2 * i + (par - 1))
                    load_rows(V, 2 * i + par, par, 2 * i + (par - 1))
            sp.wait_ge(prod_done, NKEY)
            sp.dma_start(norm_f, t["norm_f_g"].partition_broadcast(P)).then_inc(rows_loaded, 16)
            sp.dma_start(rows, t["rows"].partition_broadcast(P)).then_inc(rows_loaded, 16)
            sp.dma_start(ba_w, t["w_in_2"][:, DNBA:DNBA + 2 * DH].rearrange("(c p) n -> p c n", p=P)).then_inc(rows_loaded, 16)
            sp.dma_start(wsT, t["spatial_w_t"].rearrange("p (g q) -> p g q", g=4)).then_inc(rows_loaded, 16)
            sp.wait_ge(u_mm, NKEY)
            sp.wait_ge(mkv_stored, 16)
            sp.dma_start(mkv[:].rearrange("p a n -> p (a n)"), t["mkv_keep"]).then_inc(mkv_loaded, 16)
            sp.wait_ge(v_mm, NKEY)
            for k, (name, make) in enumerate(tiles2):
                if k >= RING:
                    sp.wait_ge(*tile2_used(tiles2[k - RING][0]))
                dst, src = make(k % RING)
                sp.dma_start(dst, src).then_inc(tile_loaded[k % RING], 16)
            sp.dma_start(norm_post, t["norm_post_2"][0].partition_broadcast(P)).then_inc(rows_loaded, 16)
            for n in range(NT):
                sp.wait_ge(out_done, n + 1)
                sp.dma_start(out[0, n * P:(n + 1) * P, :], outsb[:, n]).then_inc(stored, 16)
            sp.wait_ge(stored, 16 * NT)

        @block.gpsimd
        def _(pool):
            steps = [0]

            def link(ins):
                steps[0] += 1
                ins.then_inc(pool_step, 1)
                pool.wait_ge(pool_step, steps[0])

            def rsqrt(o, m, s, width, n):
                link(pool.tensor_scalar(m, s, 1.0 / width, EPS, ALU.mult, ALU.add))
                return pool.tensor_tensor(o, m, n, ALU.pow)

            pool.memset(ident[:], 0.0).then_inc(pool_step, 1)
            pool.memset(ones, 1.0).then_inc(pool_step, 1)
            pool.memset(mhalf[:], -0.5).then_inc(pool_step, 1)
            steps[0] = 3
            pool.wait_ge(pool_step, 3)
            pool.affine_select(out=ident[:], in_=ident[:], compare_op=ALU.not_equal, fill=1.0, base=0,
                               pattern=[[-1, P]], channel_multiplier=1)
            pool.affine_select(out=upper[:], in_=ones, compare_op=ALU.is_ge, fill=0.0, base=0,
                               pattern=[[1, P]], channel_multiplier=-1)
            pool.iota(iota, pattern=[[1, P]], base=0, channel_multiplier=0, allow_small_or_imprecise_dtypes=True)
            pool.iota(xi, pattern=[[1, P]], base=0, channel_multiplier=0)
            pool.iota(xj, pattern=[[0, P]], base=0, channel_multiplier=1).then_inc(consts_made, 1)
            pool.wait_ge(sumsq_done, 2)
            rsqrt(rstd, mean, sumsq, D, mhalf[:, 0:NT]).then_inc(rstd_done, 1)
            for l in range(LEVELS):
                m = 1 << l
                if l == 0:
                    pool.wait_ge(cum_done, 2 * NF)
                if l >= 2:
                    pool.wait_ge(lvl_scaled, l - 1)
                c = cum.rearrange("p f (b two m) -> p (f b) two m", two=2, m=m)
                d = dec[:, l % 2].rearrange("p f (b two m) -> p (f b) two m", two=2, m=m)
                mid = c[:, :, 0, m - 1:m].broadcast_to([P, NF * T // (2 * m), m])
                pool.tensor_tensor(d[:, :, 1, :], c[:, :, 1, :], mid, ALU.subtract)
                pool.tensor_tensor(d[:, :, 0, :], mid, c[:, :, 0, :], ALU.subtract).then_inc(lvl_exponent, 1)
            pool.wait_ge(lvl_scaled, LEVELS - 1)
            last = cum[:, :, P - 1:P].broadcast_to([P, NF, P])
            pool.tensor_tensor(dec[:, 1, :, 0:P], last, cum[:, :, 0:P], ALU.subtract).then_inc(lvl_exponent, 1)
            for n in range(NT):
                pool.wait_ge(osum_done, n + 1)
                rsqrt(rstd_o[:, n], mean_o[:, n], sumsq_o[:, n], P, mhalf[:, 0:HEADS1]).then_inc(orstd_done, 1)
            pool.wait_ge(sumsq_done, 4)
            rsqrt(rstd_h, mean_h, sumsq_h, D, mhalf[:, 0:NT]).then_inc(rstd_done, 1)
            pool.wait_ge(sumsq_done, 6)
            rsqrt(rstd_m, mean_m, sumsq_m, D, mhalf[:, 0:NT]).then_inc(rstd_done, 1)
            for r in range(ROUNDS - 1):
                for a in range(2):
                    pool.wait_ge(matched, 2 * r + a + 1)
                    pool.tensor_tensor(pick[:, r % 2, a], pick[:, r % 2, a], round_keys(r, a), ALU.mult).then_inc(pick_kept, 1)

            def weigh(n, at, buf, first=False):
                pool.wait_ge(onehot_ready, n)
                if not first:
                    pool.wait_ge(g_mm, n - GBUF)
                pool.tensor_tensor(hotB[:, buf, 1:GT], matchB[:, buf, 1:GT], bcast(chosenT[:, 2, at], 2, NKEY), ALU.mult).then_inc(onehot_weighted, 1)

            for b in range(GBUF):
                weigh(b + 1, slice(b * GT + 1, b * GT + GT), b, first=True)
            with pool.Fori(1, NGRP // GBUF) as i:
                for b in range(GBUF):
                    weigh(GBUF * i + (b + 1), bass.ds(i * (GBUF * GT) + (b * GT + 1), GT - 1), b)
            pool.wait_ge(wl_done, NKEY)
            pool.memset(ones, 1.0).then_inc(consts_made, 1)
            pool.wait_ge(sumsq_done, 8)
            rsqrt(rstd_f, mean_f, sumsq_f, D, mhalf[:, 0:NT]).then_inc(rstd_done, 1)
            pool.wait_ge(sumsq_done, 10)
            rsqrt(rstd_x, mean_x, sumsq_x, D, mhalf[:, 0:NT]).then_inc(rstd_done, 1)
            pool.wait_ge(rin_done, 1)
            pool.tensor_tensor(rr.rearrange("p n f -> p (n f)"), rin.rearrange("p n f -> p (n f)"), mhalf[:], ALU.pow).then_inc(rr_done, 1)
            pool.wait_ge(gmv_sq, 2)
            rsqrt(rstd_v, mean_v, sumsq_v, TILE, mhalf[:, 0:NT]).then_inc(gmv_rstd, 1)
            for n in range(NT):
                pool.wait_ge(dosum_done, n + 1)
                rsqrt(rstd_a[:, n], mean_a[:, n], sumsq_a[:, n], HEAD, mhalf[:, 0:DH]).then_inc(dors_done, 1)
            pool.wait_ge(sumsq_done, 12)
            rsqrt(rstd_p, mean_p, sumsq_p, D, mhalf[:, 0:NT]).then_inc(rstd_done, 1)

        @block.scalar
        def _(act):
            steps = [0]

            def link(ins):
                steps[0] += 1
                ins.then_inc(act_step, 1)
                act.wait_ge(act_step, steps[0])

            act.dma_start(cols[:], t["cols"]).then_inc(params_loaded, 16)
            act.dma_start(glow_w, t["w_in"][:, GLOW:GLOW + RANK].rearrange("(c p) n -> p c n", p=P)).then_inc(params_loaded, 16)
            act.dma_start(gate_up.rearrange("p a n -> p (a n)"), t["gla_w_gate_up"][0]).then_inc(params_loaded, 16)
            act.dma_start(gnorm[:, 0], t["hg_norm_g"][0].partition_broadcast(P)).then_inc(params_loaded, 16)
            act.dma_start(gnorm[:, 1], t["gla_norm_g"][0].partition_broadcast(P)).then_inc(params_loaded, 16)
            act.wait_ge(x_loaded, 16)
            for n in range(NT):
                act.activation(sqtmp[:, n], resid[:, n], ACT.Square, accum_out=sumsq[:, n:n + 1]).then_inc(sumsq_done, 1)
            act.wait_ge(params_loaded, 80)
            act.wait_ge(lb_in, 1)
            act.activation(lbe.rearrange("p a f -> p (a f)"), lbe.rearrange("p a f -> p (a f)"), ACT.Exp).then_inc(lb_exp, 1)

            def copy_out_T(n_before, dst, gcol=None, first=4):
                for c in (2, 3, 6, 7):
                    act.wait_ge(transposed, n_before + c // 2 + 1)
                    src = ps[:, 4 + c // 2, (c % 2) * T:(c % 2 + 1) * T]
                    if gcol is None:
                        ins = act.activation(dst[:, c], src, ACT.Copy)
                    else:
                        ins = act.activation(dst[:, c], src, ACT.Copy, scale=cols[:, gcol + c:gcol + c + 1])
                    ins.then_inc(actT_done[0], 1)

            copy_out_T(0, actT, C_N1)

            def from_group(g):
                act.wait_ge(group_done, group_no[g] + 1)
                return ps[:, gbank(g), :]

            def out_group(g, dst, func, **kw):
                act.activation(dst, from_group(g), func, **kw).then_inc(group_out, 1)

            def feat(ap):
                return ap.rearrange("p f t -> p (f t)")

            for a in range(2):
                out_group(f"hq{a}", feat(qF[:, 2 * a:2 * a + 2]), ACT.Silu)
            for a in range(2):
                out_group(f"hf{a}", feat(gF[:, 2 * a:2 * a + 2]), ACT.Sigmoid)
            out_group("gqk0", feat(qF[:, 4:6]), ACT.Copy, scale=GLA_SCALE)
            out_group("gqk1", feat(kF[:, 4:6]), ACT.Copy)
            act.wait_ge(group_done, group_no["glow"] + 1)
            act.activation(glowT[0:RANK], ps[0:RANK, gbank("glow"), 0:T], ACT.Copy).then_inc(group_out, 1)
            act.wait_ge(fgate_done, 1)
            act.activation(feat(gF[:, 0:4]), feat(gF[:, 0:4]), ACT.Ln).then_inc(logf_done, 1)
            act.wait_ge(gate_mm, 1)
            for a in range(2):
                act.activation(zg[:, a], ps[:, 7, a * T:(a + 1) * T], ACT.Identity,
                               bias=cols[:, C_BG + a:C_BG + a + 1]).then_inc(act_step, 1)
            steps[0] += 2
            act.wait_ge(act_step, steps[0])
            link(act.activation(feat(zabs), feat(zg), ACT.Abs))
            link(act.activation(feat(zabs), feat(zabs), ACT.Exp, scale=-1.0))
            act.activation(feat(zabs), feat(zabs), ACT.Ln, bias=1.0).then_inc(softplus_done, 1)
            for a in range(NT):
                out_group(f"hi{a}", vtok[:, a, 0:TILE], ACT.Copy)
            for a in range(NT):
                out_group(f"gv{a}", vtok[:, a, TILE:D], ACT.Copy)
            for l in range(LEVELS):
                act.wait_ge(lvl_exponent, l + 1)
                act.activation(feat(dec[:, l % 2]), feat(dec[:, l % 2]), ACT.Exp).then_inc(lvl_decay, 1)
            act.wait_ge(lvl_exponent, LEVELS + 1)
            act.activation(dec[:, 1, :, 0:P], dec[:, 1, :, 0:P], ACT.Exp)
            act.activation(dec[:, 1, :, P:T], cum[:, :, P:T], ACT.Exp).then_inc(lvl_decay, 1)
            for g, dst, f in (("hgate0", gate1[:, 0, 0:TILE], ACT.Silu), ("hgate1", gate1[:, 1, 0:TILE], ACT.Silu),
                              ("ggate0", gate1[:, 0, TILE:D], ACT.Silu), ("ggate1", gate1[:, 1, TILE:D], ACT.Silu)):
                out_group(g, dst, f)
            act.wait_ge(lvl_scores, 2 * (LEVELS + 1) + 1)
            act.activation(cross.rearrange("p h i -> p (h i)"), ps[:, 4:6, :].rearrange("p b n -> p (b n)"), ACT.Copy).then_inc(cross_out, 1)
            for n in range(NT):
                act.wait_ge(o_done, n + 1)
                act.activation(sqtmp[:, n], ps[:, 4 + 2 * n:6 + 2 * n, :].rearrange("p b n -> p (b n)"), ACT.Square).then_inc(osq_done, 1)
            copy_out_T(4, mixT)
            act.wait_ge(h_done, 4)
            for n in range(NT):
                act.activation(sqtmp[:, n], resid[:, n], ACT.Square, accum_out=sumsq_h[:, n:n + 1]).then_inc(sumsq_done, 1)
            act.wait_ge(mem_loaded, 16)
            act.wait_ge(sumsq_done, 4)
            for n in range(NT):
                act.activation(sqtmp[:, n], memtok[:, n], ACT.Square, accum_out=sumsq_m[:, n:n + 1]).then_inc(sumsq_done, 1)
            copy_out_T(8, actT, C_N2)

            def out_scores(r):
                for n in range(NT):
                    act.wait_ge(sub_done, NT * r + n + 1)
                    act.activation(ssb[:, n, 4 * r:4 * r + 4].rearrange("p a n -> p (a n)"), ps[:, 4 + (NT * r + n) % 4, :], ACT.Copy).then_inc(sub_out, 1)

            for r in range(ROUNDS):
                for b in range(2):
                    out_group(f"wq{r}{b}", feat(qT[:, 4 * r + 2 * b:4 * r + 2 * b + 2]), ACT.Copy)
                    if r and not b:
                        out_scores(r - 1)
                if r == 0:
                    act.wait_ge(rstd_done, 3)
                    act.wait_ge(sumsq_done, 6)
                    for n in range(NT):
                        act.activation(memtok[:, n], memtok[:, n], ACT.Copy, scale=rstd_m[:, n:n + 1]).then_inc(mem_scaled, 1)
            out_scores(ROUNDS - 1)
            for c in range(KC):
                act.wait_ge(mem_T, c // 2 + 1)
                act.activation(memT[:, c], ps[:, c // 2, (c % 2) * T:(c % 2 + 1) * T], ACT.Copy, scale=cols[:, C_MEM + c:C_MEM + c + 1]).then_inc(memT_done, 1)
            for k, g in enumerate(("mk0", "mk1", "mv0", "mv1")):
                out_group(g, mkv_new.rearrange("p a n -> p (a n)")[:, k * TILE:(k + 1) * TILE], ACT.Copy)
            act.activation(feat(xround.bitcast(F32R)), feat(actT), ACT.Copy).then_inc(x_split, 1)
            act.wait_ge(soft_in, 1)
            e = best.rearrange("p n h k -> p (n h k)")
            act.activation(e, e, ACT.Exp).then_inc(soft_exp, 1)
            act.wait_ge(x_split, 2)
            act.activation(xh[:].rearrange("p c t -> p (c t)"), feat(xround), ACT.Copy).then_inc(x_split, 1)

            def g_evac(n, at, b):
                act.wait_ge(g_mm, n)
                act.activation(G[:, at, :].rearrange("p t j -> p (t j)"), ps[:, b, :], ACT.Copy).then_inc(g_out, 1)

            act.wait_ge(pickT_done, 3)
            act.wait_ge(mkv_stored, 16)
            tok = lambda g: slice(g * GT, g * GT + 1)

            def distances(n, at, b):
                act.activation(dist[:, b], iota, ACT.Abs, scale=-1.0, bias=chosenT[:, 1, at]).then_inc(dist_done, 1)

            def hot_row(n, at, b):
                act.wait_ge(dist_done, n)
                act.activation(hotB[:, b, 0], dist[:, b], ACT.Relu, scale=minus_w[:, at], bias=chosenT[:, 2, at]).then_inc(onehot_by_act, 1)

            for g in range(3):
                distances(g + 1, tok(g), g)
            for g in range(2):
                hot_row(g + 1, tok(g), g)
            with act.Fori(0, NGRP // GBUF - 1) as i:
                for b in range(GBUF):
                    act.wait_ge(onehot_by_act, GBUF * i + (b + 1))
                    distances(GBUF * i + (b + 4), bass.ds(i * (GBUF * GT) + (b + 3) * GT, 1), (b + 3) % GBUF)
                    hot_row(GBUF * i + (b + 3), bass.ds(i * (GBUF * GT) + (b + 2) * GT, 1), (b + 2) % GBUF)
                    g_evac(GBUF * i + (b + 1), bass.ds(i * (GBUF * GT) + b * GT, GT), b)
            for b in range(GBUF):
                g = NGRP - GBUF + b
                if b == 0:
                    act.wait_ge(onehot_by_act, g + 1)
                    distances(g + 4, tok(g + 3), 3)
                if b < 2:
                    hot_row(g + 3, tok(g + 2), b + 2)
                g_evac(g + 1, slice(g * GT, g * GT + GT), b)

            loaded = (u_loaded, v_loaded)

            def split_hi(which, loads, par):
                act.wait_ge(loaded[which][par], loads)
                act.activation(hi[:, which, par], raw[:, which, par], ACT.Copy).then_inc(hi_done[which], 1)

            def second_key(n, loads, par, first=False, last=False, wait=True):
                if wait:
                    act.wait_ge(v_mm, n - 2)
                split_hi(V, loads, par)
                act.wait_ge(u_mm, n)
                if not first:
                    act.wait_ge(wl_done, n - 1)
                act.activation(act_j, ps[:, par, 0:T], ACT.Gelu).then_inc(gelu_done, 1)
                if not last:
                    split_hi(U, loads + 16, par)
                act.wait_ge(prod_done, n)
                if not first:
                    act.wait_ge(v_mm, n - 1)
                act.activation(wh[:], act_j, ACT.Copy).then_inc(wh_done, 1)

            for par in range(2):
                split_hi(U, 16, par)
            second_key(1, 16, 0, first=True, wait=False)
            second_key(2, 16, 1, wait=False)
            with act.Fori(1, NKEY // 2 - 1) as i:
                for par in range(2):
                    second_key(2 * i + (par + 1), 16 * i + 16, par)
            for par in range(2):
                second_key(NKEY - 1 + par, 8 * NKEY, par, last=True)
            def sums_of_squares(src, dst):
                for n in range(NT):
                    act.activation(sq2[:, n], src[:, n], ACT.Square, accum_out=dst[:, n:n + 1]).then_inc(sumsq_done, 1)

            sq2 = probT[:, 512:512 + 2 * D].rearrange("p (n d) -> p n d", n=NT)
            act.wait_ge(peer_out, 4)
            sums_of_squares(resid, sumsq_f)
            act.wait_ge(x1_done, NT)
            act.wait_ge(sumsq_done, 8)
            sums_of_squares(resid, sumsq_x)
            copy_out_T(12, actT, C_PRE)

            def from2(g):
                act.wait_ge(g2_done, g2_no[g] + 1)
                return ps[:, g2_no[g] % 4, :]

            def out2(g, dst, func, **kw):
                act.activation(dst, from2(g), func, **kw).then_inc(g2_out, 1)

            def flat(ap):
                return ap.rearrange("p a b -> p (a b)")

            act.wait_ge(conv_zero, 1)
            for k, name in enumerate(("dnq", "dnk", "dnv")):
                for a in range(2):
                    f = 4 * k + 2 * a
                    act.activation(convin[:, f:f + 2, CONV - 1:], from2(f"{name}{a}").rearrange("p (f t) -> p f t", f=2), ACT.Copy).then_inc(g2_out, 1)
            act.wait_ge(g2_done, g2_no["ba"] + 1)
            act.activation(flat(ba), ps[:, g2_no["ba"] % 4, 0:2 * TH], ACT.Copy).then_inc(g2_out, 1)
            act.wait_ge(g2_out, g2_no["ba"] + 1)
            act.activation(beta, ba[:, :, 0:DH], ACT.Sigmoid).then_inc(beta_done, 1)
            for k in range(3):
                act.wait_ge(conv_done, k + 1)
                act.activation(flat(convT[:, 4 * k:4 * k + 4]), flat(convT[:, 4 * k:4 * k + 4]), ACT.Silu).then_inc(dnsilu_done, 1)
            act.wait_ge(dnsilu_done, 2)
            act.activation(flat(sqk), flat(convT[:, 0:2 * DH]), ACT.Square).then_inc(dnsq_done, 1)
            for a in range(NT):
                out2(f"dnz{a}", zdn[:, a], ACT.Silu)
            act.wait_ge(dz_done, 1)
            link(act.activation(flat(dsp), flat(dz), ACT.Abs))
            link(act.activation(flat(dsp), flat(dsp), ACT.Exp, scale=-1.0))
            act.activation(flat(dsp), flat(dsp), ACT.Ln, bias=1.0)
            act.activation(nega, a_log, ACT.Exp).then_inc(dln_done, 1)
            for a in range(NT):
                out2(f"gmu{a}", gu[:, a], ACT.Gelu_apprx_tanh)
            act.wait_ge(gcs_done, 2)
            act.activation(flat(egc), gcs[:, 0], ACT.Exp)
            act.activation(ekd, ekd, ACT.Exp).then_inc(egc_done, 1)
            for a in range(NT):
                out2(f"gmv{a}", gv2[:, a], ACT.Gelu_apprx_tanh)
            act.wait_ge(g2_out, g2_no["gmv1"] + 1)
            for n in range(NT):
                act.activation(prob[:, n * TILE:(n + 1) * TILE], gv2[:, n], ACT.Square, accum_out=sumsq_v[:, n:n + 1]).then_inc(gmv_sq, 1)
            for a in range(NT):
                out2(f"gmz{a}", gz[:, a], ACT.Silu)
            act.wait_ge(row_mm, 2)
            act.activation(flat(brow), ps[:, 6:8, :].rearrange("p b n -> p (b n)"), ACT.Copy).then_inc(brow_done, 1)
            act.wait_ge(dm_in, 1)
            act.activation(flat(qg), ps[:, 5, :], ACT.Exp)
            act.activation(flat(Dm), flat(Dm), ACT.Exp).then_inc(dm_done, 1)
            for a in range(2):
                out2(f"swq{a}", flat(swqT[:, 2 * a:2 * a + 2]), ACT.Copy)
            act.wait_ge(row_mm, 3)
            act.activation(flat(qrow), ps[:, 4:6, :].rearrange("p b n -> p (b n)"), ACT.Copy).then_inc(qrow_done, 1)
            out2("swkv", swkv, ACT.Copy)
            act.wait_ge(x0_tr, 1)
            act.activation(flat(X), ps[:, 4:6, :].rearrange("p b n -> p (b n)"), ACT.Copy).then_inc(x_done, 1)
            for l in range(1, LEVELS):
                for n in range(NT):
                    act.wait_ge(y_mm, NT * (l - 1) + n + 1)
                    act.activation(flat(Y[:, 4 * n:4 * n + 4]), ps[:, 4 + n, :], ACT.Copy).then_inc(y_out, 1)
                if l == 1:
                    for a in range(NT):
                        out2(f"swz{a}", swz[:, a], ACT.Silu)
                if l == 2:
                    for a in range(2):
                        out2(f"xmq{a}", flat(xmqT[:, 2 * a:2 * a + 2]), ACT.Copy)
                if l == 3:
                    for a in range(NT):
                        out2(f"xmz{a}", xmz[:, a], ACT.Silu)
            act.wait_ge(u_out_mm, 1)
            act.activation(flat(du), ps[:, 4:6, :].rearrange("p b n -> p (b n)"), ACT.Copy).then_inc(du_done, 1)
            act.activation(flat(wT), ps[:, 6, :], ACT.Copy).then_inc(wt_done, 1)
            act.wait_ge(s1_mm, 1)
            act.activation(flat(S1), ps[:, 7, :], ACT.Copy).then_inc(s1_done, 1)
            for n in range(NT):
                act.wait_ge(do_mm, n + 1)
                act.activation(prob[:, n * TILE:(n + 1) * TILE], ps[:, 4 + n, :], ACT.Square).then_inc(dosq_done, 1)
            off = 0
            for n in range(NT):
                width = (n + 1) * P
                pr = prob[:, off:off + SH * width].rearrange("p (h j) -> p h j", h=SH)
                prT = probT[:, off:off + SH * width]
                off += SH * width
                act.wait_ge(s_masked, n + 1)
                for h in range(SH):
                    act.activation(pr[:, h], pr[:, h], ACT.Exp, bias=snm[:, n, h:h + 1], accum_out=sden[:, n, h:h + 1])
                act.activation(ssk[:, n], ssk[:, n], ACT.Exp).then_inc(s_exp, 1)
                act.wait_ge(s_tr, n + 1)
                act.activation(prT, ps[:, (0 if n else 4):(4 if n else 6), :].rearrange("p b n -> p (b n)"), ACT.Copy).then_inc(s_trout, 1)
            for n in range(NT):
                pr = prob[:, n * 1024:(n + 1) * 1024].rearrange("p (h j) -> p h j", h=XH)
                prT = probT[:, n * 1024:(n + 1) * 1024]
                act.wait_ge(xs_max, n + 1)
                for h in range(XH):
                    ins = act.activation(pr[:, h], ps[:, 4 + 2 * n + h // 2, (h % 2) * T:(h % 2 + 1) * T], ACT.Exp, scale=HEAD ** -0.5,
                                         bias=xnm[:, n, h:h + 1], accum_out=xden[:, n, h:h + 1])
                ins.then_inc(xs_exp, 1)
            for n in range(NT):
                prT = probT[:, n * 1024:(n + 1) * 1024]
                act.wait_ge(xs_tr, n + 1)
                act.activation(prT, ps[:, 4 + 2 * n:6 + 2 * n, :].rearrange("p b n -> p (b n)"), ACT.Copy).then_inc(xs_trout, 1)
            for n in range(NBR):
                for k in range(4):
                    if n >= 2:
                        act.wait_ge(up_out, 4 * (n - 2) + k + 1)
                    out2(f"gate{n}{k // 2}{k % 2}", gsb[:, n % 2, k], ACT.Sigmoid)
            copy_out_T(16, actT)
            for n in range(NT):
                for h in range(2):
                    act.wait_ge(fin_mm, 2 * h + n + 1)
                    act.activation(outsb[:, n, h * TILE:(h + 1) * TILE], ps[:, 2 * h + n, :], ACT.Copy).then_inc(fin_copied, 1)
            act.wait_ge(fin_copied, 2 * NT)
            act.wait_ge(merged_done, 4)
            for n in range(NT):
                act.activation(merged[:, n], outsb[:, n], ACT.Square, accum_out=sumsq_p[:, n:n + 1]).then_inc(sumsq_done, 1)

        @block.vector
        def _(dve):
            steps = [0]

            def link(ins):
                steps[0] += 1
                ins.then_inc(dve_step, 1)
                dve.wait_ge(dve_step, steps[0])

            def mark(ins):
                steps[0] += 1
                ins.then_inc(dve_step, 1)

            def wait_marked():
                dve.wait_ge(dve_step, steps[0])

            mark(dve.memset(own, 0.0))
            mark(dve.memset(qd, 0.0))
            mark(dve.memset(kd, 0.0))
            dve.wait_ge(params_loaded, 80)
            logit = cols[:, C_LOG:C_LOG + 8].rearrange("p (a f) -> p a f", a=2)
            link(dve.tensor_tensor(lbm, logit[:, 0], logit[:, 1], ALU.max))
            dve.tensor_tensor(lbe, logit, bcast(lbm, 1, 2), ALU.subtract).then_inc(lb_in, 1)
            dve.wait_ge(rstd_done, 1)
            for n in range(NT):
                dve.tensor_scalar(scaled[:, n], resid[:, n], rstd[:, n:n + 1], None, ALU.mult).then_inc(scaled_done, 1)
            dve.wait_ge(params_loaded, 80)

            def copy_out_T(n_before, dst, gcol=None, first=4):
                for c in (0, 1, 4, 5):
                    dve.wait_ge(transposed, n_before + c // 2 + 1)
                    src = ps[:, 4 + c // 2, (c % 2) * T:(c % 2 + 1) * T]
                    if gcol is None:
                        ins = dve.tensor_copy(dst[:, c], src)
                    else:
                        ins = dve.tensor_scalar(dst[:, c], src, cols[:, gcol + c:gcol + c + 1], None, ALU.mult)
                    ins.then_inc(actT_done[1], 1)

            copy_out_T(0, actT, C_N1)
            dve.wait_ge(consts_made, 1)
            link(dve.tensor_tensor(xx, xi, xj, ALU.bitwise_xor))
            link(dve.tensor_copy(xf, xx))
            link(dve.tensor_tensor(xf, xf, upper[:], ALU.mult))
            for l in range(LEVELS + 1):
                mark(dve.tensor_scalar(ge[:, l], xf, float(1 << l), None, ALU.is_ge))
            wait_marked()
            dve.tensor_tensor(masks[:, 0:LEVELS], ge[:, 0:LEVELS], ge[:, 1:LEVELS + 1], ALU.subtract)
            dve.tensor_copy(masks[:, LEVELS], ident[:]).then_inc(masks_done, 1)
            dve.wait_ge(lb_exp, 1)
            link(dve.tensor_tensor(lbs, lbe[:, 0], lbe[:, 1], ALU.add))
            link(dve.reciprocal(lbr, lbs))
            link(dve.tensor_tensor(lb, lbe[:, 0], lbr, ALU.mult))
            link(dve.tensor_scalar(lb1, lb, -1.0, 1.0, ALU.mult, ALU.add))
            dve.wait_ge(group_out, group_no["hf1"] + 1)
            for f in range(4):
                mark(dve.tensor_scalar(gF[:, f], gF[:, f], lb1[:, f:f + 1], lb[:, f:f + 1], ALU.mult, ALU.add))
            wait_marked()
            dve.tensor_scalar(kF[:, 0:4], gF[:, 0:4], -1.0, 1.0, ALU.mult, ALU.add).then_inc(fgate_done, 1)
            dve.wait_ge(softplus_done, 1)
            link(dve.tensor_scalar(zg, zg, 0.0, 1.0 / GATE_NORM, ALU.min, ALU.mult))
            link(dve.scalar_tensor_tensor(gF[:, 4:6], zabs, -1.0 / GATE_NORM, zg, ALU.mult, ALU.add))
            dve.wait_ge(logf_done, 1)
            for f in range(NF):
                for n in range(NT):
                    tok = slice(n * P, n * P + P)
                    dve.tensor_tensor_scan(cum[:, f, tok], ones, gF[:, f, tok], 0.0, ALU.mult, ALU.add).then_inc(cum_done, 1)

            def keep(n, mask):
                for k in range(4):
                    tau, half = k // 2, k % 2
                    dve.wait_ge(lvl_scores, 2 * n + tau + 1)
                    if n:
                        dve.wait_ge(lvl_kept, 4 * (n - 1) + k + 1)
                    dve.copy_predicated(own[:, tau, 4 * half:4 * half + 4, :], bcast(mask, 1, 4),
                                        ps[:, 4 + k, :].rearrange("p (h i) -> p h i", h=4)).then_inc(lvl_kept, 1)

            for l in range(LEVELS + 1):
                m = 1 << l
                b = l % 2
                dve.wait_ge(lvl_decay, l + 1)
                if l >= 2:
                    dve.wait_ge(lvl_scores, 2 * l)
                half = lambda a: a.rearrange("p f (b two m) -> p (f b) two m", two=2, m=m)
                dve.tensor_tensor(half(qd[:, b])[:, :, 1, :], half(qF)[:, :, 1, :], half(dec[:, b])[:, :, 1, :], ALU.mult)
                dve.tensor_tensor(half(kd[:, b])[:, :, 0, :], half(kF)[:, :, 0, :], half(dec[:, b])[:, :, 0, :], ALU.mult).then_inc(lvl_scaled, 1)
                if l == 0:
                    dve.wait_ge(masks_done, 1)
                keep(l, masks[:, LEVELS if l == 0 else l - 1])
            dve.wait_ge(group_out, group_no["ggate1"] + 1)
            for n in range(NT):
                for a in range(2):
                    g = gate1[:, n, a * TILE:(a + 1) * TILE].rearrange("p (h v) -> p h v", h=4)
                    mark(dve.tensor_tensor(g, g, bcast(gnorm[:, a], 1, 4), ALU.mult))
            for n in range(NT):
                dve.wait_ge(osq_done, n + 1)
                dve.tensor_reduce(sumsq_o[:, n], sqtmp[:, n].rearrange("p (h v) -> p h v", h=HEADS1), AX.X, ALU.add).then_inc(osum_done, 1)
            wait_marked()
            for n in range(NT):
                dve.wait_ge(orstd_done, n + 1)
                for h in range(HEADS1):
                    dve.scalar_tensor_tensor(mixed[:, n, h * P:(h + 1) * P], ps[:, 4 + 2 * n + h // 4, (h % 4) * P:(h % 4 + 1) * P],
                                             rstd_o[:, n, h:h + 1], gate1[:, n, h * P:(h + 1) * P], ALU.mult, ALU.mult).then_inc(mixed_done, 1)
            copy_out_T(4, mixT)
            for k in range(4):
                half, n = k // 2, k % 2
                dve.wait_ge(wout_done, k + 1)
                part = resid[:, n, half * TILE:(half + 1) * TILE]
                dve.tensor_tensor(part, part, ps[:, k, :], ALU.add).then_inc(h_done, 1)
            dve.wait_ge(rstd_done, 2)
            for n in range(NT):
                dve.tensor_scalar(scaled_p[:, n], resid[:, n], rstd_h[:, n:n + 1], None, ALU.mult).then_inc(scaled_done, 1)
            copy_out_T(8, actT, C_N2)
            iota16 = iota[:, 0:TOP]

            def round_picks(r, a):
                for n in range(NT):
                    dst = chosen[:, n, a].rearrange("p (h k) -> p h k", h=PH)[:, 2 * r:2 * r + 2]
                    mark(dve.tensor_reduce(dst, pick[:, r % 2, a, 2 * n:2 * n + 2], AX.X, ALU.add))

            for r in range(ROUNDS):
                halves = [(ssb[:, n, 4 * r + 2 * h + a], srest[:, n, 2 * h + a], stop_[:, r, a, 2 * n + h], sidx[:, r, a, 2 * n + h])
                          for n in range(NT) for h in range(2) for a in range(2)]
                pairs = [(n, 2 * r + h, 2 * n + h) for n in range(NT) for h in range(2)]
                dve.wait_ge(sub_out, NT * r + NT)
                for score, rest, top, index in halves:
                    mark(dve.max(top[:, 0:8], score))
                wait_marked()
                for score, rest, top, index in halves:
                    mark(dve.max_index(index[:, 0:8], top[:, 0:8], score))
                    mark(dve.match_replace(rest, top[:, 0:8], score, NEG))
                wait_marked()
                for score, rest, top, index in halves:
                    mark(dve.max(top[:, 8:16], rest))
                wait_marked()
                for score, rest, top, index in halves:
                    mark(dve.max_index(index[:, 8:16], top[:, 8:16], rest))
                for at, a0, a1, nb in ((0, 0, FULL, TOP), (FULL * TOP, FULL, TOP, 4)):
                    mark(dve.tensor_tensor(cand[:, :, at:at + (a1 - a0) * nb].rearrange("p c (a b) -> p c a b", b=nb),
                                           bcast(stop_[:, r, 0, :, a0:a1], 3, nb), bcast(stop_[:, r, 1, :, 0:nb], 2, a1 - a0), ALU.add))
                wait_marked()
                mark(dve.tensor_copy(sidxf[:, r], sidx[:, r]))
                for n, h, k in pairs:
                    mark(dve.max(best[:, n, h, 0:8], cand[:, k]))
                wait_marked()
                for n, h, k in pairs:
                    mark(dve.max_index(pos[:, n, h, 0:8], best[:, n, h, 0:8], cand[:, k]))
                    mark(dve.match_replace(crest[:, k], best[:, n, h, 0:8], cand[:, k], NEG))
                wait_marked()
                for n, h, k in pairs:
                    mark(dve.max(best[:, n, h, 8:16], crest[:, k]))
                wait_marked()
                for n, h, k in pairs:
                    mark(dve.max_index(pos[:, n, h, 8:16], best[:, n, h, 8:16], crest[:, k]))
                if r:
                    for a in range(2):
                        dve.wait_ge(pick_kept, 2 * (r - 1) + a + 1)
                        round_picks(r - 1, a)
                wait_marked()
                places = pos[:, :, 2 * r:2 * r + 2].rearrange("p n h k -> p n (h k)")
                for k, shift in enumerate((0, 2, 4)):
                    mark(dve.tensor_scalar(posi[:, k], places, shift, None, ALU.logical_shift_right))
                wait_marked()
                link(dve.tensor_copy(posf, posi))
                p1, p4, p16 = (posf[:, k].rearrange("p n (h k) -> p (n h) k", h=2) for k in range(3))
                link(dve.scalar_tensor_tensor(place[:, 0], p4, float(FULL * TOP // 4 - FULL), p16, ALU.subtract, ALU.max))
                link(dve.tensor_scalar(p4, place[:, 0], 4.0, float(FULL * TOP - 4 * FULL), ALU.mult, ALU.add))
                link(dve.scalar_tensor_tensor(p4, place[:, 0], float(TOP), p4, ALU.mult, ALU.min))
                link(dve.tensor_tensor(place[:, 1], p1, p4, ALU.subtract))
                for a in range(2):
                    ins = dve.tensor_tensor(pick[:, r % 2, a], bcast(place[:, a], 3, TOP), bcast(bcast(iota16, 1, TOP), 1, 2 * NT), ALU.is_equal)
                    ins.then_inc(matched, 1)
            top1 = einv
            link(dve.tensor_copy(top1, best[:, :, :, 0]))
            dve.tensor_tensor(best, best, bcast(top1, 3, TOP), ALU.subtract).then_inc(soft_in, 1)
            dve.wait_ge(matched, 2 * ROUNDS)
            for a in range(2):
                view = pick[:, (ROUNDS - 1) % 2, a]
                mark(dve.tensor_tensor(view, view, round_keys(ROUNDS - 1, a), ALU.mult))
            wait_marked()
            for a in range(2):
                round_picks(ROUNDS - 1, a)
            dve.wait_ge(soft_exp, 1)
            link(dve.tensor_reduce(esum, best, AX.X, ALU.add))
            link(dve.reciprocal(einv, esum))
            for n in range(NT):
                dve.tensor_tensor(chosen[:, n, 2].rearrange("p (h k) -> p h k", h=PH), best[:, n], bcast(einv[:, n], 2, TOP), ALU.mult).then_inc(picks_done, 1)
            dve.wait_ge(x_split, 1)
            dve.tensor_tensor(xl[:], actT[:], xround, ALU.subtract).then_inc(x_split, 1)
            for n in range(NT):
                dve.wait_ge(pick_mm, n + 1)
                dve.tensor_copy(chosenT[:, :, n * P:(n + 1) * P], ps[:, n, 0:3 * P].rearrange("p (a t) -> p a t", a=3)).then_inc(pickT_done, 1)
            dve.wait_ge(pickT_done, 2)
            dve.tensor_scalar(minus_w, chosenT[:, 2], -1.0, None, ALU.mult).then_inc(pickT_done, 1)
            dve.wait_ge(pickT_done, 3)

            def onehots(at, at1, buf):
                dve.tensor_tensor(hotA[:, buf], bcast(iota, 1, GT), bcast(chosenT[:, 0, at], 2, NKEY), ALU.is_equal)
                dve.tensor_tensor(matchB[:, buf, 1:GT], bcast(iota, 1, GT - 1), bcast(chosenT[:, 1, at1], 2, NKEY), ALU.is_equal).then_inc(onehot_ready, 1)

            for b in range(GBUF):
                onehots(slice(b * GT, b * GT + GT), slice(b * GT + 1, b * GT + GT), b)
            with dve.Fori(1, NGRP // GBUF) as i:
                for b in range(GBUF):
                    dve.wait_ge(g_mm, GBUF * i + (b + 1 - GBUF))
                    onehots(bass.ds(i * (GBUF * GT) + b * GT, GT), bass.ds(i * (GBUF * GT) + (b * GT + 1), GT - 1), b)
            dve.wait_ge(g_out, NGRP)

            def split_lo(which, n, par):
                dve.wait_ge(hi_done[which], n)
                dve.tensor_tensor(lo[:, which, par], raw[:, which, par], hi[:, which, par].bitcast(F32), ALU.subtract).then_inc(lo_done[which], 1)

            def second_key(n, at, par, last=False):
                split_lo(V, n, par)
                dve.wait_ge(gelu_done, n)
                dve.tensor_tensor(act_j, act_j, G[:, :, at].rearrange("p t j -> p (t j)"), ALU.mult).then_inc(prod_done, 1)
                if not last:
                    split_lo(U, n + 2, par)
                dve.wait_ge(wh_done, n)
                dve.tensor_tensor(wl[:], act_j, wh[:].bitcast(F32), ALU.subtract).then_inc(wl_done, 1)

            for par in range(2):
                split_lo(U, par + 1, par)
            for n in range(2):
                second_key(n + 1, slice(n, n + 1), n)
            with dve.Fori(1, NKEY // 2 - 1) as i:
                for par in range(2):
                    second_key(2 * i + (par + 1), bass.ds(2 * i + par, 1), par)
            for n in range(NKEY - 2, NKEY):
                second_key(n + 1, slice(n, n + 1), n % 2, last=True)
            for k in range(4):
                dve.wait_ge(v_mm, NKEY)
                part = resid[:, k // 2, (k % 2) * TILE:(k % 2 + 1) * TILE]
                dve.tensor_tensor(part, part, ps[:, 4 + k, :], ALU.add).then_inc(peer_out, 1)
            dve.wait_ge(rows_loaded, 64)
            dve.wait_ge(rstd_done, 4)
            for n in range(NT):
                dve.scalar_tensor_tensor(resid[:, n], resid[:, n], rstd_f[:, n:n + 1], norm_f, ALU.mult, ALU.mult).then_inc(x1_done, 1)
            dve.wait_ge(rstd_done, 5)
            for n in range(NT):
                dve.tensor_scalar(scaled2[:, n], resid[:, n], rstd_x[:, n:n + 1], None, ALU.mult).then_inc(scaled_done, 1)
            link(dve.tensor_tensor(window[:, 0], ident[:], upper[:], ALU.subtract))
            link(dve.tensor_scalar(window[:, 0], window[:, 0], 1.0, None, ALU.add))
            mark(dve.tensor_scalar(window[:, 1], window[:, 0], -MASKED, MASKED, ALU.mult, ALU.add))
            wait_marked()
            mark(dve.tensor_scalar(window[:, 0], window[:, 0], MASKED, None, ALU.mult))
            mark(dve.tensor_tensor(wsT, wsT, bcast(upper[:], 1, 4), ALU.mult))
            copy_out_T(12, actT, C_PRE)
            dve.wait_ge(transposed, 16)
            dve.memset(convin[:, :, 0:CONV - 1], 0.0).then_inc(conv_zero, 1)
            for k, name in enumerate(("dnq", "dnk", "dnv")):
                dve.wait_ge(g2_out, g2_no[name + "1"] + 1)
                for tap in reversed(range(CONV)):
                    for f in range(4 * k, 4 * k + 4):
                        w = cols[:, C_CONV + tap * 12 + f:C_CONV + tap * 12 + f + 1]
                        src = convin[:, f, tap:tap + T]
                        if tap == CONV - 1:
                            mark(dve.tensor_scalar(convT[:, f], src, w, None, ALU.mult))
                        elif tap:
                            mark(dve.scalar_tensor_tensor(convT[:, f], src, w, convT[:, f], ALU.mult, ALU.add))
                        else:
                            ins = dve.scalar_tensor_tensor(convT[:, f], src, w, convT[:, f], ALU.mult, ALU.add)
                    wait_marked()
                ins.then_inc(conv_done, 1)
            dve.wait_ge(g2_out, g2_no["ba"] + 1)
            dve.tensor_tensor(dz, ba[:, :, DH:2 * DH], bcast(dt_bias, 1, NT), ALU.add).then_inc(dz_done, 1)
            dve.wait_ge(ss_mm, 1)
            dve.tensor_scalar(rin.rearrange("p n f -> p (n f)"), ps[:, 4, 0:2 * TH], EPS, None, ALU.add).then_inc(rin_done, 1)
            dve.wait_ge(dln_done, 1)
            link(dve.scalar_tensor_tensor(dsp, dz, 0.0, dsp, ALU.max, ALU.add))
            dve.scalar_tensor_tensor(dg, dsp, -1.0, bcast(nega, 1, NT), ALU.mult, ALU.mult).then_inc(dg_done, 1)
            dve.wait_ge(rr_done, 1)
            dve.wait_ge(beta_done, 1)
            mark(dve.tensor_tensor(brk, beta, rr[:, :, DH:2 * DH], ALU.mult))
            mark(dve.tensor_scalar(rqs, rr[:, :, 0:DH], HEAD ** -0.5, None, ALU.mult))
            dve.wait_ge(dg_done, 1)
            wait_marked()
            for a, v in enumerate((dg, brk, rqs)):
                ins = dve.tensor_copy(rep[:, a], bcast(v.rearrange("p n h -> p (n h)"), 2, P))
            ins.then_inc(rep_done, 1)
            dve.wait_ge(gc_mm, 1)
            dve.tensor_copy(gcs, ps[:, 5, 0:2 * TH].rearrange("p (a h) -> p a h", a=2)).then_inc(gcs_done, 1)
            dve.wait_ge(gcs_done, 1)
            dve.tensor_tensor(ekd, gcs[:, 1, 0:DH], gcs[:, 0, 0:DH], ALU.subtract).then_inc(gcs_done, 1)
            dve.wait_ge(row_mm, 1)
            for th in range(TH):
                ins = dve.tensor_scalar(Dm[:, th], ps[:, 4 + th // DH, (th % DH) * P:(th % DH + 1) * P], gcs[:, 0, th:th + 1], 0.0, ALU.subtract, ALU.min)
            ins.then_inc(dm_in, 1)
            dve.wait_ge(egc_done, 1)
            mark(dve.tensor_tensor(kbf, brk, egc, ALU.mult))
            mark(dve.tensor_tensor(ekd, ekd, rr[:, 0, DH:2 * DH], ALU.mult))
            wait_marked()
            dve.wait_ge(gmv_rstd, 1)
            for n in range(NT):
                dve.scalar_tensor_tensor(gv2[:, n], gv2[:, n], rstd_v[:, n:n + 1], gm_gain, ALU.mult, ALU.mult).then_inc(gmv_done, 1)

            def head_cols(k):
                return slice((k % DH) * P, (k % DH + 1) * P)

            dve.wait_ge(dm_done, 1)
            dve.wait_ge(kk_mm, 1)
            for th in range(TH):
                mark(dve.scalar_tensor_tensor(LT[:, th], ps[:, 6 + th // DH, head_cols(th)], rr[:, th // DH, DH + th % DH:DH + th % DH + 1], Dm[:, th], ALU.mult, ALU.mult))
            dve.wait_ge(brow_done, 1)
            wait_marked()
            dve.tensor_tensor(LT, LT, brow, ALU.mult).then_inc(lt_done, 1)
            dve.wait_ge(lt_done, 1)
            link(dve.tensor_tensor(BT, LT, bcast(masks[:, 0], 1, TH), ALU.mult))
            dve.tensor_tensor(Z, bcast(ident[:], 1, TH), BT, ALU.subtract).then_inc(z0_done, 1)
            dve.wait_ge(kv_tr, 1)
            for h in range(DH):
                dve.tensor_scalar(kdl[:, h], ps[:, 6, head_cols(h)], ekd[:, h:h + 1], None, ALU.mult)
            for th in range(TH):
                n, h = th // DH, th % DH
                ins = dve.tensor_scalar(kbg[:, th], ps[:, 6 + n, head_cols(th)], kbf[:, n, h:h + 1], None, ALU.mult)
            ins.then_inc(kv_out, 1)
            dve.wait_ge(kv_tr, 2)
            for th in range(TH):
                n, h = th // DH, th % DH
                ins = dve.tensor_scalar(vb[:, th], ps[:, 6 + n, head_cols(th)], beta[:, n, h:h + 1], None, ALU.mult)
            ins.then_inc(kv_out, 1)
            dve.wait_ge(qk_mm, 1)
            for th in range(TH):
                mark(dve.scalar_tensor_tensor(AQ[:, th], ps[:, 6 + th // DH, head_cols(th)], rr[:, th // DH, DH + th % DH:DH + th % DH + 1], Dm[:, th], ALU.mult, ALU.mult))
            dve.wait_ge(qrow_done, 1)
            wait_marked()
            link(dve.tensor_tensor(AQ, AQ, qrow, ALU.mult))
            dve.tensor_tensor(AQ, AQ, bcast(upper[:], 1, TH), ALU.mult).then_inc(aq_done, 1)
            link(dve.tensor_tensor(qg, qg, qrow[:, DH:TH], ALU.mult))
            dve.tensor_tensor(qg, qg, convT[:, 0:DH, P:T], ALU.mult).then_inc(qg_done, 1)
            for l in range(1, LEVELS):
                if l >= 2:
                    dve.wait_ge(y_mm, NT * (l - 1))
                else:
                    dve.wait_ge(z0_done, 1)
                dve.tensor_tensor(BT, LT, bcast(masks[:, l], 1, TH), ALU.mult).then_inc(bt_done, 1)
                for n in range(NT):
                    part = slice(DH * n, DH * n + DH)
                    dve.wait_ge(pz_mm, NT * (l - 1) + n + 1)
                    if l < LEVELS - 1:
                        dve.tensor_tensor(X[:, part], X[:, part], ps[:, 6 + n, :].rearrange("p (h c) -> p h c", h=DH), ALU.subtract).then_inc(x_done, 1)
                    dve.tensor_tensor(Z[:, part], Z[:, part], ps[:, 4 + n, :].rearrange("p (h c) -> p h c", h=DH), ALU.subtract).then_inc(z_done, 1)
            dve.wait_ge(ws_mm, 1)
            dve.wait_ge(du_done, 1)
            dve.tensor_tensor(vnew, du[:, DH:TH], ps[:, 6, :].rearrange("p (h c) -> p h c", h=DH), ALU.subtract).then_inc(vnew_done, 1)
            for n in range(NT):
                dve.wait_ge(gm_mm, n + 1)
                for g in range(4):
                    part = gu[:, n, g * P:(g + 1) * P]
                    mark(dve.scalar_tensor_tensor(part, ps[:, 2 + n, g * P:(g + 1) * P], cols[:, C_SB + g:C_SB + g + 1], part, ALU.add, ALU.mult))
                wait_marked()
                dve.tensor_tensor(gu[:, n], gu[:, n], gz[:, n], ALU.mult).then_inc(y_done[1], 1)
            for n in range(NT):
                zz = zdn[:, n].rearrange("p (h v) -> p h v", h=DH)
                mark(dve.tensor_tensor(zz, zz, bcast(dn_gain, 1, DH), ALU.mult))
            for n in range(NT):
                dve.wait_ge(dosq_done, n + 1)
                dve.tensor_reduce(sumsq_a[:, n], prob[:, n * TILE:(n + 1) * TILE].rearrange("p (h v) -> p h v", h=DH), AX.X, ALU.add).then_inc(dosum_done, 1)
            wait_marked()
            for n in range(NT):
                dve.wait_ge(dors_done, n + 1)
                for h in range(DH):
                    part = zdn[:, n, h * P:(h + 1) * P]
                    ins = dve.scalar_tensor_tensor(part, ps[:, 4 + n, h * P:(h + 1) * P], rstd_a[:, n, h:h + 1], part, ALU.mult, ALU.mult)
                ins.then_inc(y_done[0], 1)
            off = 0
            for n in range(NT):
                width = (n + 1) * P
                pr = prob[:, off:off + SH * width].rearrange("p (h j) -> p h j", h=SH)
                off += SH * width
                banks, per = ((4, 4), (0, 2))[n]
                add = window[:, 1] if n == 0 else window.rearrange("p a j -> p (a j)")
                dve.wait_ge(ss_mm2, n + 1)
                for b in range(SH // per):
                    mark(dve.scalar_tensor_tensor(pr[:, per * b:per * b + per], ps[:, banks + b, :].rearrange("p (h j) -> p h j", h=per), SHD ** -0.5,
                                                  bcast(add, 1, per), ALU.mult, ALU.add))
                wait_marked()
                link(dve.tensor_reduce(smax[:, n], pr, AX.X, ALU.max))
                link(dve.tensor_tensor(smax[:, n], smax[:, n], sinks, ALU.max))
                mark(dve.tensor_tensor(ssk[:, n], sinks, smax[:, n], ALU.subtract))
                dve.tensor_scalar(snm[:, n], smax[:, n], -1.0, None, ALU.mult).then_inc(s_masked, 1)
            for n in range(NT):
                dve.wait_ge(s_exp, n + 1)
                link(dve.tensor_tensor(sden[:, n], sden[:, n], ssk[:, n], ALU.add))
                link(dve.reciprocal(srec[:, n], sden[:, n]))
                dve.wait_ge(so_mm, n + 1)
                for h in range(SH):
                    part = swz[:, n, h * SHD:(h + 1) * SHD]
                    ins = dve.scalar_tensor_tensor(part, ps[:, 6 + n, h * SHD:(h + 1) * SHD], srec[:, n, h:h + 1], part, ALU.mult, ALU.mult)
                ins.then_inc(y_done[2], 1)
            for n in range(NT):
                dve.wait_ge(xs_mm, n + 1)
                link(dve.tensor_reduce(xmax[:, n], ps[:, 4 + 2 * n:6 + 2 * n, :].rearrange("p b (h j) -> p (b h) j", h=2), AX.X, ALU.max))
                dve.tensor_scalar(xnm[:, n], xmax[:, n], -(HEAD ** -0.5), None, ALU.mult).then_inc(xs_max, 1)
            for n in range(NT):
                dve.wait_ge(xs_exp, n + 1)
                link(dve.reciprocal(xrec[:, n], xden[:, n]))
                dve.wait_ge(xo_mm, n + 1)
                for h in range(XH):
                    part = xmz[:, n, h * HEAD:(h + 1) * HEAD]
                    ins = dve.scalar_tensor_tensor(part, ps[:, n, h * HEAD:(h + 1) * HEAD], xrec[:, n, h:h + 1], part, ALU.mult, ALU.mult)
                ins.then_inc(y_done[3], 1)
            for n in range(NBR):
                dve.wait_ge(yT_mm, n + 1)
                b = 4 + 2 * (n % 2)
                dve.tensor_copy(yT[:, 4 * n:4 * n + 4].rearrange("p c t -> p (c t)"), ps[:, b:b + 2, :].rearrange("p b n -> p (b n)")).then_inc(yT_done, 1)
            for n in range(NBR):
                for k in range(4):
                    dve.wait_ge(up_mm, 4 * n + k + 1)
                    dve.wait_ge(g2_out, g2_no[f"gate{n}{k // 2}{k % 2}"] + 1)
                    part = merged[:, k % 2, (k // 2) * TILE:(k // 2 + 1) * TILE]
                    g = gsb[:, n % 2, k]
                    if n == 0:
                        dve.tensor_tensor(part, g, ps[:, 4 + k, :], ALU.mult).then_inc(up_out, 1)
                    else:
                        link(dve.tensor_tensor(g, g, ps[:, 4 + k, :], ALU.mult))
                        dve.wait_ge(up_out, 4 * (n - 1) + k + 1)
                        dve.tensor_tensor(part, part, g, ALU.add).then_inc(merged_done if n == NBR - 1 else up_out, 1)
            copy_out_T(16, actT)
            dve.wait_ge(rstd_done, 6)
            dve.wait_ge(rows_loaded, 80)
            for n in range(NT):
                mark(dve.scalar_tensor_tensor(outsb[:, n], outsb[:, n], rstd_p[:, n:n + 1], norm_post, ALU.mult, ALU.mult))
                wait_marked()
                dve.tensor_tensor(outsb[:, n], outsb[:, n], resid[:, n], ALU.add).then_inc(out_done, 1)

        @block.tensor
        def _(pe):
            def transpose_all(src, waits, dst_free):
                waits()
                dst_free()
                for c in range(KC):
                    for n in range(NT):
                        ins = pe.transpose(ps[:, 4 + c // 2, (c % 2) * T + n * P:(c % 2) * T + (n + 1) * P],
                                           src[:, n, c * P:(c + 1) * P], ident[:])
                    if c % 2:
                        ins.then_inc(transposed, 1)

            def actT_ready(n):
                pe.wait_ge(actT_done[0], 4 * n)
                pe.wait_ge(actT_done[1], 4 * n)

            def need(name):
                pe.wait_ge(tile_loaded[slot(name)], 16 * (tile_no[name] // RING + 1))

            def bank_free(g):
                k = group_no[g]
                if k >= 4:
                    pe.wait_ge(group_out, k - 3)

            def features(name, xT, subs):
                need(name)
                w = tile_view(name)
                for s in subs:
                    g = f"{name}{s}"
                    bank_free(g)
                    for a in range(2):
                        f0 = (2 * s + a) * P
                        for c in range(KC):
                            ins = pe.matmul(ps[:, gbank(g), a * T:(a + 1) * T], w[:, c, f0:f0 + P], xT[:, c, :], start=(c == 0), stop=(c == KC - 1))
                    ins.then_inc(group_done, 1)

            def tokens(name, xT):
                need(name)
                w = tile_view(name)
                for n in range(NT):
                    g = f"{name}{n}"
                    bank_free(g)
                    for c in range(KC):
                        ins = pe.matmul(ps[:, gbank(g), :], xT[:, c, n * P:(n + 1) * P], w[:, c, :], start=(c == 0), stop=(c == KC - 1))
                    ins.then_inc(group_done, 1)

            pe.wait_ge(consts_made, 1)
            transpose_all(scaled, lambda: pe.wait_ge(scaled_done, 2), lambda: None)
            actT_ready(1)
            features("hq", actT, (0, 1))
            features("hf", actT, (0, 1))
            features("gqk", actT, (0, 1))
            bank_free("glow")
            for c in range(KC):
                ins = pe.matmul(ps[0:RANK, gbank("glow"), 0:T], glow_w[:, c], actT[:, c], start=(c == 0), stop=(c == KC - 1))
            ins.then_inc(group_done, 1)
            pe.wait_ge(group_out, group_no["glow"] + 1)
            for a in range(2):
                ins = pe.matmul(ps[:, 7, a * T:(a + 1) * T], gate_up[:, a], glowT[0:RANK], start=True, stop=True)
            ins.then_inc(gate_mm, 1)
            for name in ("hi", "gv"):
                tokens(name, actT)

            def scores(n, q, k):
                for tau in range(NT):
                    if n:
                        pe.wait_ge(lvl_kept, 4 * (n - 1) + 2 * tau + 2)
                    tok = slice(tau * P, tau * P + P)
                    for h in range(HEADS1):
                        f, rows = head_rows(h)
                        ins = pe.matmul(ps[:, 4 + 2 * tau + PLACE[h] // 4, (PLACE[h] % 4) * P:(PLACE[h] % 4 + 1) * P], k[rows, f, tok], q[rows, f, tok], start=True, stop=True)
                    ins.then_inc(lvl_scores, 1)

            pe.wait_ge(softplus_done, 1)
            pe.wait_ge(fgate_done, 1)
            scores(0, qF, kF)
            for l in range(LEVELS):
                if l in (1, 3):
                    tokens("hgate" if l == 1 else "ggate", actT)
                pe.wait_ge(lvl_scaled, l + 1)
                scores(l + 1, qd[:, l % 2], kd[:, l % 2])
            pe.wait_ge(lvl_scaled, LEVELS + 1)
            pe.wait_ge(lvl_kept, 4 * LEVELS + 2)
            for h in range(HEADS1):
                f, rows = head_rows(h)
                ins = pe.matmul(ps[:, 4 + PLACE[h] // 4, (PLACE[h] % 4) * P:(PLACE[h] % 4 + 1) * P], kd[rows, 1, f, 0:P], qd[rows, 1, f, P:T], start=True, stop=True)
            ins.then_inc(lvl_scores, 1)
            pe.wait_ge(cross_out, 1)
            pe.wait_ge(lvl_kept, 4 * (LEVELS + 1))
            for n in range(NT):
                for h in range(HEADS1):
                    o = ps[:, 4 + 2 * n + h // 4, (h % 4) * P:(h % 4 + 1) * P]
                    ins = pe.matmul(o, own[:, n, PLACE[h]], vtok[:, n, h * P:(h + 1) * P], start=True, stop=(n == 0))
                    if n:
                        ins = pe.matmul(o, cross[:, PLACE[h]], vtok[:, 0, h * P:(h + 1) * P], start=False, stop=True)
                ins.then_inc(o_done, 1)
            transpose_all(mixed, lambda: pe.wait_ge(mixed_done, 2 * HEADS1), lambda: None)
            actT_ready(2)
            for k in range(4):
                half, n = k // 2, k % 2
                name = f"wo{half}"
                need(name)
                for c in range(KC):
                    ins = pe.matmul(ps[:, k, :], mixT[:, c, n * P:(n + 1) * P], tile_view(name)[:, c, :], start=(c == 0), stop=(c == KC - 1))
                ins.then_inc(wout_done, 1)
            transpose_all(scaled_p, lambda: pe.wait_ge(scaled_done, 4), lambda: None)
            actT_ready(3)
            pe.wait_ge(h_done, 4)

            def key_scores(r):
                pe.wait_ge(group_out, group_no[f"wq{r}1"] + 1)
                for n in range(NT):
                    k = NT * r + n
                    if k >= 4:
                        pe.wait_ge(sub_out, k - 3)
                    for a in range(4):
                        ins = pe.matmul(ps[:, 4 + k % 4, a * P:(a + 1) * P], qT[:, 4 * r + a, n * P:(n + 1) * P], keysT[:, 4 * r + a], start=True, stop=True)
                    ins.then_inc(sub_done, 1)

            for r in range(ROUNDS):
                features(f"wq{r}", actT, (0,))
                if r == 1:
                    pe.wait_ge(keys_loaded, 16)
                if r:
                    key_scores(r - 1)
                features(f"wq{r}", actT, (1,))
            key_scores(ROUNDS - 1)
            pe.wait_ge(mem_scaled, NT)
            pe.wait_ge(group_out, group_no["wq31"] + 1)
            for c in range(KC):
                for n in range(NT):
                    ins = pe.transpose(ps[:, c // 2, (c % 2) * T + n * P:(c % 2) * T + (n + 1) * P], memtok[:, n, c * P:(c + 1) * P], ident[:])
                if c % 2:
                    ins.then_inc(mem_T, 1)
            pe.wait_ge(memT_done, KC)
            features("mk", memT, (0, 1))
            tokens("mv", memT)
            pe.wait_ge(group_out, group_no["mv1"] + 1)
            for n in range(NT):
                pe.wait_ge(picks_done, n + 1)
                for a in range(3):
                    ins = pe.transpose(ps[:, n, a * P:(a + 1) * P], chosen[:, n, a], ident[:])
                ins.then_inc(pick_mm, 1)
            pe.wait_ge(pickT_done, 2)

            def weights_of(n, buf):
                pe.wait_ge(onehot_ready, n)
                pe.wait_ge(onehot_by_act, n)
                pe.wait_ge(onehot_weighted, n)
                for k in range(GT):
                    ins = pe.matmul(ps[:, buf, k * P:(k + 1) * P], hotA[:, buf, k], hotB[:, buf, k], start=True, stop=True)
                ins.then_inc(g_mm, 1)

            for b in range(GBUF):
                weights_of(b + 1, b)
            with pe.Fori(1, NGRP // GBUF) as i:
                for b in range(GBUF):
                    pe.wait_ge(g_out, GBUF * i + (b + 1 - GBUF))
                    weights_of(GBUF * i + (b + 1), b)

            u_hi, u_lo = (v[:, U].rearrange("p s (c i) -> p s c i", c=KC) for v in (hi, lo))

            def u_pass(n, par):
                pe.wait_ge(lo_done[U], n)
                o = ps[:, par, 0:T]
                for c in range(KC):
                    pe.matmul(o, u_hi[:, par, c], xh[:, c], start=(c == 0), stop=False)
                    pe.matmul(o, u_hi[:, par, c], xl[:, c], start=False, stop=False)
                    ins = pe.matmul(o, u_lo[:, par, c], xh[:, c], start=False, stop=(c == KC - 1))
                ins.then_inc(u_mm, 1)

            def v_pass(n, par, first=False, last=False):
                pe.wait_ge(lo_done[V], n)
                pe.wait_ge(wl_done, n)
                for tau in range(NT):
                    tok = slice(tau * P, (tau + 1) * P)
                    for k, (w, v) in enumerate(((wh, hi), (wh, lo), (wl, hi))):
                        for half in range(2):
                            ins = pe.matmul(ps[:, 4 + 2 * tau + half, :], w[:, tok], v[:, V, par, half * TILE:(half + 1) * TILE],
                                            start=(first and k == 0), stop=(last and k == 2))
                ins.then_inc(v_mm, 1)

            pe.wait_ge(g_out, NGRP)
            pe.wait_ge(x_split, 3)
            u_pass(1, 0)
            u_pass(2, 1)
            v_pass(1, 0, first=True)
            with pe.Fori(1, NKEY // 2) as i:
                pe.wait_ge(gelu_done, 2 * i - 1)
                u_pass(2 * i + 1, 0)
                v_pass(2 * i, 1)
                pe.wait_ge(gelu_done, 2 * i)
                u_pass(2 * i + 2, 1)
                v_pass(2 * i + 1, 0)
            v_pass(NKEY, 1, last=True)
            transpose_all(scaled2, lambda: pe.wait_ge(scaled_done, 6), lambda: pe.wait_ge(peer_out, 4))
            actT_ready(4)

            def need2(name):
                k = tile2_no[name]
                pe.wait_ge(tile_loaded[k % RING], 16 * (loads1[k % RING] + k // RING + 1))
                return ring[:, k % RING, :]

            def free2(g):
                k = g2_no[g]
                if k >= 4:
                    pe.wait_ge(g2_out, k - 3)
                return ps[:, k % 4, :]

            def features2(name):
                w = need2(name).rearrange("p (c n) -> p c n", c=KC)
                for s in range(2):
                    o = free2(f"{name}{s}")
                    for a in range(2):
                        for c in range(KC):
                            ins = pe.matmul(o[:, a * T:(a + 1) * T], w[:, c, (2 * s + a) * P:(2 * s + a + 1) * P], actT[:, c], start=(c == 0), stop=(c == KC - 1))
                    ins.then_inc(g2_done, 1)

            def tokens2(name, suffix=""):
                w = need2(name).rearrange("p (c n) -> p c n", c=KC)
                for n in range(NT):
                    o = free2(f"{name}{n}")
                    for c in range(KC):
                        ins = pe.matmul(o, actT[:, c, n * P:(n + 1) * P], w[:, c], start=(c == 0), stop=(c == KC - 1))
                    ins.then_inc(g2_done, 1)

            for name in ("dnq", "dnk", "dnv"):
                features2(name)
            pe.wait_ge(rows_loaded, 64)
            o = free2("ba")
            for n in range(NT):
                for c in range(KC):
                    ins = pe.matmul(o[:, n * 2 * DH:(n + 1) * 2 * DH], actT[:, c, n * P:(n + 1) * P], ba_w[:, c], start=(c == 0), stop=(c == KC - 1))
            ins.then_inc(g2_done, 1)
            tokens2("dnz")
            tokens2("gmu")
            pe.wait_ge(consts_made, 2)
            pe.wait_ge(dnsq_done, 1)
            for n in range(NT):
                for f in range(2 * DH):
                    ins = pe.matmul(ps[:, 4, n * 2 * DH + f:n * 2 * DH + f + 1], sqk[:, f, n * P:(n + 1) * P], ones[:, 0:1], start=True, stop=True)
            ins.then_inc(ss_mm, 1)
            pe.wait_ge(dg_done, 1)
            pe.matmul(ps[:, 5, 0:TH], upper[:], dg.rearrange("p n h -> p (n h)"), start=True, stop=True)
            pe.matmul(ps[:, 5, TH:2 * TH], ones, dg.rearrange("p n h -> p (n h)"), start=True, stop=True).then_inc(gc_mm, 1)
            tokens2("gmv")

            def th_out(b, th):
                return ps[:, b + th // DH, (th % DH) * P:(th % DH + 1) * P]

            def repeat_row(b, a, m):
                for th in range(TH):
                    ins = pe.matmul(th_out(b, th), rep[:, a, th], m, start=True, stop=True)
                ins.then_inc(row_mm, 1)

            pe.wait_ge(rep_done, 1)
            pe.wait_ge(rin_done, 1)
            pe.wait_ge(gcs_done, 1)
            repeat_row(4, 0, upper[:])
            repeat_row(6, 1, ident[:])
            tokens2("gmz")
            pe.wait_ge(brow_done, 1)
            pe.wait_ge(dnsilu_done, 3)
            for th in range(TH):
                n, h = th // DH, th % DH
                k = convT[:, DH + h, n * P:(n + 1) * P]
                ins = pe.matmul(th_out(6, th), k, k, start=True, stop=True)
            ins.then_inc(kk_mm, 1)
            pe.wait_ge(dm_done, 1)
            repeat_row(4, 2, ident[:])
            features2("swq")
            pe.wait_ge(lt_done, 1)
            for a in range(2):
                if a:
                    pe.wait_ge(kv_out, 1)
                for th in range(TH):
                    n, h = th // DH, th % DH
                    ins = pe.transpose(th_out(6, th), convT[:, (1 + a) * DH + h, n * P:(n + 1) * P], ident[:])
                ins.then_inc(kv_tr, 1)
            w = need2("swkv")[:, 0:KC * T].rearrange("p (c n) -> p c n", c=KC)
            o = free2("swkv")
            for c in range(KC):
                pe.matmul(o[:, 0:T], w[:, c, 0:P], actT[:, c], start=(c == 0), stop=(c == KC - 1))
            for n in range(NT):
                for c in range(KC):
                    ins = pe.matmul(o[:, T + n * P:T + (n + 1) * P], actT[:, c, n * P:(n + 1) * P], w[:, c, P:2 * P], start=(c == 0), stop=(c == KC - 1))
            ins.then_inc(g2_done, 1)
            pe.wait_ge(kv_out, 2)
            for th in range(TH):
                n, h = th // DH, th % DH
                ins = pe.matmul(th_out(6, th), convT[:, DH + h, n * P:(n + 1) * P], convT[:, h, n * P:(n + 1) * P], start=True, stop=True)
            ins.then_inc(qk_mm, 1)
            pe.wait_ge(z0_done, 1)
            pe.wait_ge(qrow_done, 1)
            for th in range(TH):
                ins = pe.transpose(th_out(4, th), Z[:, th], ident[:])
            ins.then_inc(x0_tr, 1)
            for l in range(1, LEVELS):
                pe.wait_ge(bt_done, l)
                for n in range(NT):
                    pe.wait_ge(x_done, NT * (l - 1) + n if l > 1 else 1)
                    if l > 1:
                        pe.wait_ge(x_done, 1 + NT * (l - 2) + n + 1)
                        pe.wait_ge(z_done, NT * (l - 2) + n + 1)
                    for th in range(DH * n, DH * n + DH):
                        ins = pe.matmul(th_out(4, th), BT[:, th], X[:, th], start=True, stop=True)
                    ins.then_inc(y_mm, 1)
                if l == 1:
                    pe.wait_ge(aq_done, 1)
                for n in range(NT):
                    pe.wait_ge(y_out, NT * (l - 1) + n + 1)
                    if l < LEVELS - 1:
                        for th in range(DH * n, DH * n + DH):
                            ins = pe.matmul(th_out(6, th), Z[:, th], Y[:, th], start=True, stop=True)
                    for th in range(DH * n, DH * n + DH):
                        ins = pe.matmul(th_out(4, th), Y[:, th], Z[:, th], start=True, stop=True)
                    ins.then_inc(pz_mm, 1)
                if l == 1:
                    tokens2("swz")
                if l == 2:
                    features2("xmq")
                if l == 3:
                    tokens2("xmz")
            pe.wait_ge(z_done, NT * (LEVELS - 1))
            pe.wait_ge(kv_out, 2)
            for th in range(TH):
                pe.matmul(th_out(4, th), Z[:, th], vb[:, th], start=True, stop=True)
            for h in range(DH):
                ins = pe.matmul(ps[:, 6, h * P:(h + 1) * P], kbg[:, DH + h], Z[:, DH + h], start=True, stop=True)
            ins.then_inc(u_out_mm, 1)
            pe.wait_ge(du_done, 1)
            for h in range(DH):
                ins = pe.matmul(ps[:, 7, h * P:(h + 1) * P], kdl[:, h], du[:, h], start=True, stop=True)
            ins.then_inc(s1_mm, 1)
            pe.wait_ge(s1_done, 1)
            pe.wait_ge(wt_done, 1)
            for h in range(DH):
                ins = pe.matmul(ps[:, 6, h * P:(h + 1) * P], wT[:, h], S1[:, h], start=True, stop=True)
            ins.then_inc(ws_mm, 1)
            pe.wait_ge(gmv_done, NT)
            pe.wait_ge(g2_out, g2_no["xmz1"] + 1)
            for n in range(NT):
                for g in range(4):
                    ins = pe.matmul(ps[:, 2 + n, g * P:(g + 1) * P], wsT[:, g], gv2[:, n, g * P:(g + 1) * P], start=True, stop=True)
                ins.then_inc(gm_mm, 1)
            pe.wait_ge(aq_done, 1)
            for h in range(DH):
                ins = pe.matmul(th_out(4, h), AQ[:, h], du[:, h], start=True, stop=True)
            ins.then_inc(do_mm, 1)
            pe.wait_ge(qg_done, 1)
            pe.wait_ge(vnew_done, 1)
            for h in range(DH):
                pe.matmul(th_out(4, DH + h), qg[:, h], S1[:, h], start=True, stop=False)
                ins = pe.matmul(th_out(4, DH + h), AQ[:, DH + h], vnew[:, h], start=False, stop=True)
            ins.then_inc(do_mm, 1)
            pe.wait_ge(y_done[0], NT)
            pe.wait_ge(y_done[1], NT)
            for n in range(NT):
                banks, per = ((4, 4), (0, 2))[n]
                width = (n + 1) * P
                for h in range(SH):
                    half = slice(SHD * (h // 4), SHD * (h // 4) + SHD)
                    ins = pe.matmul(ps[:, banks + h // per, (h % per) * width:(h % per + 1) * width], swqT[half, h % 4, n * P:(n + 1) * P], swkT[half, 0:width],
                                    start=True, stop=True)
                ins.then_inc(ss_mm2, 1)
            off = 0
            for n in range(NT):
                width = (n + 1) * P
                pr = prob[:, off:off + SH * width].rearrange("p (h j) -> p h j", h=SH)
                off += SH * width
                pe.wait_ge(s_exp, n + 1)
                if n:
                    pe.wait_ge(s_masked, 2)
                for h in range(SH):
                    for b in range(n + 1):
                        at = (h * (n + 1) + b) * P
                        ins = pe.transpose(ps[:, (0 if n else 4) + at // TILE, at % TILE:at % TILE + P], pr[:, h, b * P:(b + 1) * P], ident[:])
                ins.then_inc(s_tr, 1)
            off = 0
            for n in range(NT):
                width = (n + 1) * P
                prT = probT[:, off:off + SH * width].rearrange("p (h b i) -> p h b i", h=SH, b=n + 1)
                off += SH * width
                pe.wait_ge(s_trout, n + 1)
                for h in range(SH):
                    for b in range(n + 1):
                        ins = pe.matmul(ps[:, 6 + n, h * SHD:(h + 1) * SHD], prT[:, h, b], swv[:, b, SHD * (h // 4):SHD * (h // 4) + SHD], start=(b == 0), stop=(b == n))
                ins.then_inc(so_mm, 1)
            pe.wait_ge(mkv_loaded, 16)
            for n in range(NT):
                if n:
                    pe.wait_ge(y_done[2], NT)
                for h in range(XH):
                    ins = pe.matmul(ps[:, 4 + 2 * n + h // 2, (h % 2) * T:(h % 2 + 1) * T], xmqT[:, h, n * P:(n + 1) * P], mkT[:, h], start=True, stop=True)
                ins.then_inc(xs_mm, 1)
            for n in range(NT):
                pr = prob[:, n * 1024:(n + 1) * 1024].rearrange("p (h j) -> p h j", h=XH)
                pe.wait_ge(xs_exp, n + 1)
                for h in range(XH):
                    for b in range(2):
                        at = (2 * h + b) * P
                        ins = pe.transpose(ps[:, 4 + 2 * n + at // TILE, at % TILE:at % TILE + P], pr[:, h, b * P:(b + 1) * P], ident[:])
                ins.then_inc(xs_tr, 1)
            for n in range(NT):
                prT = probT[:, n * 1024:(n + 1) * 1024].rearrange("p (h b i) -> p h b i", h=XH, b=2)
                pe.wait_ge(xs_trout, n + 1)
                for h in range(XH):
                    for b in range(2):
                        ins = pe.matmul(ps[:, n, h * HEAD:(h + 1) * HEAD], prT[:, h, b], mv[:, b, h * HEAD:(h + 1) * HEAD], start=(b == 0), stop=(b == 1))
                ins.then_inc(xo_mm, 1)
            for n, y in enumerate((zdn, gu, swz, xmz)):
                pe.wait_ge(y_done[n], NT)
                if n >= 2:
                    pe.wait_ge(yT_done, n - 1)
                b = 4 + 2 * (n % 2)
                for c in range(4):
                    for k in range(NT):
                        at = c * T + k * P
                        ins = pe.transpose(ps[:, b + at // TILE, at % TILE:at % TILE + P], y[:, k, c * P:(c + 1) * P], ident[:])
                ins.then_inc(yT_mm, 1)
            for n in range(NBR):
                for h in range(2):
                    name = f"gate{n}{h}"
                    tokens2(name)
                w = need2(f"up{n}").rearrange("p (c n) -> p c n", c=4)
                pe.wait_ge(yT_done, NBR)
                for k in range(4):
                    half, tau = k // 2, k % 2
                    if n:
                        pe.wait_ge(up_out, 4 * (n - 1) + k + 1)
                    for c in range(4):
                        ins = pe.matmul(ps[:, 4 + k, :], yT[:, 4 * n + c, tau * P:(tau + 1) * P], w[:, c, half * TILE:(half + 1) * TILE], start=(c == 0), stop=(c == 3))
                    ins.then_inc(up_mm, 1)
            transpose_all(merged, lambda: pe.wait_ge(merged_done, 4), lambda: None)
            actT_ready(5)
            pe.wait_ge(g2_out, len(groups2))
            for k in range(4):
                half, n = k // 2, k % 2
                w = need2(f"out{half}").rearrange("p (c n) -> p c n", c=KC)
                for c in range(KC):
                    ins = pe.matmul(ps[:, k, :], actT[:, c, n * P:(n + 1) * P], w[:, c], start=(c == 0), stop=(c == KC - 1))
                ins.then_inc(fin_mm, 1)


def layout(inputs):
    import numpy as np
    a = {k: np.asarray(v) for k, v in inputs.items()}

    def col(v):
        return v.reshape(-1, P).T

    r = {}
    for n in ("x", "mem_2", "gla_w_gate_up", "hg_norm_g", "gla_norm_g"):
        r[n] = a[n]
    for n in ("w_in", "w_out", "peer_w_q", "w_in_2", "w_mem_kv_2", "w_out_2"):
        r[n] = a[n][0]
    r["w_up_2"] = a["w_up_2"][0]
    r["cols"] = np.concatenate([col(a["norm1_g"]), col(a["norm2_g"]), col(a["norm_pre_2"]), col(a["norm_mem_2"]),
                                col(a["hg_lower_logits"]), col(a["gla_b_gate"]),
                                col(a["conv_w_2"]), col(a["spatial_b_2"])], axis=1)
    r["w_swq_2"] = a["w_in_2"][0][:, SWQ:SWQ + TILE].reshape(D, 2, 4, SHD).transpose(0, 2, 1, 3).reshape(D, TILE)
    r["norm_f_g"] = a["norm_f_g"]
    r["norm_post_2"] = a["norm_post_2"]
    r["rows"] = np.concatenate([a["gm_norm_2"][0], a["dn_norm_2"][0], a["a_log_2"][0], a["dt_bias_2"][0], a["sinks_2"][0]])
    r["spatial_w_t"] = a["spatial_w_2"][0].transpose(2, 0, 1).reshape(P, 4 * P)
    r["sub_keys_t"] = a["peer_sub_keys"][0].reshape(HP, NKEY, P).transpose(2, 0, 1).reshape(P, HP * NKEY)
    r["u_t"] = a["peer_u"][0].reshape(NKEY, NKEY, KC, P).transpose(1, 3, 2, 0).reshape(NKEY, P, D)
    r["v_t"] = a["peer_v"][0].reshape(NKEY, NKEY, D).transpose(1, 0, 2)
    return r


def kernel(**inputs):
    import concourse.bacc as bacc
    from concourse import mybir as mb
    from concourse.bass_utils import run_bass_kernel_spmd

    nc = bacc.Bacc("TRN2", target_bir_lowering=False, num_devices=1)
    arrays, t = {}, {}
    import numpy as np
    for name, a in layout(inputs).items():
        a = np.ascontiguousarray(a)
        arrays[f"in_{name}"] = a
        t[name] = nc.dram_tensor(f"in_{name}", a.shape, mb.dt.from_np(a.dtype), kind="ExternalInput").ap()
    out = nc.dram_tensor("out_0", (1, T, D), F32, kind="ExternalOutput").ap()
    build(nc, t, out)
    r = run_bass_kernel_spmd(nc, [arrays], core_ids=[0])
    return r.results[0]["out_0"]
```

```python
import concourse.bass as bass
from concourse import mybir
from contextlib import ExitStack

F32 = mybir.dt.float32
F32R = mybir.dt.float32r
U32 = mybir.dt.uint32
I32 = mybir.dt.int32
U8 = mybir.dt.uint8
ALU = mybir.AluOpType
ACT = mybir.ActivationFunctionType
AX = mybir.AxisListType

P = 128
D = 1024
T = 256
NT = T // P
KC = D // P
EPS = 1e-6
TILE = 512
RING = 3

HQ, HF, HI, HGATE, GQ, GV, GLOW, GGATE = 0, 512, 1024, 1536, 2048, 2560, 3072, 3088
RANK = 16
HEADS1 = 8
NF = 6
LEVELS = 7
GLA_SCALE = 64.0 ** -0.5
GATE_NORM = 16.0

PH = 8
HP = 2 * PH
NKEY = 128
TOP = 16
SLOTS = PH * TOP
NEG = -3.0e38
GT = 4
GBUF = 4
ROUND_HEADS = ((0, 2), (2, 4), (4, 6), (6, 8))
ROUNDS = len(ROUND_HEADS)
FULL = 4
CAND = FULL * TOP + (TOP - FULL) * 4
NGRP = T // GT

DNQ, DNK, DNV, DNZ, DNBA, GMU, GMV, GMZ, SWQ, SWKV, SWZ, XMQ, XMZ, GATES = (
    0, 512, 1024, 1536, 2048, 2056, 2568, 3080, 3592, 4104, 4360, 4872, 5384, 5896)
DH = 4
TH = NT * DH
CONV = 4
SH, SHD = 8, 64
XH = 4
HEAD = 128
NBR = 4
MASKED = -1.0e30
LEVEL_PIECES1 = ("hgate0", "hgate1", "ggate0", "ggate1")
LEVEL_PIECES = ("swz0", "swz1", "xmq0", "xmq1", "xmz0", "xmz1")
UP_AFTER = ("gate201", "gate211", "gate301", "gate311")
SW_BANKS = ((4, 5), (2, 3, 6, 7))


PIECES1 = [f"{name}{s}" for name in ("hq", "hf", "gqk") for s in range(2)] + ["glow"]
PIECES1 += [f"{name}{s}" for name in ("hi", "gv", "hgate", "ggate", "wo0", "wo1") for s in range(2)]
NP1 = len(PIECES1)
PIECES = PIECES1 + [f"{name}{s}" for name in ("dnq", "dnk", "dnv", "dnz", "gmu", "gmv", "gmz", "swq") for s in range(2)] + ["swkv"]
PIECES += [f"{name}{s}" for name in ("swz", "xmq", "xmz") for s in range(2)]
PIECES += [f"gate{_n}{_h}{_s}" for _n in range(2) for _h in range(2) for _s in range(2)]
for _n in range(NBR):
    PIECES += [f"gate{2 + _n // 2}{_n % 2}{_s}" for _s in range(2)] + [f"up{_n}{_s}" for _s in range(2)]
PIECES += [f"out{_h}{_s}" for _h in range(2) for _s in range(2)]


def bcast(ap, dim, n):
    a = ap.unsqueeze(dim)
    shape = list(a.shape)
    shape[dim] = n
    return a.broadcast_to(shape)


def head_rows(h):
    if h < 4:
        return h, slice(0, P)
    g = h - 4
    return 4 + g // 2, slice(64 * (g % 2), 64 * (g % 2) + 64)


PLACE = [0, 1, 4, 5, 2, 6, 3, 7]


def build(nc, t, out):
    ctx = ExitStack()
    with ctx:
        def sb(name, shape, dt=F32):
            return ctx.enter_context(nc.sbuf_tensor(name, shape, dt))

        def sem(name):
            return ctx.enter_context(nc.semaphore(name))

        def lease(*tensors):
            with ExitStack() as own:
                return [own.enter_context(nc.sbuf_tensor(name, shape, dt)) for name, shape, dt in tensors]

        resid = sb("resid", [P, NT, D])
        ident = sb("ident", [P, P])
        oi = sb("oi", [P, 2, P])
        ones, iota = oi[:, 0], oi[:, 1]
        act_j = oi[:].rearrange("p a b -> p (a b)")
        upper = sb("upper", [P, P])
        masks = sb("masks", [P, LEVELS + 1, P], U8)
        cols = sb("cols", [P, 94])
        mhalf = sb("mhalf", [P, 16])
        wh = sb("wh", [P, T], F32R)
        wl = sb("wl", [P, T], F32R)
        small = sb("small", [P, 512])
        big, ring, actT = lease(("big", [P, NKEY * T], F32), ("ring", [P, RING, KC * TILE], F32), ("actT", [P, KC, T], F32))
        yh, _, yl, _, raw, hi, lo, xh, xl = lease(
            ("yh", [P, NBR * 4, T], F32R), ("unused1", [P, 8 * D], F32), ("yl", [P, NBR * 4, T], F32R), ("unused2", [P, 16 * D], F32),
            ("raw", [P, 2, 2, D], F32), ("hi", [P, 2, 2, D], F32R), ("lo", [P, 2, 2, D], F32R),
            ("xh", [P, KC, T], F32R), ("xl", [P, KC, T], F32R))
        ps = ctx.enter_context(nc.psum_tensor("ps", [P, 8, TILE], F32))

        C_N1, C_N2, C_PRE, C_MEM, C_LOG, C_BG, C_CONV, C_SB = 0, 8, 16, 24, 32, 40, 42, 90

        def arena(base, width):
            at = [0]

            def take(*shape, dt=F32):
                n = 1
                for s in shape:
                    n *= s
                assert at[0] + n <= width, (at[0], n)
                v = base[:, at[0]:at[0] + n]
                at[0] += n
                if dt is not F32:
                    v = v.bitcast(dt)
                if len(shape) == 1:
                    return v
                names = " ".join(f"a{i}" for i in range(len(shape)))
                return v.rearrange(f"p ({names}) -> p {names}", **{f"a{i}": s for i, s in enumerate(shape)})
            return take

        take_small = arena(small[:], 512)
        sumsq = take_small(NT)
        mean = take_small(NT)
        rstd = take_small(NT)
        lbe = take_small(2, 4)
        lbm = take_small(4)
        lbs = take_small(4)
        lbr = take_small(4)
        lb = take_small(4)
        lb1 = take_small(4)
        sumsq_o = take_small(NT, HEADS1)
        mean_o = take_small(NT, HEADS1)
        rstd_o = take_small(NT, HEADS1)
        sumsq_m = take_small(NT)
        mean_m = take_small(NT)
        rstd_m = take_small(NT)
        sumsq_h = take_small(NT)
        mean_h = take_small(NT)
        rstd_h = take_small(NT)
        esum = take_small(PH, NT)
        einv = take_small(PH, NT)

        take1 = arena(big[:], NKEY * T)
        scaled = take1(NT, D)
        qF = take1(NF, T)
        kF = take1(NF, T)
        gF = take1(NF, T)
        cum = take1(NF, T)
        dec = take1(2, NF, T)
        qd = take1(2, NF, T)
        kd = take1(2, NF, T)
        vtok = take1(NT, D)
        gate1 = take1(NT, D)
        glowT = take1(T)
        gate_up = take1(2, P)[0:RANK]
        zg = gate1[:, 0, 0:TILE].rearrange("p (a t) -> p a t", a=2)
        zabs = gate1[:, 0, TILE:D].rearrange("p (a t) -> p a t", a=2)
        own = take1(NT, HEADS1, P)
        cross = take1(HEADS1, P)
        mixed = take1(NT, D)
        mixT = take1(KC, T)
        sqtmp = take1(NT, D)
        xi = take1(P, dt=I32)
        xj = take1(P, dt=I32)
        xx = take1(P, dt=I32)
        xf = take1(P)
        ge = cross
        gnorm = take1(2, P)
        memtok = own.rearrange("p n h i -> p n (h i)")
        memT = mixT
        mkv_new = sqtmp

        x_then_norm_f_loaded = sem("x_then_norm_f_loaded")
        params_loaded = sem("params_loaded")
        mem_loaded = sem("mem_loaded")
        mem_scaled = sem("mem_scaled")
        mem_T = sem("mem_T")
        memT_done = sem("memT_done")
        tile_loaded = [sem(f"tile_loaded{i}") for i in range(RING)]
        consts_made = sem("consts_made")
        pool_step = sem("pool_step")
        dve_step = sem("dve_step")
        act_step = sem("act_step")
        sumsq_done = sem("sumsq_done")
        rstd_done = sem("rstd_done")
        scaled_done = sem("scaled_done")
        transposed = sem("transposed")
        actT_done = [sem("actT_by_act"), sem("actT_by_dve")]
        group_done = sem("group_done")
        group_out = sem("group_out")
        fgate_done = sem("fgate_done")
        logf_done = sem("logf_done")
        gate_mm = sem("gate_mm")
        softplus_done = sem("softplus_done")
        cum_done = sem("cum_done")
        lb_in = sem("lb_in")
        lb_exp = sem("lb_exp")
        masks_done = sem("masks_done")
        lvl_exponent = sem("lvl_exponent")
        lvl_decay = sem("lvl_decay")
        lvl_scaled = sem("lvl_scaled")
        lvl_scores = sem("lvl_scores")
        lvl_kept = sem("lvl_kept")
        cross_out = sem("cross_out")
        o_done = sem("o_done")
        osq_done = sem("osq_done")
        osum_done = sem("osum_done")
        orstd_done = sem("orstd_done")
        mixed_done = sem("mixed_done")
        wout_done = sem("wout_done")
        h_done = sem("h_done")
        sub_done = sem("sub_done")
        sub_out = sem("sub_out")
        matched = sem("matched")
        pick_kept = sem("pick_kept")
        picks_done = sem("picks_done")
        pick_mm = sem("pick_mm")
        pickT_done = sem("pickT_done")
        soft_in = sem("soft_in")
        soft_exp = sem("soft_exp")
        onehot_ready = sem("onehot_ready")
        onehot_weighted = sem("onehot_weighted")
        onehot_by_act = sem("onehot_by_act")
        dist_done = sem("dist_done")
        g_mm = sem("g_mm")
        g_out = sem("g_out")
        u_loaded = [sem(f"u_loaded{i}") for i in range(2)]
        v_loaded = [sem(f"v_loaded{i}") for i in range(2)]
        u_mm = sem("u_mm")
        gelu_done = sem("gelu_done")
        prod_done = sem("prod_done")
        wh_done = sem("wh_done")
        wl_done = sem("wl_done")
        hi_done = [sem("u_hi_done"), sem("v_hi_done")]
        lo_done = [sem("u_lo_done"), sem("v_lo_done")]
        x_split = sem("x_split")
        mkv_moved = sem("mkv_moved")
        v_mm = sem("v_mm")
        peer_out = sem("peer_out")

        t["mkv_keep"] = nc.dram_tensor("mkv_keep", (P, 2048), F32, kind="Internal").ap()

        def wtile(name, c0, n=TILE):
            src = t[name][:, c0:c0 + n].rearrange("(c p) n -> p c n", p=P)
            return lambda s: (ring[:, s, 0:KC * n].rearrange("p (c n) -> p c n", c=KC), src)

        tiles1 = [("wq0", wtile("peer_w_q", 0)), ("wq1", wtile("peer_w_q", TILE)),
                  ("wq2", wtile("peer_w_q", 2 * TILE)), ("wq3", wtile("peer_w_q", 3 * TILE)),
                  ("mk", wtile("w_mem_kv_2", 0)), ("mv", wtile("w_mem_kv_2", TILE))]
        tile_no = {name: i for i, (name, _) in enumerate(tiles1)}
        N1 = len(tiles1)

        loads_p = [len(range(s, NP1, 2)) for s in range(2)] + [0]
        loads1 = [loads_p[s] + len(range(s, N1, RING)) for s in range(RING)]
        features_of = ("hq", "hf", "gqk", "dnq", "dnk", "dnv", "swq", "xmq")
        tokens_of = ["hi", "gv", "hgate", "ggate", "wo0", "wo1", "dnz", "gmu", "gmv", "gmz", "swz", "xmz"]
        tokens_of += [f"gate{n}{h}" for n in range(NBR) for h in range(2)] + ["out0", "out1"]
        pieces = PIECES
        piece_no = {name: k for k, name in enumerate(pieces)}
        loaded_pieces = [name for name in pieces if name[:2] != "up"]
        load_no = {name: k for k, name in enumerate(loaded_pieces)}
        raw2, hi2, lo2 = (v[:].rearrange("p s a n -> p s (a n)") for v in (raw, hi, lo))

        def piece_slot(name):
            k = piece_no[name]
            return (k if k < NP1 else k - NP1) % 2

        def raw_slot(name):
            k = load_no[name]
            return (k if k < NP1 else k - NP1) % 2

        def piece_loads(name):
            k, s = load_no[name], raw_slot(name)
            return 16 * (k // 2 + 1 if k < NP1 else loads1[s] + (k - NP1) // 2 + 1)

        def raw_piece(name):
            if name[:2] == "up":
                return up_w[:, int(name[2]), :, int(name[3]) * TILE:(int(name[3]) + 1) * TILE]
            return raw2[:, raw_slot(name)]

        def part_of(v, name):
            v = v[:, piece_slot(name)]
            return v.rearrange("p (c n) -> p c n", c=4) if name[:2] == "up" else v

        up_order = [(k % 2, k // 2) for k in range(4)]

        def slot(name):
            return tile_no[name] % RING

        def tile_view(name):
            return ring[:, slot(name), :].rearrange("p (c n) -> p c n", c=KC)

        groups1 = ["hq0", "hq1", "hf0", "hf1", "gqk0", "gqk1", "glow", "hi0", "hi1", "gv0", "gv1",
                   "hgate0", "hgate1", "ggate0", "ggate1",
                   "wq00", "wq01", "wq10", "wq11", "wq20", "wq21", "wq30", "wq31", "mk0", "mk1", "mv0", "mv1"]
        group_no = {g: i for i, g in enumerate(groups1)}

        def gbank(g):
            return group_no[g] % 4

        def tile_used(name):
            return group_done, group_no[name + "1"] + 1

        takeP = arena(big[:], NKEY * T)
        scaled_p = takeP(NT, D)
        qT = takeP(HP, T)
        ssb = takeP(NT, HP, NKEY)
        srest = takeP(2, NT * 2, NKEY)
        stop_ = takeP(2, PH, NT, TOP)
        sidx = takeP(2, PH, NT, TOP, dt=U32)
        sidxf = takeP(2, PH, NT, TOP)
        cand = takeP(NT * 2, CAND)
        crest = takeP(NT * 2, CAND)
        best = takeP(PH, NT, TOP)
        pos = takeP(PH, NT, TOP, dt=U32)
        posi = takeP(3, NT * 2, TOP, dt=U32)
        posf = takeP(3, NT * 2, TOP)
        place = takeP(2, NT * 2, TOP)
        pick = takeP(2, 2, NT * 2, TOP, TOP)
        chosen = takeP(NT, 3, SLOTS)
        G = big[:].rearrange("p (t j) -> p t j", j=NKEY)
        takeR = arena(ring[:, 1:3, :].rearrange("p s n -> p (s n)"), 2 * KC * TILE)
        chosenT = takeR(3, T)
        hotA = takeR(GBUF, GT, NKEY)
        matchB = takeR(GBUF, GT, NKEY)
        hotB = takeR(GBUF, GT, NKEY)
        dist = takeR(GBUF, NKEY)
        minus_w = takeR(T)
        xround = takeP(KC, T)

        def heads_of(r):
            return slice(*ROUND_HEADS[r])

        def rows_of(r):
            return slice(0, NT * (ROUND_HEADS[r][1] - ROUND_HEADS[r][0]))

        def pairs_of(v, r):
            return v[:, heads_of(r)].rearrange("p h n k -> p (h n) k")

        def round_keys(r, a):
            return bcast(pairs_of(sidxf[:, a], r), 2, TOP)

        keysT = mixed.rearrange("p n (a m) -> p (n a) m", m=NKEY)
        U, V = 0, 1

        take2 = arena(big[:], NKEY * T)
        u1 = take2(3108)
        u2 = take2(2048)
        u3 = take2(3072)
        u4 = take2(3072)
        u5 = take2(2048)
        u6 = take2(3072 + 512)
        zdn = take2(NT, TILE)
        gu = take2(NT, TILE)
        gv2 = take2(NT, TILE)
        gz = take2(NT, TILE)
        swqT = take2(4, T)
        swkv = take2(TILE)
        swz = take2(NT, TILE)
        prob = take2(3072)
        probT = take2(3072)
        xmqT = take2(4, T)
        xmz = take2(NT, TILE)
        rows = take2(656)
        window = take2(2, P)
        gm_gain, dn_gain = rows[:, 0:TILE], rows[:, TILE:TILE + P]
        a_log, dt_bias, sinks = rows[:, 640:644], rows[:, 644:648], rows[:, 648:656]
        scaled2 = u1[:, 0:2048].rearrange("p (n d) -> p n d", n=NT)
        convin = u1.rearrange("p (f t) -> p f t", f=3 * DH)
        a1 = arena(u1, 3108)
        LT, AQ, BT = a1(TH, P), a1(TH, P), a1(TH, P)
        norm_f = u2[:, 0:D]
        sqk = u2.rearrange("p (f t) -> p f t", f=2 * DH)
        a2 = arena(u2, 2048)
        X, Z = a2(TH, P), a2(TH, P)
        rep = u3.rearrange("p (a h m) -> p a h m", a=3, h=TH)
        a3 = arena(u3, 3072)
        Y, kbg, vb = a3(TH, P), a3(TH, P), a3(TH, P)
        convT = u4.rearrange("p (f t) -> p f t", f=3 * DH)
        a5 = arena(u5, 2048)
        du, wT, S1 = a5(TH, P), a5(DH, P), a5(DH, P)
        a6 = arena(u6, 3584)
        Dm, brow, qrow, qg = a6(TH, P), a6(TH, P), a6(TH, P), a6(DH, P)
        a3b = arena(brow.rearrange("p h c -> p (h c)"), 1024)
        kdl, vnew = a3b(DH, P), a3b(DH, P)
        ba_hi, ba_lo = (v[:, 0:KC * 2 * DH].rearrange("p (c n) -> p c n", c=KC) for v in (wh, wl))
        mkv = u4[:, 0:2048]
        mkT = mkv[:, 0:1024].rearrange("p (h m) -> p h m", h=XH)
        mv = mkv[:, 1024:2048].rearrange("p (n d) -> p n d", n=NT)
        wsT = probT[:, 0:4 * P].rearrange("p (g q) -> p g q", g=4)
        swkT, swv = swkv[:, 0:T], swkv[:, T:2 * T].rearrange("p (n d) -> p n d", n=NT)
        take3 = arena(big[:, 0:17000], 17000)
        take3(NBR * 4 * T)
        gsb = take3(2, 4, TILE)
        merged = take3(NT, D)
        outsb = take3(NT, D)
        norm_post = big[:, 16 * D:17 * D]
        up_w = big[:, 4 * 4 * D:].rearrange("p (n c d) -> p n c d", n=NBR, c=4)
        sumsq_f, mean_f, rstd_f = (take_small(NT) for _ in range(3))
        sumsq_x, mean_x, rstd_x = (take_small(NT) for _ in range(3))
        sumsq_p, mean_p, rstd_p = (take_small(NT) for _ in range(3))
        ba_w = take_small(KC, 2 * DH)
        ba = take_small(NT, 2 * DH)
        beta = take_small(NT, DH)
        dz = take_small(NT, DH)
        dsp = take_small(NT, DH)
        nega = take_small(DH)
        dg = take_small(NT, DH)
        rin = take_small(NT, 2 * DH)
        rr = take_small(NT, 2 * DH)
        gcs = take_small(2, TH)
        egc = take_small(NT, DH)
        ekd = take_small(DH)
        brk = take_small(NT, DH)
        rqs = take_small(NT, DH)
        kbf = take_small(NT, DH)
        sumsq_a, mean_a, rstd_a = (take_small(NT, DH) for _ in range(3))
        sumsq_v, mean_v, rstd_v = (take_small(NT) for _ in range(3))
        smax, snm, sden, srec, ssk = (take_small(NT, SH) for _ in range(5))
        xmax, xnm, xden, xrec = (take_small(NT, XH) for _ in range(4))

        rows_loaded = sem("rows_loaded")
        up_loaded = sem("up_loaded")
        hg_done = sem("hg_done")
        ba_split = sem("ba_split")
        g2_done = sem("g2_done")
        half_mm = sem("half_mm")
        piece_hi = sem("piece_hi")
        piece_lo = sem("piece_lo")
        g2_out = sem("g2_out")
        conv_done = sem("conv_done")
        conv_zero = sem("conv_zero")
        dnsilu_done = sem("dnsilu_done")
        ss_mm = sem("ss_mm")
        rin_done = sem("rin_done")
        rr_done = sem("rr_done")
        beta_done = sem("beta_done")
        dz_done = sem("dz_done")
        dln_done = sem("dln_done")
        dg_done = sem("dg_done")
        gc_mm = sem("gc_mm")
        gcs_done = sem("gcs_done")
        egc_done = sem("egc_done")
        rep_done = sem("rep_done")
        row_mm = sem("row_mm")
        dm_in = sem("dm_in")
        dm_done = sem("dm_done")
        brow_done = sem("brow_done")
        qrow_done = sem("qrow_done")
        kk_mm = sem("kk_mm")
        lt_done = sem("lt_done")
        qk_mm = sem("qk_mm")
        aq_done = sem("aq_done")
        kv_tr = sem("kv_tr")
        kv_out = sem("kv_out")
        z0_done = sem("z0_done")
        x0_tr = sem("x0_tr")
        x_done = sem("x_done")
        bt_done = sem("bt_done")
        y_mm = sem("y_mm")
        y_out = sem("y_out")
        pz_mm = sem("pz_mm")
        z_done = sem("z_done")
        u_out_mm = sem("u_out_mm")
        du_done = sem("du_done")
        s1_mm = sem("s1_mm")
        s1_done = sem("s1_done")
        ws_mm = sem("ws_mm")
        vnew_done = sem("vnew_done")
        qg_done = sem("qg_done")
        do_mm = sem("do_mm")
        dosq_done = sem("dosq_done")
        dosum_done = sem("dosum_done")
        dors_done = sem("dors_done")
        y_done = [sem(f"y_done{n}") for n in range(NBR)]
        gmv_sq = sem("gmv_sq")
        gmv_rstd = sem("gmv_rstd")
        gmv_done = sem("gmv_done")
        gm_mm = sem("gm_mm")
        ss_mm2 = sem("sw_scores")
        s_masked = sem("sw_masked")
        s_exp = sem("sw_exp")
        s_tr = sem("sw_transposed")
        s_trout = sem("sw_probT")
        so_mm = sem("sw_out")
        xs_mm = sem("xm_scores")
        xs_max = sem("xm_max")
        xs_exp = sem("xm_exp")
        xs_tr = sem("xm_transposed")
        xs_trout = sem("xm_probT")
        xo_mm = sem("xm_out")
        yT_mm = sem("yT_mm")
        yT_hi = sem("yT_hi")
        yT_done = sem("yT_done")
        up_mm = sem("up_mm")
        up_out = sem("up_out")
        merged_done = sem("merged_done")
        fin_mm = sem("fin_mm")
        fin_copied = sem("fin_copied")
        out_done = sem("out_done")
        stored = sem("stored")

        groups2 = ["dnq0", "dnq1", "dnk0", "dnk1", "dnv0", "dnv1", "ba", "dnz0", "dnz1", "gmu0", "gmu1", "gmv0", "gmv1",
                   "gmz0", "gmz1", "swq0", "swq1", "swkv", "swz0", "swz1", "xmq0", "xmq1", "xmz0", "xmz1"]
        for n in range(NBR):
            groups2 += [f"gate{n}{h}{k}" for h in range(2) for k in range(NT)]
        g2_no = {g: i for i, g in enumerate(groups2)}
        early = [g for g in groups2 if g[:5] in ("gate0", "gate1")]
        g2_bank = {g: i % 2 if g in early else i % 4 for g, i in g2_no.items()}

        def piece_used(name):
            if name[:2] == "up":
                n, half = int(name[2]), int(name[3])
                return up_mm, 4 * n + max(k for k, (_, h) in enumerate(up_order) if h == half) + 1
            done, number = (group_done, group_no) if piece_no[name] < NP1 else (g2_done, g2_no)
            if name in ("swkv", "glow") or name[:-1] in features_of:
                return done, number[name] + 1
            if name[-1] == "0":
                return half_mm, tokens_of.index(name[:-1]) + 1
            if name[:2] == "wo":
                return wout_done, 2 * int(name[2]) + 2
            if name[:3] == "out":
                return fin_mm, 2 * int(name[3]) + 2
            return done, number[name] + 1

        def next_piece(name, ahead):
            return pieces[piece_no[name] + ahead]

        block = ctx.enter_context(nc.Block())

        @block.sync
        def _(sp):
            sp.dma_start(resid[:], t["x"].rearrange("b (n p) d -> p (b n) d", p=P)).then_inc(x_then_norm_f_loaded, 16)
            def load_piece(k):
                slot = raw_slot(loaded_pieces[k])
                if k == NP1 or k == NP1 + 1:
                    sp.wait_ge(lo_done[slot], NKEY)
                elif k >= 2:
                    sp.wait_ge(piece_lo, piece_no[loaded_pieces[k - 2]] + 1)
                sp.dma_start(raw2[:, slot], t["pieces"][k]).then_inc(tile_loaded[slot], 16)

            sp.wait_ge(params_loaded, 64)
            for k in range(NP1):
                load_piece(k)
            sp.wait_ge(o_done, NT)
            sp.dma_start(memtok, t["mem_2"].rearrange("b (n p) d -> p (b n) d", p=P)).then_inc(mem_loaded, 16)
            for k, (name, make) in enumerate(tiles1):
                if k == 0:
                    sp.wait_ge(piece_lo, NP1)
                elif k == 1:
                    sp.wait_ge(wout_done, 4)
                elif k >= RING:
                    sp.wait_ge(*tile_used(tiles1[k - RING][0]))
                dst, src = make(k % RING)
                sp.dma_start(dst, src).then_inc(tile_loaded[k % RING], 16)
                if name == "wq0":
                    sp.wait_ge(transposed, 8)
                    sp.wait_ge(sumsq_done, 6)
                    sp.dma_start(keysT.rearrange("p a n -> p (a n)"), t["sub_keys_t"]).then_inc(mem_loaded, 16)
            sp.wait_ge(*tile_used("wq3"))
            loaded = (u_loaded, v_loaded)

            def load_rows(which, j, par, before=None):
                if before is not None:
                    sp.wait_ge(lo_done[which], before)
                sp.dma_start(raw[:, which, par], t[("u_t", "v_t")[which]][bass.ds(j, 1), :, :].rearrange("o p n -> p (o n)")).then_inc(loaded[which][par], 16)

            for j in range(2):
                load_rows(U, j, j)
                load_rows(V, j, j)
            sp.wait_ge(group_out, group_no["mv1"] + 1)
            sp.dma_start(t["mkv_keep"], mkv_new.rearrange("p a n -> p (a n)")).then_inc(mkv_moved, 16)
            with sp.Fori(1, NKEY // 2) as i:
                for par in range(2):
                    load_rows(U, 2 * i + par, par, 2 * i + (par - 1))
                    load_rows(V, 2 * i + par, par, 2 * i + (par - 1))
            load_piece(NP1)
            sp.wait_ge(prod_done, NKEY)
            sp.dma_start(norm_f, t["norm_f_g"].partition_broadcast(P)).then_inc(x_then_norm_f_loaded, 16)
            load_piece(NP1 + 1)
            sp.dma_start(rows, t["rows"].partition_broadcast(P)).then_inc(rows_loaded, 16)
            sp.dma_start(ba_w.rearrange("p c n -> p (c n)"), t["ba"]).then_inc(rows_loaded, 16)
            sp.dma_start(wsT, t["spatial_w_t"].rearrange("p (g q) -> p g q", g=4)).then_inc(rows_loaded, 16)
            for k in range(NP1 + 2, len(loaded_pieces)):
                load_piece(k)
                if loaded_pieces[k] == "gate001":
                    sp.wait_ge(qg_done, 1)
                    sp.wait_ge(qk_mm, 1)
                    sp.dma_start(mkv, t["mkv_keep"]).then_inc(mkv_moved, 16)
                if loaded_pieces[k] in UP_AFTER:
                    n = UP_AFTER.index(loaded_pieces[k])
                    if n == 0:
                        sp.wait_ge(yT_mm, NBR)
                    else:
                        sp.wait_ge(up_loaded, 16 * n)
                    sp.dma_start(up_w[:, n], t["up"][n]).then_inc(up_loaded, 16)
            sp.wait_ge(piece_lo, piece_no["up01"] + 1)
            sp.dma_start(norm_post, t["norm_post_2"][0].partition_broadcast(P)).then_inc(rows_loaded, 16)
            for n in range(NT):
                sp.wait_ge(out_done, n + 1)
                sp.dma_start(out[0, n * P:(n + 1) * P, :], outsb[:, n]).then_inc(stored, 16)
            sp.wait_ge(stored, 16 * NT)

        @block.gpsimd
        def _(pool):
            steps = [0]

            def link(ins):
                steps[0] += 1
                ins.then_inc(pool_step, 1)
                pool.wait_ge(pool_step, steps[0])

            def rsqrt(o, m, s, width, n):
                link(pool.tensor_scalar(m, s, 1.0 / width, EPS, ALU.mult, ALU.add))
                return pool.tensor_tensor(o, m, n, ALU.pow)

            pool.memset(ident[:], 0.0).then_inc(pool_step, 1)
            pool.memset(ones, 1.0).then_inc(pool_step, 1)
            pool.memset(mhalf[:], -0.5).then_inc(pool_step, 1)
            steps[0] = 3
            pool.wait_ge(pool_step, 3)
            pool.affine_select(out=ident[:], in_=ident[:], compare_op=ALU.not_equal, fill=1.0, base=0,
                               pattern=[[-1, P]], channel_multiplier=1)
            pool.affine_select(out=upper[:], in_=ones, compare_op=ALU.is_ge, fill=0.0, base=0,
                               pattern=[[1, P]], channel_multiplier=-1)
            pool.iota(iota, pattern=[[1, P]], base=0, channel_multiplier=0, allow_small_or_imprecise_dtypes=True)
            pool.iota(xi, pattern=[[1, P]], base=0, channel_multiplier=0)
            pool.iota(xj, pattern=[[0, P]], base=0, channel_multiplier=1).then_inc(consts_made, 1)
            for n in range(NT):
                pool.wait_ge(sumsq_done, 1 + n)
                rsqrt(rstd[:, n:n + 1], mean[:, n:n + 1], sumsq[:, n:n + 1], D, mhalf[:, 0:1]).then_inc(rstd_done, 1)
            for l in range(LEVELS):
                m = 1 << l
                if l == 0:
                    pool.wait_ge(cum_done, 2 * NF)
                if l >= 2:
                    pool.wait_ge(lvl_scaled, l - 1)
                c = cum.rearrange("p f (b two m) -> p (f b) two m", two=2, m=m)
                d = dec[:, l % 2].rearrange("p f (b two m) -> p (f b) two m", two=2, m=m)
                mid = c[:, :, 0, m - 1:m].broadcast_to([P, NF * T // (2 * m), m])
                pool.tensor_tensor(d[:, :, 1, :], c[:, :, 1, :], mid, ALU.subtract)
                pool.tensor_tensor(d[:, :, 0, :], mid, c[:, :, 0, :], ALU.subtract).then_inc(lvl_exponent, 1)
            pool.wait_ge(lvl_scaled, LEVELS - 1)
            last = cum[:, :, P - 1:P].broadcast_to([P, NF, P])
            pool.tensor_tensor(dec[:, 1, :, 0:P], last, cum[:, :, 0:P], ALU.subtract).then_inc(lvl_exponent, 1)
            for n in range(NT):
                pool.wait_ge(osum_done, n + 1)
                rsqrt(rstd_o[:, n], mean_o[:, n], sumsq_o[:, n], P, mhalf[:, 0:HEADS1]).then_inc(orstd_done, 1)
            for n in range(NT):
                pool.wait_ge(sumsq_done, 3 + n)
                rsqrt(rstd_h[:, n:n + 1], mean_h[:, n:n + 1], sumsq_h[:, n:n + 1], D, mhalf[:, 0:1]).then_inc(rstd_done, 1)
            pool.wait_ge(sumsq_done, 6)
            rsqrt(rstd_m, mean_m, sumsq_m, D, mhalf[:, 0:NT]).then_inc(rstd_done, 1)
            for r in range(ROUNDS - 1):
                for a in range(2):
                    pool.wait_ge(matched, 2 * r + a + 1)
                    rows = pick[:, r % 2, a, rows_of(r)]
                    pool.tensor_tensor(rows, rows, round_keys(r, a), ALU.mult).then_inc(pick_kept, 1)

            pool.wait_ge(x_split, 1)
            pool.tensor_tensor(xl[:], actT[:], xround, ALU.subtract).then_inc(x_split, 1)

            def weigh(n, at, buf, first=False):
                pool.wait_ge(onehot_ready, n)
                if not first:
                    pool.wait_ge(g_mm, n - GBUF)
                pool.tensor_tensor(hotB[:, buf, 1:GT], matchB[:, buf, 1:GT], bcast(chosenT[:, 2, at], 2, NKEY), ALU.mult).then_inc(onehot_weighted, 1)

            for b in range(GBUF):
                weigh(b + 1, slice(b * GT + 1, b * GT + GT), b, first=True)
            with pool.Fori(1, NGRP // GBUF) as i:
                for b in range(GBUF):
                    weigh(GBUF * i + (b + 1), bass.ds(i * (GBUF * GT) + (b * GT + 1), GT - 1), b)
            pool.wait_ge(wl_done, NKEY)
            pool.memset(ones, 1.0).then_inc(consts_made, 1)
            for n in range(NT):
                f, x, half = slice(n, n + 1), slice(n, n + 1), mhalf[:, 0:1]
                pool.wait_ge(sumsq_done, 6 + 2 * n + 1)
                link(rsqrt(rstd_f[:, f], mean_f[:, f], sumsq_f[:, f], D, half))
                link(pool.tensor_tensor(mean_x[:, x], rstd_f[:, f], rstd_f[:, f], ALU.mult))
                pool.wait_ge(sumsq_done, 6 + 2 * n + 2)
                link(pool.tensor_tensor(sumsq_x[:, x], sumsq_x[:, x], mean_x[:, x], ALU.mult))
                link(rsqrt(rstd_x[:, x], mean_x[:, x], sumsq_x[:, x], D, half))
                pool.tensor_tensor(rstd_x[:, x], rstd_x[:, x], rstd_f[:, f], ALU.mult).then_inc(rstd_done, 1)
            pool.wait_ge(rin_done, 1)
            pool.tensor_tensor(rr.rearrange("p n f -> p (n f)"), rin.rearrange("p n f -> p (n f)"), mhalf[:], ALU.pow).then_inc(rr_done, 1)
            pool.wait_ge(gmv_sq, 2)
            rsqrt(rstd_v, mean_v, sumsq_v, TILE, mhalf[:, 0:NT]).then_inc(gmv_rstd, 1)
            for n in range(NT):
                pool.wait_ge(dosum_done, n + 1)
                rsqrt(rstd_a[:, n], mean_a[:, n], sumsq_a[:, n], HEAD, mhalf[:, 0:DH]).then_inc(dors_done, 1)
            for n in range(NT):
                pool.wait_ge(sumsq_done, 10 + n + 1)
                rsqrt(rstd_p[:, n:n + 1], mean_p[:, n:n + 1], sumsq_p[:, n:n + 1], D, mhalf[:, 0:1]).then_inc(rstd_done, 1)

        @block.scalar
        def _(act):
            steps = [0]

            def link(ins):
                steps[0] += 1
                ins.then_inc(act_step, 1)
                act.wait_ge(act_step, steps[0])

            act.dma_start(cols[:], t["cols"]).then_inc(params_loaded, 16)
            act.dma_start(gate_up.rearrange("p a n -> p (a n)"), t["gla_w_gate_up"][0]).then_inc(params_loaded, 16)
            act.dma_start(gnorm[:, 0], t["hg_norm_g"][0].partition_broadcast(P)).then_inc(params_loaded, 16)
            act.dma_start(gnorm[:, 1], t["gla_norm_g"][0].partition_broadcast(P)).then_inc(params_loaded, 16)
            act.wait_ge(x_then_norm_f_loaded, 16)
            for n in range(NT):
                act.activation(sqtmp[:, n], resid[:, n], ACT.Square, accum_out=sumsq[:, n:n + 1]).then_inc(sumsq_done, 1)
            act.wait_ge(params_loaded, 64)
            act.wait_ge(lb_in, 1)
            act.activation(lbe.rearrange("p a f -> p (a f)"), lbe.rearrange("p a f -> p (a f)"), ACT.Exp).then_inc(lb_exp, 1)

            def copy_out_T(n_before, dst, gcol):
                for c in (2, 3, 6, 7):
                    act.wait_ge(transposed, n_before + c // 2 + 1)
                    src = ps[:, 4 + c // 2, (c % 2) * T:(c % 2 + 1) * T]
                    act.activation(dst[:, c], src, ACT.Copy, scale=cols[:, gcol + c:gcol + c + 1]).then_inc(actT_done[0], 1)

            def copy_hi_T(n_before, gcol):
                for c in range(KC):
                    act.wait_ge(transposed, n_before + c // 2 + 1)
                    src = ps[:, 4 + c // 2, (c % 2) * T:(c % 2 + 1) * T]
                    act.activation(xh[:, c], src, ACT.Copy, scale=cols[:, gcol + c:gcol + c + 1]).then_inc(actT_done[0], 1)

            def copy_hi_tiles(n_before):
                for n in range(NT):
                    for half in range(2):
                        act.wait_ge(transposed, n_before + 2 * n + half + 1)
                        act.activation(xh[:, 4 * half:4 * half + 4, n * P:(n + 1) * P], ps[:, 4 + 2 * n + half, :].rearrange("p (c t) -> p c t", c=4), ACT.Copy).then_inc(actT_done[0], 1)

            def piece_split_hi(name):
                k = piece_no[name]
                if name[:2] == "up":
                    act.wait_ge(up_loaded, 16 * int(name[2]) + 16)
                else:
                    act.wait_ge(tile_loaded[raw_slot(name)], piece_loads(name))
                if k == NP1 or k == NP1 + 1:
                    act.wait_ge((u_mm, v_mm)[piece_slot(name)], NKEY)
                elif k >= 2:
                    act.wait_ge(*piece_used(next_piece(name, -2)))
                act.activation(part_of(hi2, name), raw_piece(name), ACT.Copy).then_inc(piece_hi, 1)

            def split_2nd_after(name):
                piece_split_hi(next_piece(name, 2))

            piece_split_hi("hq0")
            copy_hi_T(0, C_N1)
            piece_split_hi("hq1")

            def from_group(g):
                act.wait_ge(group_done, group_no[g] + 1)
                return ps[:, gbank(g), :]

            def out_group(g, dst, func, **kw):
                act.activation(dst, from_group(g), func, **kw).then_inc(group_out, 1)

            def feat(ap):
                return ap.rearrange("p f t -> p (f t)")

            for a in range(2):
                out_group(f"hq{a}", feat(qF[:, 2 * a:2 * a + 2]), ACT.Silu)
                split_2nd_after(f"hq{a}")
            for a in range(2):
                out_group(f"hf{a}", feat(gF[:, 2 * a:2 * a + 2]), ACT.Sigmoid)
                split_2nd_after(f"hf{a}")
            out_group("gqk0", feat(qF[:, 4:6]), ACT.Copy, scale=GLA_SCALE)
            split_2nd_after("gqk0")
            out_group("gqk1", feat(kF[:, 4:6]), ACT.Copy)
            split_2nd_after("gqk1")
            act.wait_ge(group_done, group_no["glow"] + 1)
            act.activation(glowT[0:RANK], ps[0:RANK, gbank("glow"), 0:T], ACT.Copy).then_inc(group_out, 1)
            split_2nd_after("glow")
            act.wait_ge(fgate_done, 1)
            act.activation(feat(gF[:, 0:4]), feat(gF[:, 0:4]), ACT.Ln).then_inc(logf_done, 1)
            act.wait_ge(gate_mm, 1)
            for a in range(2):
                act.activation(zg[:, a], ps[:, 7, a * T:(a + 1) * T], ACT.Identity,
                               bias=cols[:, C_BG + a:C_BG + a + 1]).then_inc(act_step, 1)
            steps[0] += 2
            act.wait_ge(act_step, steps[0])
            link(act.activation(feat(zabs), feat(zg), ACT.Abs))
            link(act.activation(feat(zabs), feat(zabs), ACT.Exp, scale=-1.0))
            act.activation(feat(zabs), feat(zabs), ACT.Ln, bias=1.0).then_inc(softplus_done, 1)
            split_2nd_after("hi0")
            for a in range(NT):
                out_group(f"hi{a}", vtok[:, a, 0:TILE], ACT.Copy)
            split_2nd_after("hi1")
            split_2nd_after("gv0")
            for a in range(NT):
                out_group(f"gv{a}", vtok[:, a, TILE:D], ACT.Copy)
            split_2nd_after("gv1")
            for l in range(LEVELS):
                act.wait_ge(lvl_exponent, l + 1)
                act.activation(feat(dec[:, l % 2]), feat(dec[:, l % 2]), ACT.Exp).then_inc(lvl_decay, 1)
                if 1 <= l <= 4:
                    split_2nd_after(LEVEL_PIECES1[l - 1])
            act.wait_ge(lvl_exponent, LEVELS + 1)
            act.activation(dec[:, 1, :, 0:P], dec[:, 1, :, 0:P], ACT.Exp)
            act.activation(dec[:, 1, :, P:T], cum[:, :, P:T], ACT.Exp).then_inc(lvl_decay, 1)
            for g, dst, f in (("hgate0", gate1[:, 0, 0:TILE], ACT.Silu), ("hgate1", gate1[:, 1, 0:TILE], ACT.Silu),
                              ("ggate0", gate1[:, 0, TILE:D], ACT.Silu), ("ggate1", gate1[:, 1, TILE:D], ACT.Silu)):
                out_group(g, dst, f)
            act.wait_ge(lvl_scores, 2 * (LEVELS + 1) + 1)
            act.activation(cross.rearrange("p h i -> p (h i)"), ps[:, 4:6, :].rearrange("p b n -> p (b n)"), ACT.Copy).then_inc(cross_out, 1)
            for n in range(NT):
                act.wait_ge(o_done, n + 1)
                act.activation(sqtmp[:, n], ps[:, 4 + 2 * n:6 + 2 * n, :].rearrange("p b n -> p (b n)"), ACT.Square).then_inc(osq_done, 1)
            copy_hi_tiles(4)
            for name in ("wo00", "wo01"):
                split_2nd_after(name)
            for n in range(NT):
                act.wait_ge(h_done, 3 + n)
                act.activation(sqtmp[:, n], resid[:, n], ACT.Square, accum_out=sumsq_h[:, n:n + 1]).then_inc(sumsq_done, 1)
            act.wait_ge(mem_loaded, 16)
            act.wait_ge(sumsq_done, 4)
            for n in range(NT):
                act.activation(sqtmp[:, n], memtok[:, n], ACT.Square, accum_out=sumsq_m[:, n:n + 1]).then_inc(sumsq_done, 1)
            copy_out_T(8, actT, C_N2)

            def out_scores(r):
                h0, h1 = ROUND_HEADS[r]
                for n in range(NT):
                    act.wait_ge(sub_done, NT * r + n + 1)
                    act.activation(ssb[:, n, 2 * h0:2 * h1].rearrange("p a n -> p (a n)"), ps[:, 4 + (NT * r + n) % 4, 0:2 * (h1 - h0) * P], ACT.Copy).then_inc(sub_out, 1)

            for r in range(ROUNDS):
                for h in range(*ROUND_HEADS[r]):
                    out_group(f"wq{h // 2}{h % 2}", feat(qT[:, 2 * h:2 * h + 2]), ACT.Copy)
                out_scores(r)
                if r == 1:
                    act.wait_ge(rstd_done, 5)
                    act.wait_ge(sumsq_done, 6)
                    for n in range(NT):
                        act.activation(memtok[:, n], memtok[:, n], ACT.Copy, scale=rstd_m[:, n:n + 1]).then_inc(mem_scaled, 1)
            for c in range(KC):
                act.wait_ge(mem_T, c // 2 + 1)
                act.activation(memT[:, c], ps[:, c // 2, (c % 2) * T:(c % 2 + 1) * T], ACT.Copy, scale=cols[:, C_MEM + c:C_MEM + c + 1]).then_inc(memT_done, 1)
            for k, g in enumerate(("mk0", "mk1", "mv0", "mv1")):
                out_group(g, mkv_new.rearrange("p a n -> p (a n)")[:, k * TILE:(k + 1) * TILE], ACT.Copy)
            act.activation(feat(xround.bitcast(F32R)), feat(actT), ACT.Copy).then_inc(x_split, 1)
            act.wait_ge(soft_in, 1)
            e = best.rearrange("p h n k -> p (h n k)")
            act.activation(e, e, ACT.Exp).then_inc(soft_exp, 1)
            act.wait_ge(x_split, 2)
            act.activation(xh[:].rearrange("p c t -> p (c t)"), feat(xround), ACT.Copy).then_inc(x_split, 1)

            def g_evac(n, at, b):
                act.wait_ge(g_mm, n)
                act.activation(G[:, at, :].rearrange("p t j -> p (t j)"), ps[:, b, :], ACT.Copy).then_inc(g_out, 1)

            act.wait_ge(pickT_done, 3)
            act.wait_ge(mkv_moved, 16)
            tok = lambda g: slice(g * GT, g * GT + 1)

            def distances(n, at, b):
                act.activation(dist[:, b], iota, ACT.Abs, scale=-1.0, bias=chosenT[:, 1, at]).then_inc(dist_done, 1)

            def hot_row(n, at, b):
                act.wait_ge(dist_done, n)
                act.activation(hotB[:, b, 0], dist[:, b], ACT.Relu, scale=minus_w[:, at], bias=chosenT[:, 2, at]).then_inc(onehot_by_act, 1)

            for g in range(3):
                distances(g + 1, tok(g), g)
            for g in range(2):
                hot_row(g + 1, tok(g), g)
            with act.Fori(0, NGRP // GBUF - 1) as i:
                for b in range(GBUF):
                    act.wait_ge(onehot_by_act, GBUF * i + (b + 1))
                    distances(GBUF * i + (b + 4), bass.ds(i * (GBUF * GT) + (b + 3) * GT, 1), (b + 3) % GBUF)
                    hot_row(GBUF * i + (b + 3), bass.ds(i * (GBUF * GT) + (b + 2) * GT, 1), (b + 2) % GBUF)
                    g_evac(GBUF * i + (b + 1), bass.ds(i * (GBUF * GT) + b * GT, GT), b)
            for b in range(GBUF):
                g = NGRP - GBUF + b
                if b == 0:
                    act.wait_ge(onehot_by_act, g + 1)
                    distances(g + 4, tok(g + 3), 3)
                if b < 2:
                    hot_row(g + 3, tok(g + 2), b + 2)
                g_evac(g + 1, slice(g * GT, g * GT + GT), b)

            loaded = (u_loaded, v_loaded)

            def split_hi(which, loads, par):
                act.wait_ge(loaded[which][par], loads)
                act.activation(hi[:, which, par], raw[:, which, par], ACT.Copy).then_inc(hi_done[which], 1)

            def second_key(n, loads, par, first=False, last=False, wait=True):
                if wait:
                    act.wait_ge(v_mm, n - 2)
                split_hi(V, loads, par)
                act.wait_ge(u_mm, n)
                if not first:
                    act.wait_ge(wl_done, n - 1)
                act.activation(act_j, ps[:, par, 0:T], ACT.Gelu).then_inc(gelu_done, 1)
                if not last:
                    split_hi(U, loads + 16, par)
                act.wait_ge(prod_done, n)
                if not first:
                    act.wait_ge(v_mm, n - 1)
                act.activation(wh[:], act_j, ACT.Copy).then_inc(wh_done, 1)

            for par in range(2):
                split_hi(U, 16, par)
            second_key(1, 16, 0, first=True, wait=False)
            second_key(2, 16, 1, wait=False)
            with act.Fori(1, NKEY // 2 - 1) as i:
                for par in range(2):
                    second_key(2 * i + (par + 1), 16 * i + 16, par)
            for par in range(2):
                second_key(NKEY - 1 + par, 8 * NKEY, par, last=True)
            piece_split_hi("dnq0")
            for n in range(NT):
                act.wait_ge(peer_out, 2 * n + 2)
                act.activation(probT[:, 512 + n * D:512 + (n + 1) * D], resid[:, n], ACT.Square, accum_out=sumsq_f[:, n:n + 1]).then_inc(sumsq_done, 1)
                act.wait_ge(hg_done, n + 1)
                act.activation(prob[:, n * D:(n + 1) * D], scaled2[:, n], ACT.Square, accum_out=sumsq_x[:, n:n + 1]).then_inc(sumsq_done, 1)
            piece_split_hi("dnq1")
            act.wait_ge(rows_loaded, 48)
            act.activation(ba_hi, ba_w, ACT.Copy).then_inc(ba_split, 1)
            copy_hi_T(12, C_PRE)

            def from2(g):
                act.wait_ge(g2_done, g2_no[g] + 1)
                return ps[:, g2_bank[g], :]

            def out2(g, dst, func, **kw):
                act.activation(dst, from2(g), func, **kw).then_inc(g2_out, 1)

            def flat(ap):
                return ap.rearrange("p a b -> p (a b)")

            act.wait_ge(conv_zero, 1)
            for k, name in enumerate(("dnq", "dnk", "dnv")):
                for a in range(2):
                    f = 4 * k + 2 * a
                    act.activation(convin[:, f:f + 2, CONV - 1:], from2(f"{name}{a}").rearrange("p (f t) -> p f t", f=2), ACT.Copy).then_inc(g2_out, 1)
                    split_2nd_after(f"{name}{a}")
            act.wait_ge(g2_done, g2_no["ba"] + 1)
            act.activation(flat(ba), ps[:, g2_bank["ba"], 0:2 * TH], ACT.Copy).then_inc(g2_out, 1)
            act.wait_ge(g2_out, g2_no["ba"] + 1)
            act.activation(beta, ba[:, :, 0:DH], ACT.Sigmoid).then_inc(beta_done, 1)
            for k in range(3):
                act.wait_ge(conv_done, k + 1)
                act.activation(flat(convT[:, 4 * k:4 * k + 4]), flat(convT[:, 4 * k:4 * k + 4]), ACT.Silu).then_inc(dnsilu_done, 1)
            act.wait_ge(dnsilu_done, 2)
            act.activation(flat(sqk), flat(convT[:, 0:2 * DH]), ACT.Square).then_inc(dnsilu_done, 1)
            split_2nd_after("dnz0")
            for a in range(NT):
                out2(f"dnz{a}", zdn[:, a], ACT.Silu)
            split_2nd_after("dnz1")
            act.wait_ge(dz_done, 1)
            link(act.activation(flat(dsp), flat(dz), ACT.Abs))
            link(act.activation(flat(dsp), flat(dsp), ACT.Exp, scale=-1.0))
            act.activation(flat(dsp), flat(dsp), ACT.Ln, bias=1.0)
            act.activation(nega, a_log, ACT.Exp).then_inc(dln_done, 1)
            split_2nd_after("gmu0")
            for a in range(NT):
                out2(f"gmu{a}", gu[:, a], ACT.Gelu_apprx_tanh)
            split_2nd_after("gmu1")
            act.wait_ge(gcs_done, 2)
            act.activation(flat(egc), gcs[:, 0], ACT.Exp)
            act.activation(ekd, ekd, ACT.Exp).then_inc(egc_done, 1)
            split_2nd_after("gmv0")
            for a in range(NT):
                out2(f"gmv{a}", gv2[:, a], ACT.Gelu_apprx_tanh)
            split_2nd_after("gmv1")
            act.wait_ge(g2_out, g2_no["gmv1"] + 1)
            for n in range(NT):
                act.activation(prob[:, n * TILE:(n + 1) * TILE], gv2[:, n], ACT.Square, accum_out=sumsq_v[:, n:n + 1]).then_inc(gmv_sq, 1)
            act.wait_ge(row_mm, 2)
            act.activation(flat(brow), ps[:, 6:8, :].rearrange("p b n -> p (b n)"), ACT.Copy).then_inc(brow_done, 1)
            act.wait_ge(dm_in, 1)
            act.activation(flat(qg), ps[:, 5, :], ACT.Exp)
            act.activation(flat(Dm), flat(Dm), ACT.Exp).then_inc(dm_done, 1)
            split_2nd_after("gmz0")
            for a in range(NT):
                out2(f"gmz{a}", gz[:, a], ACT.Silu)
            split_2nd_after("gmz1")
            for a in range(2):
                out2(f"swq{a}", flat(swqT[:, 2 * a:2 * a + 2]), ACT.Copy)
                split_2nd_after(f"swq{a}")
            act.wait_ge(row_mm, 3)
            act.activation(flat(qrow), ps[:, 4:6, :].rearrange("p b n -> p (b n)"), ACT.Copy).then_inc(qrow_done, 1)
            out2("swkv", swkv, ACT.Copy)
            split_2nd_after("swkv")
            act.wait_ge(x0_tr, 1)
            act.activation(flat(X), ps[:, 4:6, :].rearrange("p b n -> p (b n)"), ACT.Copy).then_inc(x_done, 1)
            for l in range(1, LEVELS):
                for n in range(NT):
                    act.wait_ge(y_mm, NT * (l - 1) + n + 1)
                    act.activation(flat(Y[:, 4 * n:4 * n + 4]), ps[:, 4 + n, :], ACT.Copy).then_inc(y_out, 1)
                if l == 3:
                    for a in range(NT):
                        out2(f"swz{a}", swz[:, a], ACT.Silu)
                if l in (4, 5):
                    out2(f"xmq{l - 4}", flat(xmqT[:, 2 * (l - 4):2 * (l - 4) + 2]), ACT.Copy)
                if l >= 2:
                    split_2nd_after(LEVEL_PIECES[l - 2])
            act.wait_ge(u_out_mm, 1)
            act.activation(flat(du), ps[:, 4:6, :].rearrange("p b n -> p (b n)"), ACT.Copy).then_inc(du_done, 1)
            act.activation(flat(wT), ps[:, 6, :], ACT.Copy).then_inc(du_done, 1)
            for a in range(NT):
                out2(f"xmz{a}", xmz[:, a], ACT.Silu)
            split_2nd_after("xmz1")

            def out_gates(n, h):
                for tau in range(NT):
                    if n >= 2:
                        act.wait_ge(up_out, 4 * (n - 2) + up_order.index((tau, h)) + 1)
                    out2(f"gate{n}{h}{tau}", gsb[:, n % 2, 2 * h + tau], ACT.Sigmoid)

            split_2nd_after("gate000")
            act.wait_ge(s1_mm, 1)
            act.activation(flat(S1), ps[:, 7, :], ACT.Copy).then_inc(s1_done, 1)
            out_gates(0, 0)
            split_2nd_after("gate001")
            for n in range(NT):
                act.wait_ge(do_mm, n + 1)
                act.activation(prob[:, n * TILE:(n + 1) * TILE], ps[:, 4 + n, :], ACT.Square).then_inc(dosq_done, 1)
            split_2nd_after("gate010")
            out_gates(0, 1)
            split_2nd_after("gate011")
            sw_rows = []
            off = 0
            for n in range(NT):
                width = (n + 1) * P
                sw_rows.append((prob[:, off:off + SH * width].rearrange("p (h j) -> p h j", h=SH), probT[:, off:off + SH * width]))
                off += SH * width

            def sw_exp(n):
                act.wait_ge(s_masked, n + 1)
                for h in range(SH):
                    act.activation(sw_rows[n][0][:, h], sw_rows[n][0][:, h], ACT.Exp, bias=snm[:, n, h:h + 1], accum_out=sden[:, n, h:h + 1])
                act.activation(ssk[:, n], ssk[:, n], ACT.Exp).then_inc(s_exp, 1)

            def sw_copy_T(n):
                act.wait_ge(s_tr, n + 1)
                act.activation(sw_rows[n][1], ps[:, (2 if n else 4):6, :].rearrange("p b n -> p (b n)"), ACT.Copy).then_inc(s_trout, 1)

            sw_exp(0)
            split_2nd_after("gate100")
            sw_exp(1)
            sw_copy_T(0)
            out_gates(1, 0)
            split_2nd_after("gate101")
            sw_copy_T(1)
            split_2nd_after("gate110")
            for n in range(NT):
                pr = prob[:, n * 1024:(n + 1) * 1024].rearrange("p (h j) -> p h j", h=XH)
                act.wait_ge(xs_max, n + 1)
                for h in range(XH):
                    ins = act.activation(pr[:, h], ps[:, 4 + 2 * n + h // 2, (h % 2) * T:(h % 2 + 1) * T], ACT.Exp, scale=HEAD ** -0.5,
                                         bias=xnm[:, n, h:h + 1], accum_out=xden[:, n, h:h + 1])
                ins.then_inc(xs_exp, 1)
            out_gates(1, 1)
            split_2nd_after("gate111")
            for n in range(NT):
                prT = probT[:, n * 1024:(n + 1) * 1024]
                act.wait_ge(xs_tr, n + 1)
                act.activation(prT, ps[:, 4 + 2 * n:6 + 2 * n, :].rearrange("p b n -> p (b n)"), ACT.Copy).then_inc(xs_trout, 1)
            for n in range(NBR):
                act.wait_ge(yT_mm, n + 1)
                b = 4 + 2 * (n % 2)
                act.activation(yh[:, 4 * n:4 * n + 4].rearrange("p c t -> p (c t)"), ps[:, b:b + 2, :].rearrange("p b n -> p (b n)"), ACT.Copy).then_inc(yT_hi, 1)
            for j in range(NBR):
                n, h = 2 + j // 2, j % 2
                split_2nd_after(f"gate{n}{h}0")
                split_2nd_after(f"gate{n}{h}1")
                if j == NBR - 1:
                    out_gates(n, h)
                split_2nd_after(f"up{j}0")
                split_2nd_after(f"up{j}1")
                if j < NBR - 1:
                    out_gates(n, h)
            copy_hi_tiles(16)
            for name in ("out00", "out01"):
                split_2nd_after(name)
            for h in range(2):
                for n in range(NT):
                    act.wait_ge(fin_mm, 2 * h + n + 1)
                    act.activation(outsb[:, n, h * TILE:(h + 1) * TILE], ps[:, 2 * h + n, :], ACT.Copy).then_inc(fin_copied, 1)
            for n in range(NT):
                act.wait_ge(fin_copied, NT + n + 1)
                act.activation(gsb[:, n, 0:2].rearrange("p a d -> p (a d)"), outsb[:, n], ACT.Square, accum_out=sumsq_p[:, n:n + 1]).then_inc(sumsq_done, 1)

        @block.vector
        def _(dve):
            steps = [0]

            def link(ins):
                steps[0] += 1
                ins.then_inc(dve_step, 1)
                dve.wait_ge(dve_step, steps[0])

            def mark(ins):
                steps[0] += 1
                ins.then_inc(dve_step, 1)

            def wait_marked():
                dve.wait_ge(dve_step, steps[0])

            mark(dve.memset(own, 0.0))
            mark(dve.memset(qd, 0.0))
            mark(dve.memset(kd, 0.0))
            dve.wait_ge(params_loaded, 64)
            logit = cols[:, C_LOG:C_LOG + 8].rearrange("p (a f) -> p a f", a=2)
            link(dve.tensor_tensor(lbm, logit[:, 0], logit[:, 1], ALU.max))
            dve.tensor_tensor(lbe, logit, bcast(lbm, 1, 2), ALU.subtract).then_inc(lb_in, 1)
            for n in range(NT):
                dve.wait_ge(rstd_done, 1 + n)
                dve.tensor_scalar(scaled[:, n], resid[:, n], rstd[:, n:n + 1], None, ALU.mult).then_inc(scaled_done, 1)
            dve.wait_ge(params_loaded, 64)

            def copy_out_T(n_before, dst, gcol):
                for c in (0, 1, 4, 5):
                    dve.wait_ge(transposed, n_before + c // 2 + 1)
                    src = ps[:, 4 + c // 2, (c % 2) * T:(c % 2 + 1) * T]
                    dve.tensor_scalar(dst[:, c], src, cols[:, gcol + c:gcol + c + 1], None, ALU.mult).then_inc(actT_done[1], 1)

            def copy_lo_T(rounded_before, gcol):
                for c in range(KC):
                    dve.wait_ge(actT_done[0], rounded_before + 2 * (c // 2) + 2)
                    src = ps[:, 4 + c // 2, (c % 2) * T:(c % 2 + 1) * T]
                    dve.scalar_tensor_tensor(xl[:, c], src, cols[:, gcol + c:gcol + c + 1], xh[:, c].bitcast(F32), ALU.mult, ALU.subtract).then_inc(actT_done[1], 1)

            def copy_lo_tiles(rounded_before, *names):
                for n in range(NT):
                    for half in range(2):
                        dve.wait_ge(actT_done[0], rounded_before + 2 * n + half + 1)
                        cut = (slice(None), slice(4 * half, 4 * half + 4), slice(n * P, (n + 1) * P))
                        dve.tensor_tensor(xl[cut], ps[:, 4 + 2 * n + half, :].rearrange("p (c t) -> p c t", c=4), xh[cut].bitcast(F32), ALU.subtract).then_inc(actT_done[1], 1)
                    if n == 0:
                        piece_split_lo(*names)

            def piece_split_lo(*names):
                for name in names:
                    dve.wait_ge(piece_hi, piece_no[name] + 1)
                    dve.tensor_tensor(part_of(lo2, name), raw_piece(name), part_of(hi2, name).bitcast(F32), ALU.subtract).then_inc(piece_lo, 1)

            piece_split_lo("hq0")
            copy_lo_T(0, C_N1)
            piece_split_lo("hq1")
            dve.wait_ge(consts_made, 1)
            link(dve.tensor_tensor(xx, xi, xj, ALU.bitwise_xor))
            link(dve.tensor_copy(xf, xx))
            link(dve.tensor_tensor(xf, xf, upper[:], ALU.mult))
            for l in range(LEVELS + 1):
                mark(dve.tensor_scalar(ge[:, l], xf, float(1 << l), None, ALU.is_ge))
            wait_marked()
            dve.tensor_tensor(masks[:, 0:LEVELS], ge[:, 0:LEVELS], ge[:, 1:LEVELS + 1], ALU.subtract)
            dve.tensor_copy(masks[:, LEVELS], ident[:]).then_inc(masks_done, 1)
            piece_split_lo("hf0")
            dve.wait_ge(lb_exp, 1)
            link(dve.tensor_tensor(lbs, lbe[:, 0], lbe[:, 1], ALU.add))
            link(dve.reciprocal(lbr, lbs))
            link(dve.tensor_tensor(lb, lbe[:, 0], lbr, ALU.mult))
            link(dve.tensor_scalar(lb1, lb, -1.0, 1.0, ALU.mult, ALU.add))
            piece_split_lo("hf1", "gqk0")
            dve.wait_ge(group_out, group_no["hf1"] + 1)
            for f in range(4):
                mark(dve.tensor_scalar(gF[:, f], gF[:, f], lb1[:, f:f + 1], lb[:, f:f + 1], ALU.mult, ALU.add))
            wait_marked()
            dve.tensor_scalar(kF[:, 0:4], gF[:, 0:4], -1.0, 1.0, ALU.mult, ALU.add).then_inc(fgate_done, 1)
            piece_split_lo("gqk1", "glow", "hi0", "hi1")
            dve.wait_ge(softplus_done, 1)
            link(dve.tensor_scalar(zg, zg, 0.0, 1.0 / GATE_NORM, ALU.min, ALU.mult))
            link(dve.scalar_tensor_tensor(gF[:, 4:6], zabs, -1.0 / GATE_NORM, zg, ALU.mult, ALU.add))
            piece_split_lo("gv0")
            dve.wait_ge(logf_done, 1)
            for f in range(NF):
                for n in range(NT):
                    tok = slice(n * P, n * P + P)
                    dve.tensor_tensor_scan(cum[:, f, tok], ones, gF[:, f, tok], 0.0, ALU.mult, ALU.add).then_inc(cum_done, 1)

            piece_split_lo("gv1", "hgate0")

            def keep(n, mask):
                for k in range(4):
                    tau, half = k // 2, k % 2
                    dve.wait_ge(lvl_scores, 2 * n + tau + 1)
                    if n:
                        dve.wait_ge(lvl_kept, 4 * (n - 1) + k + 1)
                    dve.copy_predicated(own[:, tau, 4 * half:4 * half + 4, :], bcast(mask, 1, 4),
                                        ps[:, 4 + k, :].rearrange("p (h i) -> p h i", h=4)).then_inc(lvl_kept, 1)

            for l in range(LEVELS + 1):
                m = 1 << l
                b = l % 2
                dve.wait_ge(lvl_decay, l + 1)
                if l >= 2:
                    dve.wait_ge(lvl_scores, 2 * l)
                half = lambda a: a.rearrange("p f (b two m) -> p (f b) two m", two=2, m=m)
                dve.tensor_tensor(half(qd[:, b])[:, :, 1, :], half(qF)[:, :, 1, :], half(dec[:, b])[:, :, 1, :], ALU.mult)
                dve.tensor_tensor(half(kd[:, b])[:, :, 0, :], half(kF)[:, :, 0, :], half(dec[:, b])[:, :, 0, :], ALU.mult).then_inc(lvl_scaled, 1)
                if l == 0:
                    dve.wait_ge(masks_done, 1)
                    piece_split_lo("hgate1")
                keep(l, masks[:, LEVELS if l == 0 else l - 1])
                if 1 <= l <= 4:
                    piece_split_lo(next_piece(LEVEL_PIECES1[l - 1], 2))
            dve.wait_ge(group_out, group_no["ggate1"] + 1)
            for n in range(NT):
                for a in range(2):
                    g = gate1[:, n, a * TILE:(a + 1) * TILE].rearrange("p (h v) -> p h v", h=4)
                    mark(dve.tensor_tensor(g, g, bcast(gnorm[:, a], 1, 4), ALU.mult))
            for n in range(NT):
                dve.wait_ge(osq_done, n + 1)
                dve.tensor_reduce(sumsq_o[:, n], sqtmp[:, n].rearrange("p (h v) -> p h v", h=HEADS1), AX.X, ALU.add).then_inc(osum_done, 1)
            wait_marked()
            for n in range(NT):
                dve.wait_ge(orstd_done, n + 1)
                for h in range(HEADS1):
                    dve.scalar_tensor_tensor(mixed[:, n, h * P:(h + 1) * P], ps[:, 4 + 2 * n + h // 4, (h % 4) * P:(h % 4 + 1) * P],
                                             rstd_o[:, n, h:h + 1], gate1[:, n, h * P:(h + 1) * P], ALU.mult, ALU.mult).then_inc(mixed_done, 1)
            copy_lo_tiles(8)
            piece_split_lo("wo10", "wo11")
            for k in range(4):
                half, n = k // 2, k % 2
                dve.wait_ge(wout_done, k + 1)
                part = resid[:, n, half * TILE:(half + 1) * TILE]
                dve.tensor_tensor(part, part, ps[:, k, :], ALU.add).then_inc(h_done, 1)
            for n in range(NT):
                dve.wait_ge(rstd_done, 3 + n)
                dve.tensor_scalar(scaled_p[:, n], resid[:, n], rstd_h[:, n:n + 1], None, ALU.mult).then_inc(scaled_done, 1)
            copy_out_T(8, actT, C_N2)
            iota16 = iota[:, 0:TOP]

            def round_picks(r, a):
                h0, h1 = ROUND_HEADS[r]
                rows = pick[:, r % 2, a, rows_of(r)].rearrange("p (h n) k m -> p h n k m", n=NT)
                for n in range(NT):
                    mark(dve.tensor_reduce(chosen[:, n, a, h0 * TOP:h1 * TOP].rearrange("p (h k) -> p h k", k=TOP), rows[:, :, n], AX.X, ALU.add))

            for r in range(ROUNDS):
                pairs = [(h, n) for h in range(*ROUND_HEADS[r]) for n in range(NT)]
                halves = [(ssb[:, n, 2 * h + a], srest[:, a, k], stop_[:, a, h, n], sidx[:, a, h, n]) for k, (h, n) in enumerate(pairs) for a in range(2)]
                rows, count = rows_of(r), len(pairs)
                dve.wait_ge(sub_out, NT * r + NT)
                for score, rest, top, index in halves:
                    mark(dve.max(top[:, 0:8], score))
                wait_marked()
                for score, rest, top, index in halves:
                    mark(dve.max_index(index[:, 0:8], top[:, 0:8], score))
                    mark(dve.match_replace(rest, top[:, 0:8], score, NEG))
                wait_marked()
                for score, rest, top, index in halves:
                    mark(dve.max(top[:, 8:16], rest))
                wait_marked()
                for score, rest, top, index in halves:
                    mark(dve.max_index(index[:, 8:16], top[:, 8:16], rest))
                first, second = (pairs_of(stop_[:, a], r) for a in range(2))
                for at, a0, a1, nb in ((0, 0, FULL, TOP), (FULL * TOP, FULL, TOP, 4)):
                    mark(dve.tensor_tensor(cand[:, rows, at:at + (a1 - a0) * nb].rearrange("p c (a b) -> p c a b", b=nb),
                                           bcast(first[:, :, a0:a1], 3, nb), bcast(second[:, :, 0:nb], 2, a1 - a0), ALU.add))
                wait_marked()
                for a in range(2):
                    mark(dve.tensor_copy(pairs_of(sidxf[:, a], r), pairs_of(sidx[:, a], r)))
                for k, (h, n) in enumerate(pairs):
                    mark(dve.max(best[:, h, n, 0:8], cand[:, k]))
                wait_marked()
                for k, (h, n) in enumerate(pairs):
                    mark(dve.max_index(pos[:, h, n, 0:8], best[:, h, n, 0:8], cand[:, k]))
                    mark(dve.match_replace(crest[:, k], best[:, h, n, 0:8], cand[:, k], NEG))
                wait_marked()
                for k, (h, n) in enumerate(pairs):
                    mark(dve.max(best[:, h, n, 8:16], crest[:, k]))
                wait_marked()
                for k, (h, n) in enumerate(pairs):
                    mark(dve.max_index(pos[:, h, n, 8:16], best[:, h, n, 8:16], crest[:, k]))
                if r:
                    for a in range(2):
                        dve.wait_ge(pick_kept, 2 * (r - 1) + a + 1)
                        round_picks(r - 1, a)
                wait_marked()
                if r == ROUNDS - 1:
                    top1 = einv
                    link(dve.tensor_copy(top1, best[:, :, :, 0]))
                    dve.tensor_tensor(best, best, bcast(top1, 3, TOP), ALU.subtract).then_inc(soft_in, 1)
                for k, shift in enumerate((0, 2, 4)):
                    mark(dve.tensor_scalar(posi[:, k, rows], pairs_of(pos, r), shift, None, ALU.logical_shift_right))
                wait_marked()
                link(dve.tensor_copy(posf[:, :, rows], posi[:, :, rows]))
                p1, p4, p16 = (posf[:, k, rows] for k in range(3))
                link(dve.scalar_tensor_tensor(place[:, 0, rows], p4, float(FULL * TOP // 4 - FULL), p16, ALU.subtract, ALU.max))
                link(dve.tensor_scalar(p4, place[:, 0, rows], 4.0, float(FULL * TOP - 4 * FULL), ALU.mult, ALU.add))
                link(dve.scalar_tensor_tensor(p4, place[:, 0, rows], float(TOP), p4, ALU.mult, ALU.min))
                link(dve.tensor_tensor(place[:, 1, rows], p1, p4, ALU.subtract))
                for a in range(2):
                    ins = dve.tensor_tensor(pick[:, r % 2, a, rows], bcast(place[:, a, rows], 3, TOP), bcast(bcast(iota16, 1, TOP), 1, count), ALU.is_equal)
                    ins.then_inc(matched, 1)
            dve.wait_ge(matched, 2 * ROUNDS)
            for a in range(2):
                view = pick[:, (ROUNDS - 1) % 2, a, rows_of(ROUNDS - 1)]
                mark(dve.tensor_tensor(view, view, round_keys(ROUNDS - 1, a), ALU.mult))
            wait_marked()
            for a in range(2):
                round_picks(ROUNDS - 1, a)
            dve.wait_ge(soft_exp, 1)
            link(dve.tensor_reduce(esum, best, AX.X, ALU.add))
            link(dve.reciprocal(einv, esum))
            for n in range(NT):
                dve.tensor_tensor(chosen[:, n, 2].rearrange("p (h k) -> p h k", h=PH), best[:, :, n], bcast(einv[:, :, n], 2, TOP), ALU.mult).then_inc(picks_done, 1)
            for n in range(NT):
                dve.wait_ge(pick_mm, n + 1)
                dve.tensor_copy(chosenT[:, :, n * P:(n + 1) * P], ps[:, n, 0:3 * P].rearrange("p (a t) -> p a t", a=3)).then_inc(pickT_done, 1)
            dve.wait_ge(pickT_done, 2)
            dve.tensor_scalar(minus_w, chosenT[:, 2], -1.0, None, ALU.mult).then_inc(pickT_done, 1)
            dve.wait_ge(pickT_done, 3)

            def onehots(at, at1, buf):
                dve.tensor_tensor(hotA[:, buf], bcast(iota, 1, GT), bcast(chosenT[:, 0, at], 2, NKEY), ALU.is_equal)
                dve.tensor_tensor(matchB[:, buf, 1:GT], bcast(iota, 1, GT - 1), bcast(chosenT[:, 1, at1], 2, NKEY), ALU.is_equal).then_inc(onehot_ready, 1)

            for b in range(GBUF):
                onehots(slice(b * GT, b * GT + GT), slice(b * GT + 1, b * GT + GT), b)
            with dve.Fori(1, NGRP // GBUF) as i:
                for b in range(GBUF):
                    dve.wait_ge(g_mm, GBUF * i + (b + 1 - GBUF))
                    onehots(bass.ds(i * (GBUF * GT) + b * GT, GT), bass.ds(i * (GBUF * GT) + (b * GT + 1), GT - 1), b)
            dve.wait_ge(g_out, NGRP)

            def split_lo(which, n, par):
                dve.wait_ge(hi_done[which], n)
                dve.tensor_tensor(lo[:, which, par], raw[:, which, par], hi[:, which, par].bitcast(F32), ALU.subtract).then_inc(lo_done[which], 1)

            def second_key(n, at, par, last=False):
                split_lo(V, n, par)
                dve.wait_ge(gelu_done, n)
                dve.tensor_tensor(act_j, act_j, G[:, :, at].rearrange("p t j -> p (t j)"), ALU.mult).then_inc(prod_done, 1)
                if not last:
                    split_lo(U, n + 2, par)
                dve.wait_ge(wh_done, n)
                dve.tensor_tensor(wl[:], act_j, wh[:].bitcast(F32), ALU.subtract).then_inc(wl_done, 1)

            for par in range(2):
                split_lo(U, par + 1, par)
            for n in range(2):
                second_key(n + 1, slice(n, n + 1), n)
            with dve.Fori(1, NKEY // 2 - 1) as i:
                for par in range(2):
                    second_key(2 * i + (par + 1), bass.ds(2 * i + par, 1), par)
            for n in range(NKEY - 2, NKEY):
                second_key(n + 1, slice(n, n + 1), n % 2, last=True)
            piece_split_lo("dnq0")
            dve.wait_ge(v_mm, NKEY)
            for n in range(NT):
                for half in range(2):
                    part = resid[:, n, half * TILE:(half + 1) * TILE]
                    dve.tensor_tensor(part, part, ps[:, 4 + 2 * n + half, :], ALU.add).then_inc(peer_out, 1)
                dve.wait_ge(peer_out, 2 * n + 2)
                dve.wait_ge(x_then_norm_f_loaded, 32)
                dve.tensor_tensor(scaled2[:, n], resid[:, n], norm_f, ALU.mult).then_inc(hg_done, 1)
            dve.wait_ge(hg_done, NT)
            for n in range(NT):
                dve.wait_ge(rstd_done, 6 + n)
                dve.tensor_scalar(scaled2[:, n], scaled2[:, n], rstd_x[:, n:n + 1], None, ALU.mult).then_inc(scaled_done, 1)
            copy_lo_T(16, C_PRE)
            for n in range(NT):
                mark(dve.scalar_tensor_tensor(resid[:, n], resid[:, n], rstd_f[:, n:n + 1], norm_f, ALU.mult, ALU.mult))
            dve.wait_ge(ba_split, 1)
            dve.tensor_tensor(ba_lo, ba_w, ba_hi.bitcast(F32), ALU.subtract).then_inc(ba_split, 1)
            dve.wait_ge(transposed, 16)
            dve.memset(convin[:, :, 0:CONV - 1], 0.0).then_inc(conv_zero, 1)
            piece_split_lo("dnq1", "dnk0", "dnk1")
            for k, name in enumerate(("dnq", "dnk", "dnv")):
                dve.wait_ge(g2_out, g2_no[name + "1"] + 1)
                for tap in reversed(range(CONV)):
                    for f in range(4 * k, 4 * k + 4):
                        w = cols[:, C_CONV + tap * 12 + f:C_CONV + tap * 12 + f + 1]
                        src = convin[:, f, tap:tap + T]
                        if tap == CONV - 1:
                            mark(dve.tensor_scalar(convT[:, f], src, w, None, ALU.mult))
                        elif tap:
                            mark(dve.scalar_tensor_tensor(convT[:, f], src, w, convT[:, f], ALU.mult, ALU.add))
                        else:
                            ins = dve.scalar_tensor_tensor(convT[:, f], src, w, convT[:, f], ALU.mult, ALU.add)
                    wait_marked()
                    if tap == 2 and name != "dnv":
                        piece_split_lo({"dnq": "dnv0", "dnk": "dnz0"}[name])
                ins.then_inc(conv_done, 1)
                if name != "dnv":
                    piece_split_lo({"dnq": "dnv1", "dnk": "dnz1"}[name])
            dve.wait_ge(g2_out, g2_no["ba"] + 1)
            dve.tensor_tensor(dz, ba[:, :, DH:2 * DH], bcast(dt_bias, 1, NT), ALU.add).then_inc(dz_done, 1)
            piece_split_lo("gmu0", "gmu1")
            dve.wait_ge(dln_done, 1)
            link(dve.scalar_tensor_tensor(dsp, dz, 0.0, dsp, ALU.max, ALU.add))
            dve.scalar_tensor_tensor(dg, dsp, -1.0, bcast(nega, 1, NT), ALU.mult, ALU.mult).then_inc(dg_done, 1)
            piece_split_lo("gmv0")
            dve.wait_ge(ss_mm, 1)
            dve.tensor_scalar(rin.rearrange("p n f -> p (n f)"), ps[:, 4, 0:2 * TH], EPS, None, ALU.add).then_inc(rin_done, 1)
            piece_split_lo("gmv1")
            dve.wait_ge(rr_done, 1)
            dve.wait_ge(beta_done, 1)
            mark(dve.tensor_tensor(brk, beta, rr[:, :, DH:2 * DH], ALU.mult))
            mark(dve.tensor_scalar(rqs, rr[:, :, 0:DH], HEAD ** -0.5, None, ALU.mult))
            dve.wait_ge(dg_done, 1)
            wait_marked()
            for a, v in enumerate((dg, brk, rqs)):
                ins = dve.tensor_copy(rep[:, a], bcast(v.rearrange("p n h -> p (n h)"), 2, P))
            ins.then_inc(rep_done, 1)
            dve.wait_ge(gc_mm, 1)
            dve.tensor_copy(gcs, ps[:, 5, 0:2 * TH].rearrange("p (a h) -> p a h", a=2)).then_inc(gcs_done, 1)
            dve.wait_ge(gcs_done, 1)
            dve.tensor_tensor(ekd, gcs[:, 1, 0:DH], gcs[:, 0, 0:DH], ALU.subtract).then_inc(gcs_done, 1)
            piece_split_lo("gmz0")
            dve.wait_ge(row_mm, 1)
            for th in range(TH):
                ins = dve.tensor_scalar(Dm[:, th], ps[:, 4 + th // DH, (th % DH) * P:(th % DH + 1) * P], gcs[:, 0, th:th + 1], 0.0, ALU.subtract, ALU.min)
            ins.then_inc(dm_in, 1)
            dve.wait_ge(egc_done, 1)
            mark(dve.tensor_tensor(kbf, brk, egc, ALU.mult))
            mark(dve.tensor_tensor(ekd, ekd, rr[:, 0, DH:2 * DH], ALU.mult))
            wait_marked()
            piece_split_lo("gmz1")
            dve.wait_ge(rows_loaded, 48)
            link(dve.tensor_tensor(window[:, 0], ident[:], upper[:], ALU.subtract))
            link(dve.tensor_scalar(window[:, 0], window[:, 0], 1.0, None, ALU.add))
            mark(dve.tensor_scalar(window[:, 1], window[:, 0], -MASKED, MASKED, ALU.mult, ALU.add))
            wait_marked()
            mark(dve.tensor_scalar(window[:, 0], window[:, 0], MASKED, None, ALU.mult))
            mark(dve.tensor_tensor(wsT, wsT, bcast(upper[:], 1, 4), ALU.mult))
            dve.wait_ge(gmv_rstd, 1)
            for n in range(NT):
                dve.scalar_tensor_tensor(gv2[:, n], gv2[:, n], rstd_v[:, n:n + 1], gm_gain, ALU.mult, ALU.mult).then_inc(gmv_done, 1)

            def head_cols(k):
                return slice((k % DH) * P, (k % DH + 1) * P)

            piece_split_lo("swq0", "swq1")
            dve.wait_ge(dm_done, 1)
            dve.wait_ge(kk_mm, 1)
            for th in range(TH):
                mark(dve.scalar_tensor_tensor(LT[:, th], ps[:, 6 + th // DH, head_cols(th)], rr[:, th // DH, DH + th % DH:DH + th % DH + 1], Dm[:, th], ALU.mult, ALU.mult))
            dve.wait_ge(brow_done, 1)
            wait_marked()
            dve.tensor_tensor(LT, LT, brow, ALU.mult).then_inc(lt_done, 1)
            piece_split_lo("swkv")
            dve.wait_ge(lt_done, 1)
            link(dve.tensor_tensor(BT, LT, bcast(masks[:, 0], 1, TH), ALU.mult))
            dve.tensor_tensor(Z, bcast(ident[:], 1, TH), BT, ALU.subtract).then_inc(z0_done, 1)
            def off_diagonal(l):
                dve.tensor_tensor(BT, LT, bcast(masks[:, l], 1, TH), ALU.mult).then_inc(bt_done, 1)

            dve.wait_ge(z0_done, 1)
            off_diagonal(1)
            dve.wait_ge(kv_tr, 1)
            for h in range(DH):
                dve.tensor_scalar(kdl[:, h], ps[:, 6, head_cols(h)], ekd[:, h:h + 1], None, ALU.mult)
            for th in range(TH):
                n, h = th // DH, th % DH
                ins = dve.tensor_scalar(kbg[:, th], ps[:, 6 + n, head_cols(th)], kbf[:, n, h:h + 1], None, ALU.mult)
            ins.then_inc(kv_out, 1)
            dve.wait_ge(kv_tr, 2)
            for th in range(TH):
                n, h = th // DH, th % DH
                ins = dve.tensor_scalar(vb[:, th], ps[:, 6 + n, head_cols(th)], beta[:, n, h:h + 1], None, ALU.mult)
            ins.then_inc(kv_out, 1)
            piece_split_lo("swz0", "swz1")
            for l in range(1, LEVELS):
                if l < LEVELS - 1:
                    dve.wait_ge(y_mm, NT * l)
                    off_diagonal(l + 1)
                for n in range(NT):
                    part = slice(DH * n, DH * n + DH)
                    dve.wait_ge(pz_mm, NT * (l - 1) + n + 1)
                    if l < LEVELS - 1:
                        dve.tensor_tensor(X[:, part], X[:, part], ps[:, 6 + n, :].rearrange("p (h c) -> p h c", h=DH), ALU.subtract).then_inc(x_done, 1)
                    dve.tensor_tensor(Z[:, part], Z[:, part], ps[:, 4 + n, :].rearrange("p (h c) -> p h c", h=DH), ALU.subtract).then_inc(z_done, 1)
                if l >= 2:
                    piece_split_lo(next_piece(LEVEL_PIECES[l - 2], 2))
            dve.wait_ge(qk_mm, 1)
            for th in range(TH):
                mark(dve.scalar_tensor_tensor(AQ[:, th], ps[:, 6 + th // DH, head_cols(th)], rr[:, th // DH, DH + th % DH:DH + th % DH + 1], Dm[:, th], ALU.mult, ALU.mult))
            dve.wait_ge(qrow_done, 1)
            wait_marked()
            link(dve.tensor_tensor(AQ, AQ, qrow, ALU.mult))
            dve.tensor_tensor(AQ, AQ, bcast(upper[:], 1, TH), ALU.mult).then_inc(aq_done, 1)
            link(dve.tensor_tensor(qg, qg, qrow[:, DH:TH], ALU.mult))
            dve.tensor_tensor(qg, qg, convT[:, 0:DH, P:T], ALU.mult).then_inc(qg_done, 1)
            piece_split_lo(next_piece("xmz1", 2))
            piece_split_lo("gate010")
            for n in range(NT):
                dve.wait_ge(gm_mm, n + 1)
                for g in range(4):
                    part = gu[:, n, g * P:(g + 1) * P]
                    mark(dve.scalar_tensor_tensor(part, ps[:, 2 + n, g * P:(g + 1) * P], cols[:, C_SB + g:C_SB + g + 1], part, ALU.add, ALU.mult))
                wait_marked()
                dve.tensor_tensor(gu[:, n], gu[:, n], gz[:, n], ALU.mult).then_inc(y_done[1], 1)
            for n in range(NT):
                zz = zdn[:, n].rearrange("p (h v) -> p h v", h=DH)
                mark(dve.tensor_tensor(zz, zz, bcast(dn_gain, 1, DH), ALU.mult))
            dve.wait_ge(ws_mm, 1)
            dve.wait_ge(du_done, 1)
            dve.tensor_tensor(vnew, du[:, DH:TH], ps[:, 6, :].rearrange("p (h c) -> p h c", h=DH), ALU.subtract).then_inc(vnew_done, 1)
            piece_split_lo("gate011")
            for n in range(NT):
                dve.wait_ge(dosq_done, n + 1)
                dve.tensor_reduce(sumsq_a[:, n], prob[:, n * TILE:(n + 1) * TILE].rearrange("p (h v) -> p h v", h=DH), AX.X, ALU.add).then_inc(dosum_done, 1)
            wait_marked()
            for n in range(NT):
                dve.wait_ge(dors_done, n + 1)
                for h in range(DH):
                    part = zdn[:, n, h * P:(h + 1) * P]
                    ins = dve.scalar_tensor_tensor(part, ps[:, 4 + n, h * P:(h + 1) * P], rstd_a[:, n, h:h + 1], part, ALU.mult, ALU.mult)
                ins.then_inc(y_done[0], 1)
            piece_split_lo("gate100")
            off = 0
            for n in range(NT):
                width = (n + 1) * P
                pr = prob[:, off:off + SH * width].rearrange("p (h j) -> p h j", h=SH)
                off += SH * width
                banks, per = SW_BANKS[n], SH // len(SW_BANKS[n])
                add = window[:, 1] if n == 0 else window.rearrange("p a j -> p (a j)")
                dve.wait_ge(ss_mm2, n + 1)
                for b in range(SH // per):
                    mark(dve.scalar_tensor_tensor(pr[:, per * b:per * b + per], ps[:, banks[b], :].rearrange("p (h j) -> p h j", h=per), SHD ** -0.5,
                                                  bcast(add, 1, per), ALU.mult, ALU.add))
                wait_marked()
                link(dve.tensor_reduce(smax[:, n], pr, AX.X, ALU.max))
                link(dve.tensor_tensor(smax[:, n], smax[:, n], sinks, ALU.max))
                mark(dve.tensor_tensor(ssk[:, n], sinks, smax[:, n], ALU.subtract))
                dve.tensor_scalar(snm[:, n], smax[:, n], -1.0, None, ALU.mult).then_inc(s_masked, 1)
                piece_split_lo("gate101" if n == 0 else "gate110")
            for n in range(NT):
                dve.wait_ge(s_exp, n + 1)
                link(dve.tensor_tensor(sden[:, n], sden[:, n], ssk[:, n], ALU.add))
                link(dve.reciprocal(srec[:, n], sden[:, n]))
                if n == 0:
                    piece_split_lo("gate111")
                dve.wait_ge(so_mm, n + 1)
                for h in range(SH):
                    part = swz[:, n, h * SHD:(h + 1) * SHD]
                    ins = dve.scalar_tensor_tensor(part, ps[:, 6 + n, h * SHD:(h + 1) * SHD], srec[:, n, h:h + 1], part, ALU.mult, ALU.mult)
                ins.then_inc(y_done[2], 1)
            for n in range(NT):
                dve.wait_ge(xs_mm, n + 1)
                link(dve.tensor_reduce(xmax[:, n], ps[:, 4 + 2 * n:6 + 2 * n, :].rearrange("p b (h j) -> p (b h) j", h=2), AX.X, ALU.max))
                dve.tensor_scalar(xnm[:, n], xmax[:, n], -(HEAD ** -0.5), None, ALU.mult).then_inc(xs_max, 1)
            piece_split_lo("gate200")
            for n in range(NT):
                dve.wait_ge(xs_exp, n + 1)
                link(dve.reciprocal(xrec[:, n], xden[:, n]))
                dve.wait_ge(xo_mm, n + 1)
                for h in range(XH):
                    part = xmz[:, n, h * HEAD:(h + 1) * HEAD]
                    ins = dve.scalar_tensor_tensor(part, ps[:, 2 + n, h * HEAD:(h + 1) * HEAD], xrec[:, n, h:h + 1], part, ALU.mult, ALU.mult)
                ins.then_inc(y_done[3], 1)
            piece_split_lo("gate201")
            for n in range(NBR):
                dve.wait_ge(yT_hi, n + 1)
                b = 4 + 2 * (n % 2)
                dve.tensor_tensor(yl[:, 4 * n:4 * n + 4].rearrange("p c t -> p (c t)"), ps[:, b:b + 2, :].rearrange("p b n -> p (b n)"),
                                  yh[:, 4 * n:4 * n + 4].rearrange("p c t -> p (c t)").bitcast(F32), ALU.subtract).then_inc(yT_done, 1)
            for n in range(NBR):
                piece_split_lo(f"up{n}0", f"up{n}1")
                for k, (tau, half) in enumerate(up_order):
                    if k == 2 and n < NBR - 1:
                        piece_split_lo(next_piece(f"up{n}0", 2))
                    if k == 3 and n == NBR - 1:
                        piece_split_lo("out00")
                    dve.wait_ge(up_mm, 4 * n + k + 1)
                    dve.wait_ge(g2_out, g2_no[f"gate{n}{half}{tau}"] + 1)
                    part_sum = merged[:, tau, half * TILE:(half + 1) * TILE]
                    g = gsb[:, n % 2, 2 * half + tau]
                    if n == 0:
                        dve.tensor_tensor(part_sum, g, ps[:, 4 + k, :], ALU.mult).then_inc(up_out, 1)
                    else:
                        link(dve.tensor_tensor(g, g, ps[:, 4 + k, :], ALU.mult))
                        dve.wait_ge(up_out, 4 * (n - 1) + up_order.index((tau, half)) + 1)
                        dve.tensor_tensor(part_sum, part_sum, g, ALU.add).then_inc(merged_done if n == NBR - 1 else up_out, 1)
                if n < NBR - 1:
                    piece_split_lo(next_piece(f"up{n}1", 2))
            copy_lo_tiles(24, "out01")
            piece_split_lo("out10", "out11")
            dve.wait_ge(rows_loaded, 64)
            for n in range(NT):
                dve.wait_ge(fin_copied, NT + n + 1)
                mark(dve.tensor_tensor(merged[:, n], outsb[:, n], norm_post, ALU.mult))
                dve.wait_ge(rstd_done, 8 + n)
                wait_marked()
                dve.scalar_tensor_tensor(outsb[:, n], merged[:, n], rstd_p[:, n:n + 1], resid[:, n], ALU.mult, ALU.add).then_inc(out_done, 1)

        @block.tensor
        def _(pe):
            def transpose_by_tile(src, tile_ready):
                for n in range(NT):
                    tile_ready(n)
                    for c in range(KC):
                        ins = pe.transpose(ps[:, 4 + c // 2, (c % 2) * T + n * P:(c % 2) * T + (n + 1) * P], src[:, n, c * P:(c + 1) * P], ident[:])
                        if n == NT - 1 and c % 2:
                            ins.then_inc(transposed, 1)

            def transpose_to_tiles(src, tile_ready):
                for n in range(NT):
                    tile_ready(n)
                    for c in range(KC):
                        ins = pe.transpose(ps[:, 4 + 2 * n + c // 4, (c % 4) * P:(c % 4 + 1) * P], src[:, n, c * P:(c + 1) * P], ident[:])
                        if c % 4 == 3:
                            ins.then_inc(transposed, 1)

            def need(name):
                pe.wait_ge(tile_loaded[slot(name)], 16 * (loads_p[slot(name)] + tile_no[name] // RING + 1))

            def bank_free(g):
                k = group_no[g]
                if k >= 4:
                    pe.wait_ge(group_out, k - 3)

            def features(name, xT, subs):
                need(name)
                w = tile_view(name)
                for s in subs:
                    g = f"{name}{s}"
                    bank_free(g)
                    for a in range(2):
                        f0 = (2 * s + a) * P
                        for c in range(KC):
                            ins = pe.matmul(ps[:, gbank(g), a * T:(a + 1) * T], w[:, c, f0:f0 + P], xT[:, c, :], start=(c == 0), stop=(c == KC - 1))
                    ins.then_inc(group_done, 1)

            def tokens(name, xT):
                need(name)
                w = tile_view(name)
                for n in range(NT):
                    g = f"{name}{n}"
                    bank_free(g)
                    for c in range(KC):
                        ins = pe.matmul(ps[:, gbank(g), :], xT[:, c, n * P:(n + 1) * P], w[:, c, :], start=(c == 0), stop=(c == KC - 1))
                    ins.then_inc(group_done, 1)

            FRESH = {"hq0": 0, "dnq0": 16}

            def bank_for2(g):
                before = [k for k in range(g2_no[g]) if g2_bank[groups2[k]] == g2_bank[g]]
                if before:
                    pe.wait_ge(g2_out, before[-1] + 1)
                return ps[:, g2_bank[g], :]

            def bank_for(g):
                if g in g2_no:
                    return bank_for2(g)
                bank_free(g)
                return ps[:, gbank(g), :]

            def signal_of(name):
                return group_done if piece_no[name] < NP1 else g2_done

            def need_split(name, chunks=KC):
                pe.wait_ge(piece_lo, piece_no[name] + 1)
                return tuple(v[:, piece_slot(name)].rearrange("p (c n) -> p c n", c=chunks) for v in (hi2, lo2))

            def three_products(o, cases, fresh=None, chunks=KC):
                for c in range(chunks):
                    if fresh is not None:
                        pe.wait_ge(actT_done[1], fresh + c + 1)
                    for k, (a, b) in enumerate(cases(c)):
                        ins = pe.matmul(o, a, b, start=(c == 0 and k == 0), stop=(c == chunks - 1 and k == 2))
                return ins

            def feature_tile(o, w, f, fresh=None):
                w_hi, w_lo = w
                cut = slice(f * P, (f + 1) * P)
                return three_products(o, lambda c: ((w_hi[:, c, cut], xh[:, c]), (w_hi[:, c, cut], xl[:, c]), (w_lo[:, c, cut], xh[:, c])), fresh)

            def token_tile(o, w, n, cut=slice(0, T)):
                w_hi, w_lo = w
                tok = slice(n * P, (n + 1) * P)
                return three_products(o, lambda c: ((xh[:, c, tok], w_hi[:, c, cut]), (xh[:, c, tok], w_lo[:, c, cut]), (xl[:, c, tok], w_hi[:, c, cut])))

            def feature_piece(name):
                w = need_split(name)
                o = bank_for(name)
                for a in range(2):
                    ins = feature_tile(o[:, a * T:(a + 1) * T], w, a, fresh=FRESH.get(name) if a == 0 else None)
                ins.then_inc(signal_of(name), 1)

            def feature_pieces(name):
                for s in range(2):
                    feature_piece(f"{name}{s}")

            def token_piece(name, banks, signal, tile_ready=lambda n: None):
                w, s = need_split(name), int(name[-1])
                for n in range(NT):
                    tile_ready(n)
                    ins = token_tile(banks[n][:, s * T:(s + 1) * T], w, n)
                    if s:
                        ins.then_inc(signal, 1)
                if s == 0:
                    ins.then_inc(half_mm, 1)

            def token_pieces(name):
                banks = [bank_for(f"{name}{n}") for n in range(NT)]
                for s in range(2):
                    token_piece(f"{name}{s}", banks, signal_of(f"{name}0"))

            pe.wait_ge(consts_made, 1)
            transpose_by_tile(scaled, lambda n: pe.wait_ge(scaled_done, n + 1))
            for name in ("hq", "hf", "gqk"):
                feature_pieces(name)
            ins = feature_tile(bank_for("glow")[:, 0:T], need_split("glow"), 0)
            ins.then_inc(group_done, 1)
            pe.wait_ge(group_out, group_no["glow"] + 1)
            for a in range(2):
                ins = pe.matmul(ps[:, 7, a * T:(a + 1) * T], gate_up[:, a], glowT[0:RANK], start=True, stop=True)
            ins.then_inc(gate_mm, 1)
            for name in ("hi", "gv"):
                token_pieces(name)

            def scores(n, q, k):
                for tau in range(NT):
                    if n:
                        pe.wait_ge(lvl_kept, 4 * (n - 1) + 2 * tau + 2)
                    tok = slice(tau * P, tau * P + P)
                    for h in range(HEADS1):
                        f, rows = head_rows(h)
                        ins = pe.matmul(ps[:, 4 + 2 * tau + PLACE[h] // 4, (PLACE[h] % 4) * P:(PLACE[h] % 4 + 1) * P], k[rows, f, tok], q[rows, f, tok], start=True, stop=True)
                    ins.then_inc(lvl_scores, 1)

            pe.wait_ge(softplus_done, 1)
            pe.wait_ge(fgate_done, 1)
            scores(0, qF, kF)
            for l in range(LEVELS):
                if l < 4:
                    name = LEVEL_PIECES1[l]
                    if name[-1] == "0":
                        banks = [bank_for(f"{name[:-1]}{n}") for n in range(NT)]
                    token_piece(name, banks, group_done)
                pe.wait_ge(lvl_scaled, l + 1)
                scores(l + 1, qd[:, l % 2], kd[:, l % 2])
            pe.wait_ge(lvl_scaled, LEVELS + 1)
            pe.wait_ge(lvl_kept, 4 * LEVELS + 2)
            for h in range(HEADS1):
                f, rows = head_rows(h)
                ins = pe.matmul(ps[:, 4 + PLACE[h] // 4, (PLACE[h] % 4) * P:(PLACE[h] % 4 + 1) * P], kd[rows, 1, f, 0:P], qd[rows, 1, f, P:T], start=True, stop=True)
            ins.then_inc(lvl_scores, 1)
            pe.wait_ge(cross_out, 1)
            pe.wait_ge(lvl_kept, 4 * (LEVELS + 1))
            for n in range(NT):
                for h in range(HEADS1):
                    o = ps[:, 4 + 2 * n + h // 4, (h % 4) * P:(h % 4 + 1) * P]
                    ins = pe.matmul(o, own[:, n, PLACE[h]], vtok[:, n, h * P:(h + 1) * P], start=True, stop=(n == 0))
                    if n:
                        ins = pe.matmul(o, cross[:, PLACE[h]], vtok[:, 0, h * P:(h + 1) * P], start=False, stop=True)
                ins.then_inc(o_done, 1)
            transpose_to_tiles(mixed, lambda n: pe.wait_ge(mixed_done, (n + 1) * HEADS1))
            for half in range(2):
                for piece in range(2):
                    token_piece(f"wo{half}{piece}", [ps[:, 2 * half + n, :] for n in range(NT)], wout_done,
                                lambda n: pe.wait_ge(actT_done[1], 8 + 2 * n + 2))
            transpose_by_tile(scaled_p, lambda n: pe.wait_ge(scaled_done, 2 + n + 1))
            for k in range(2):
                pe.wait_ge(actT_done[k], 16)
            pe.wait_ge(h_done, 4)

            def key_scores(r):
                h0, h1 = ROUND_HEADS[r]
                pe.wait_ge(group_out, group_no["wq00"] + h1)
                for n in range(NT):
                    k = NT * r + n
                    if k >= 4:
                        pe.wait_ge(sub_out, k - 3)
                    for a in range(2 * h0, 2 * h1):
                        ins = pe.matmul(ps[:, 4 + k % 4, (a - 2 * h0) * P:(a - 2 * h0 + 1) * P], qT[:, a, n * P:(n + 1) * P], keysT[:, a], start=True, stop=True)
                    ins.then_inc(sub_done, 1)

            for r in range(ROUNDS):
                for h in range(*ROUND_HEADS[r]):
                    features(f"wq{h // 2}", actT, (h % 2,))
                if r == 0:
                    pe.wait_ge(mem_loaded, 32)
                key_scores(r)
            pe.wait_ge(mem_scaled, NT)
            pe.wait_ge(group_out, group_no["wq31"] + 1)
            for c in range(KC):
                for n in range(NT):
                    ins = pe.transpose(ps[:, c // 2, (c % 2) * T + n * P:(c % 2) * T + (n + 1) * P], memtok[:, n, c * P:(c + 1) * P], ident[:])
                if c % 2:
                    ins.then_inc(mem_T, 1)
            pe.wait_ge(memT_done, KC)
            features("mk", memT, (0, 1))
            tokens("mv", memT)
            pe.wait_ge(group_out, group_no["mv1"] + 1)
            for n in range(NT):
                pe.wait_ge(picks_done, n + 1)
                for a in range(3):
                    ins = pe.transpose(ps[:, n, a * P:(a + 1) * P], chosen[:, n, a], ident[:])
                ins.then_inc(pick_mm, 1)
            pe.wait_ge(pickT_done, 2)

            def weights_of(n, buf):
                pe.wait_ge(onehot_ready, n)
                pe.wait_ge(onehot_by_act, n)
                pe.wait_ge(onehot_weighted, n)
                for k in range(GT):
                    ins = pe.matmul(ps[:, buf, k * P:(k + 1) * P], hotA[:, buf, k], hotB[:, buf, k], start=True, stop=True)
                ins.then_inc(g_mm, 1)

            for b in range(GBUF):
                weights_of(b + 1, b)
            with pe.Fori(1, NGRP // GBUF) as i:
                for b in range(GBUF):
                    pe.wait_ge(g_out, GBUF * i + (b + 1 - GBUF))
                    weights_of(GBUF * i + (b + 1), b)

            u_hi, u_lo = (v[:, U].rearrange("p s (c i) -> p s c i", c=KC) for v in (hi, lo))

            def u_pass(n, par):
                pe.wait_ge(lo_done[U], n)
                o = ps[:, par, 0:T]
                for c in range(KC):
                    pe.matmul(o, u_hi[:, par, c], xh[:, c], start=(c == 0), stop=False)
                    pe.matmul(o, u_hi[:, par, c], xl[:, c], start=False, stop=False)
                    ins = pe.matmul(o, u_lo[:, par, c], xh[:, c], start=False, stop=(c == KC - 1))
                ins.then_inc(u_mm, 1)

            def v_pass(n, par, first=False, last=False):
                pe.wait_ge(lo_done[V], n)
                pe.wait_ge(wl_done, n)
                for tau in range(NT):
                    tok = slice(tau * P, (tau + 1) * P)
                    for k, (w, v) in enumerate(((wh, hi), (wh, lo), (wl, hi))):
                        for half in range(2):
                            ins = pe.matmul(ps[:, 4 + 2 * tau + half, :], w[:, tok], v[:, V, par, half * TILE:(half + 1) * TILE],
                                            start=(first and k == 0), stop=(last and k == 2))
                ins.then_inc(v_mm, 1)

            pe.wait_ge(g_out, NGRP)
            pe.wait_ge(x_split, 3)
            u_pass(1, 0)
            u_pass(2, 1)
            v_pass(1, 0, first=True)
            with pe.Fori(1, NKEY // 2) as i:
                pe.wait_ge(gelu_done, 2 * i - 1)
                u_pass(2 * i + 1, 0)
                v_pass(2 * i, 1)
                pe.wait_ge(gelu_done, 2 * i)
                u_pass(2 * i + 2, 1)
                v_pass(2 * i + 1, 0)
            v_pass(NKEY, 1, last=True)
            pe.wait_ge(peer_out, 4)
            transpose_by_tile(scaled2, lambda n: pe.wait_ge(scaled_done, 4 + n + 1))
            for name in ("dnq", "dnk", "dnv"):
                feature_pieces(name)
            pe.wait_ge(ba_split, 2)
            o = bank_for("ba")
            for n in range(NT):
                tok = slice(n * P, (n + 1) * P)
                ins = three_products(o[:, n * 2 * DH:(n + 1) * 2 * DH], lambda c: ((xh[:, c, tok], ba_hi[:, c]), (xh[:, c, tok], ba_lo[:, c]), (xl[:, c, tok], ba_hi[:, c])))
            ins.then_inc(g2_done, 1)
            token_pieces("dnz")
            token_pieces("gmu")
            pe.wait_ge(consts_made, 2)
            pe.wait_ge(dnsilu_done, 4)
            for n in range(NT):
                for f in range(2 * DH):
                    ins = pe.matmul(ps[:, 4, n * 2 * DH + f:n * 2 * DH + f + 1], sqk[:, f, n * P:(n + 1) * P], ones[:, 0:1], start=True, stop=True)
            ins.then_inc(ss_mm, 1)
            pe.wait_ge(dg_done, 1)
            pe.matmul(ps[:, 5, 0:TH], upper[:], dg.rearrange("p n h -> p (n h)"), start=True, stop=True)
            pe.matmul(ps[:, 5, TH:2 * TH], ones, dg.rearrange("p n h -> p (n h)"), start=True, stop=True).then_inc(gc_mm, 1)
            token_pieces("gmv")

            def th_out(b, th):
                return ps[:, b + th // DH, (th % DH) * P:(th % DH + 1) * P]

            def repeat_row(b, a, m):
                for th in range(TH):
                    ins = pe.matmul(th_out(b, th), rep[:, a, th], m, start=True, stop=True)
                ins.then_inc(row_mm, 1)

            pe.wait_ge(rep_done, 1)
            pe.wait_ge(rin_done, 1)
            pe.wait_ge(gcs_done, 1)
            repeat_row(4, 0, upper[:])
            repeat_row(6, 1, ident[:])
            token_pieces("gmz")
            pe.wait_ge(brow_done, 1)
            pe.wait_ge(dnsilu_done, 3)
            for th in range(TH):
                n, h = th // DH, th % DH
                k = convT[:, DH + h, n * P:(n + 1) * P]
                ins = pe.matmul(th_out(6, th), k, k, start=True, stop=True)
            ins.then_inc(kk_mm, 1)
            pe.wait_ge(dm_done, 1)
            repeat_row(4, 2, ident[:])
            feature_pieces("swq")
            def tokens_by_row(a):
                for th in range(TH):
                    n, h = th // DH, th % DH
                    ins = pe.transpose(th_out(6, th), convT[:, (1 + a) * DH + h, n * P:(n + 1) * P], ident[:])
                ins.then_inc(kv_tr, 1)

            pe.wait_ge(lt_done, 1)
            tokens_by_row(0)
            w = need_split("swkv")
            o = bank_for("swkv")
            feature_tile(o[:, 0:T], w, 0)
            for n in range(NT):
                ins = token_tile(o[:, T + n * P:T + (n + 1) * P], w, n, slice(P, 2 * P))
            ins.then_inc(g2_done, 1)
            pe.wait_ge(z0_done, 1)
            pe.wait_ge(qrow_done, 1)
            for th in range(TH):
                ins = pe.transpose(th_out(4, th), Z[:, th], ident[:])
            ins.then_inc(x0_tr, 1)
            pe.wait_ge(kv_out, 1)
            tokens_by_row(1)
            for l in range(1, LEVELS):
                pe.wait_ge(bt_done, l)
                for n in range(NT):
                    pe.wait_ge(x_done, NT * (l - 1) + n if l > 1 else 1)
                    if l > 1:
                        pe.wait_ge(x_done, 1 + NT * (l - 2) + n + 1)
                        pe.wait_ge(z_done, NT * (l - 2) + n + 1)
                    for th in range(DH * n, DH * n + DH):
                        ins = pe.matmul(th_out(4, th), BT[:, th], X[:, th], start=True, stop=True)
                    ins.then_inc(y_mm, 1)
                if l == 1:
                    pe.wait_ge(kv_out, 2)
                for n in range(NT):
                    pe.wait_ge(y_out, NT * (l - 1) + n + 1)
                    if l < LEVELS - 1:
                        for th in range(DH * n, DH * n + DH):
                            ins = pe.matmul(th_out(6, th), Z[:, th], Y[:, th], start=True, stop=True)
                    for th in range(DH * n, DH * n + DH):
                        ins = pe.matmul(th_out(4, th), Y[:, th], Z[:, th], start=True, stop=True)
                    ins.then_inc(pz_mm, 1)
                if l == LEVELS - 1:
                    pe.wait_ge(x_done, 1 + NT * (LEVELS - 2))
                    for th in range(TH):
                        n, h = th // DH, th % DH
                        ins = pe.matmul(th_out(6, th), convT[:, DH + h, n * P:(n + 1) * P], convT[:, h, n * P:(n + 1) * P], start=True, stop=True)
                    ins.then_inc(qk_mm, 1)
                piece = LEVEL_PIECES[l - 1]
                if piece[:-1] in features_of:
                    feature_piece(piece)
                else:
                    if piece[-1] == "0":
                        banks = [bank_for(f"{piece[:-1]}{n}") for n in range(NT)]
                    token_piece(piece, banks, g2_done)
            pe.wait_ge(z_done, NT * (LEVELS - 1))
            pe.wait_ge(kv_out, 2)
            for th in range(TH):
                pe.matmul(th_out(4, th), Z[:, th], vb[:, th], start=True, stop=True)
            pe.wait_ge(aq_done, 1)
            for h in range(DH):
                ins = pe.matmul(ps[:, 6, h * P:(h + 1) * P], kbg[:, DH + h], Z[:, DH + h], start=True, stop=True)
            ins.then_inc(u_out_mm, 1)

            def early_gate(name):
                tile, half = name[:-1], int(name[-1])
                banks = [bank_for(f"{tile}{n}") if half == 0 else ps[:, g2_bank[f"{tile}{n}"], :] for n in range(NT)]
                token_piece(name, banks, g2_done)

            early_gate("gate000")
            pe.wait_ge(du_done, 1)
            for h in range(DH):
                ins = pe.matmul(ps[:, 7, h * P:(h + 1) * P], kdl[:, h], du[:, h], start=True, stop=True)
            ins.then_inc(s1_mm, 1)
            pe.wait_ge(gmv_done, NT)
            pe.wait_ge(g2_out, g2_no["xmz1"] + 1)
            for n in range(NT):
                for g in range(4):
                    ins = pe.matmul(ps[:, 2 + n, g * P:(g + 1) * P], wsT[:, g], gv2[:, n, g * P:(g + 1) * P], start=True, stop=True)
                ins.then_inc(gm_mm, 1)
            early_gate("gate001")
            pe.wait_ge(s1_done, 1)
            pe.wait_ge(du_done, 2)
            for h in range(DH):
                ins = pe.matmul(ps[:, 6, h * P:(h + 1) * P], wT[:, h], S1[:, h], start=True, stop=True)
            ins.then_inc(ws_mm, 1)
            pe.wait_ge(aq_done, 1)
            for h in range(DH):
                ins = pe.matmul(th_out(4, h), AQ[:, h], du[:, h], start=True, stop=True)
            ins.then_inc(do_mm, 1)
            early_gate("gate010")
            pe.wait_ge(qg_done, 1)
            pe.wait_ge(vnew_done, 1)
            for h in range(DH):
                pe.matmul(th_out(4, DH + h), qg[:, h], S1[:, h], start=True, stop=False)
                ins = pe.matmul(th_out(4, DH + h), AQ[:, DH + h], vnew[:, h], start=False, stop=True)
            ins.then_inc(do_mm, 1)
            early_gate("gate011")
            pe.wait_ge(y_done[0], NT)
            pe.wait_ge(y_done[1], NT)
            for n in range(NT):
                banks, per = SW_BANKS[n], SH // len(SW_BANKS[n])
                width = (n + 1) * P
                for h in range(SH):
                    half = slice(SHD * (h // 4), SHD * (h // 4) + SHD)
                    ins = pe.matmul(ps[:, banks[h // per], (h % per) * width:(h % per + 1) * width], swqT[half, h % 4, n * P:(n + 1) * P], swkT[half, 0:width],
                                    start=True, stop=True)
                ins.then_inc(ss_mm2, 1)
            off = [0, SH * P]

            def sw_transpose(n):
                width = (n + 1) * P
                pr = prob[:, off[n]:off[n] + SH * width].rearrange("p (h j) -> p h j", h=SH)
                pe.wait_ge(s_exp, n + 1)
                pe.wait_ge(s_masked, n + 1)
                for h in range(SH):
                    for b in range(n + 1):
                        at = (h * (n + 1) + b) * P
                        ins = pe.transpose(ps[:, (2 if n else 4) + at // TILE, at % TILE:at % TILE + P], pr[:, h, b * P:(b + 1) * P], ident[:])
                ins.then_inc(s_tr, 1)

            def sw_out(n):
                width = (n + 1) * P
                prT = probT[:, off[n]:off[n] + SH * width].rearrange("p (h b i) -> p h b i", h=SH, b=n + 1)
                pe.wait_ge(s_trout, n + 1)
                for h in range(SH):
                    for b in range(n + 1):
                        ins = pe.matmul(ps[:, 6 + n, h * SHD:(h + 1) * SHD], prT[:, h, b], swv[:, b, SHD * (h // 4):SHD * (h // 4) + SHD], start=(b == 0), stop=(b == n))
                ins.then_inc(so_mm, 1)

            early_gate("gate100")
            sw_transpose(0)
            early_gate("gate101")
            pe.wait_ge(s_trout, 1)
            sw_transpose(1)
            sw_out(0)
            early_gate("gate110")
            sw_out(1)
            pe.wait_ge(mkv_moved, 32)
            for n in range(NT):
                if n:
                    pe.wait_ge(y_done[2], NT)
                for h in range(XH):
                    ins = pe.matmul(ps[:, 4 + 2 * n + h // 2, (h % 2) * T:(h % 2 + 1) * T], xmqT[:, h, n * P:(n + 1) * P], mkT[:, h], start=True, stop=True)
                ins.then_inc(xs_mm, 1)
            early_gate("gate111")
            for n in range(NT):
                pr = prob[:, n * 1024:(n + 1) * 1024].rearrange("p (h j) -> p h j", h=XH)
                pe.wait_ge(xs_exp, n + 1)
                for h in range(XH):
                    for b in range(2):
                        at = (2 * h + b) * P
                        ins = pe.transpose(ps[:, 4 + 2 * n + at // TILE, at % TILE:at % TILE + P], pr[:, h, b * P:(b + 1) * P], ident[:])
                ins.then_inc(xs_tr, 1)
            for n in range(NT):
                prT = probT[:, n * 1024:(n + 1) * 1024].rearrange("p (h b i) -> p h b i", h=XH, b=2)
                pe.wait_ge(xs_trout, n + 1)
                for h in range(XH):
                    for b in range(2):
                        ins = pe.matmul(ps[:, 2 + n, h * HEAD:(h + 1) * HEAD], prT[:, h, b], mv[:, b, h * HEAD:(h + 1) * HEAD], start=(b == 0), stop=(b == 1))
                ins.then_inc(xo_mm, 1)
            for n, y in enumerate((zdn, gu, swz, xmz)):
                pe.wait_ge(y_done[n], NT)
                if n >= 2:
                    pe.wait_ge(yT_done, n - 1)
                b = 4 + 2 * (n % 2)
                for c in range(4):
                    for k in range(NT):
                        at = c * T + k * P
                        ins = pe.transpose(ps[:, b + at // TILE, at % TILE:at % TILE + P], y[:, k, c * P:(c + 1) * P], ident[:])
                ins.then_inc(yT_mm, 1)
            for n in range(NBR):
                token_pieces(f"gate{2 + n // 2}{n % 2}")
                pe.wait_ge(yT_done, NBR)
                ws = {}
                for k, (tau, half) in enumerate(up_order):
                    if half not in ws:
                        ws[half] = need_split(f"up{n}{half}", 4)
                    if n:
                        pe.wait_ge(up_out, 4 * (n - 1) + k + 1)
                    w_hi, w_lo = ws[half]
                    tok = slice(tau * P, (tau + 1) * P)
                    three_products(ps[:, 4 + k, :], lambda c: ((yh[:, 4 * n + c, tok], w_hi[:, c]), (yh[:, 4 * n + c, tok], w_lo[:, c]),
                                                               (yl[:, 4 * n + c, tok], w_hi[:, c])), chunks=4).then_inc(up_mm, 1)
            transpose_to_tiles(merged, lambda n: pe.wait_ge(merged_done, n + 3))
            pe.wait_ge(g2_out, len(groups2))
            for half in range(2):
                for n in range(NT):
                    if half == 0:
                        pe.wait_ge(actT_done[1], 24 + 2 * n + 2)
                    for s in range(2):
                        ins = token_tile(ps[:, 2 * half + n, s * T:(s + 1) * T], need_split(f"out{half}{s}"), n)
                        if s:
                            ins.then_inc(fin_mm, 1)
                        elif n:
                            ins.then_inc(half_mm, 1)


def layout(inputs):
    import numpy as np
    a = {k: np.asarray(v) for k, v in inputs.items()}

    def col(v):
        return v.reshape(-1, P).T

    r = {}
    for n in ("x", "mem_2", "gla_w_gate_up", "hg_norm_g", "gla_norm_g"):
        r[n] = a[n]
    for n in ("peer_w_q", "w_mem_kv_2"):
        r[n] = a[n][0]
    w1, w2 = a["w_in"][0], a["w_in_2"][0]
    r["ba"] = w2[:, DNBA:DNBA + 2 * DH].reshape(KC, P, 2 * DH).transpose(1, 0, 2).reshape(P, KC * 2 * DH)
    r["cols"] = np.concatenate([col(a["norm1_g"]), col(a["norm2_g"]), col(a["norm_pre_2"]), col(a["norm_mem_2"]),
                                col(a["hg_lower_logits"]), col(a["gla_b_gate"]),
                                col(a["conv_w_2"]), col(a["spatial_b_2"])], axis=1)
    whole = {"hq": w1[:, HQ:HQ + TILE], "hf": w1[:, HF:HF + TILE], "gqk": w1[:, GQ:GQ + TILE], "glow": w1[:, GLOW:GLOW + T],
          "hi": w1[:, HI:HI + TILE], "gv": w1[:, GV:GV + TILE], "hgate": w1[:, HGATE:HGATE + TILE], "ggate": w1[:, GGATE:GGATE + TILE],
          "wo0": a["w_out"][0][:, 0:TILE], "wo1": a["w_out"][0][:, TILE:D],
          "swq": w2[:, SWQ:SWQ + TILE].reshape(D, 2, 4, SHD).transpose(0, 2, 1, 3).reshape(D, TILE),
          "swkv": w2[:, SWKV:SWKV + T]}
    for name, c0 in (("dnq", DNQ), ("dnk", DNK), ("dnv", DNV), ("dnz", DNZ), ("gmu", GMU), ("gmv", GMV), ("gmz", GMZ), ("swz", SWZ),
                     ("xmq", XMQ), ("xmz", XMZ)):
        whole[name] = w2[:, c0:c0 + TILE]
    r["up"] = a["w_up_2"][0].reshape(NBR, 4, P, D).transpose(0, 2, 1, 3)
    for n in range(NBR):
        for h in range(2):
            whole[f"gate{n}{h}"] = w2[:, GATES + n * D + h * TILE:GATES + n * D + (h + 1) * TILE]
    for h in range(2):
        whole[f"out{h}"] = a["w_out_2"][0][:, h * TILE:(h + 1) * TILE]

    def piece(name):
        w = whole.get(name)
        if w is None:
            w = whole[name[:-1]]
            width = w.shape[1] // 2
            w = w[:, int(name[-1]) * width:(int(name[-1]) + 1) * width]
        return w.reshape(-1, P, w.shape[1]).transpose(1, 0, 2).reshape(P, 2 * D)

    r["pieces"] = np.stack([piece(name) for name in PIECES if name[:2] != "up"])
    r["norm_f_g"] = a["norm_f_g"]
    r["norm_post_2"] = a["norm_post_2"]
    r["rows"] = np.concatenate([a["gm_norm_2"][0], a["dn_norm_2"][0], a["a_log_2"][0], a["dt_bias_2"][0], a["sinks_2"][0]])
    r["spatial_w_t"] = a["spatial_w_2"][0].transpose(2, 0, 1).reshape(P, 4 * P)
    r["sub_keys_t"] = a["peer_sub_keys"][0].reshape(HP, NKEY, P).transpose(2, 0, 1).reshape(P, HP * NKEY)
    r["u_t"] = a["peer_u"][0].reshape(NKEY, NKEY, KC, P).transpose(1, 3, 2, 0).reshape(NKEY, P, D)
    r["v_t"] = a["peer_v"][0].reshape(NKEY, NKEY, D).transpose(1, 0, 2)
    return r


def kernel(**inputs):
    import concourse.bacc as bacc
    from concourse import mybir as mb
    from concourse.bass_utils import run_bass_kernel_spmd

    nc = bacc.Bacc("TRN2", target_bir_lowering=False, num_devices=1)
    arrays, t = {}, {}
    import numpy as np
    for name, a in layout(inputs).items():
        a = np.ascontiguousarray(a)
        arrays[f"in_{name}"] = a
        t[name] = nc.dram_tensor(f"in_{name}", a.shape, mb.dt.from_np(a.dtype), kind="ExternalInput").ap()
    out = nc.dram_tensor("out_0", (1, T, D), F32, kind="ExternalOutput").ap()
    build(nc, t, out)
    r = run_bass_kernel_spmd(nc, [arrays], core_ids=[0])
    return r.results[0]["out_0"]
```
